# Optimizing a Trainium2 kernel written in Bass

```python
import jax, jax.numpy as jnp
from jax import lax
import numpy as np

D_MODEL = 1024
BATCH = 1
SEQ = 1024
DEPTH = 1

CHUNK = 64
N_MEM = 256
DN_HEADS = 4
DN_HEAD_DIM = 128
DN_WIDTH = DN_HEADS * DN_HEAD_DIM
CONV_K = 4
POOL_GROUPS = 4
POOL_WINDOWS = (2, 4, 8, 16)
POOL_WIDTH = D_MODEL // 2
POOL_GROUP_DIM = POOL_WIDTH // POOL_GROUPS
D_FF = 2816
XA_HEADS = 4
XA_HEAD_DIM = D_MODEL // XA_HEADS
LN_EPS = 1e-5
RMS_EPS = 1e-6
L2_EPS = 1e-6
ALPHA = (2.0 * DEPTH) ** 0.25
BETA_INIT = (8.0 * DEPTH) ** -0.25

OFF_QKV = 3 * DN_WIDTH
OFF_Z = OFF_QKV + DN_WIDTH
OFF_A = OFF_Z + DN_HEADS
OFF_B = OFF_A + DN_HEADS
OFF_POOL = OFF_B + POOL_WIDTH
OFF_GDN = OFF_POOL + D_MODEL
IN_COLS = OFF_GDN + D_MODEL
IN_SPLITS = (OFF_QKV, OFF_Z, OFF_A, OFF_B, OFF_POOL, OFF_GDN)

kernel_name = "hybrid_deltanet_pool_macaron_deepnorm"

def _layernorm(x, g, b):
    xf = x.astype(jnp.float32)
    mu = jnp.mean(xf, axis=-1, keepdims=True)
    var = jnp.mean(jnp.square(xf - mu), axis=-1, keepdims=True)
    y = (xf - mu) * lax.rsqrt(var + LN_EPS) * g.astype(jnp.float32) + b.astype(jnp.float32)
    return y.astype(x.dtype)

def _swiglu(x, w_gate, w_up, w_down):
    return (jax.nn.silu(x @ w_gate) * (x @ w_up)) @ w_down

def _causal_dwconv(x, w):
    c = x.shape[-1]
    return lax.conv_general_dilated(
        x, w[:, None, :].astype(x.dtype), window_strides=(1,), padding=[(CONV_K - 1, 0)],
        dimension_numbers=("NWC", "WIO", "NWC"), feature_group_count=c)

def _l2norm(x):
    return x * lax.rsqrt(jnp.sum(jnp.square(x), axis=-1, keepdims=True) + L2_EPS)

def _gated_delta_rule(q, k, v, g, beta):
    B, L, H, D = q.shape
    n = L // CHUNK
    ch = lambda t: t.reshape(B, n, CHUNK, H, D).transpose(1, 0, 3, 2, 4)
    q, k, v = ch(q), ch(k), ch(v)
    g = g.reshape(B, n, CHUNK, H).transpose(1, 0, 3, 2)
    beta = beta.reshape(B, n, CHUNK, H).transpose(1, 0, 3, 2)

    gc = jnp.cumsum(g, axis=-1)
    idx = jnp.arange(CHUNK)
    incl = idx[:, None] >= idx[None, :]
    strict = idx[:, None] > idx[None, :]
    diff = gc[..., :, None] - gc[..., None, :]
    decay = jnp.exp(jnp.where(incl, diff, -jnp.inf))

    kb = k * beta[..., None]
    a_low = jnp.where(strict, jnp.einsum("nbhcd,nbhed->nbhce", kb, k) * decay, 0.0)
    eye = jnp.eye(CHUNK, dtype=jnp.float32)
    rhs = jnp.concatenate([v * beta[..., None], kb * jnp.exp(gc)[..., None]], axis=-1)
    sol = lax.linalg.triangular_solve(a_low + eye, rhs, left_side=True, lower=True,
                                      unit_diagonal=True)
    u, w = sol[..., :D], sol[..., D:]

    attn = jnp.einsum("nbhcd,nbhed->nbhce", q, k) * decay
    q_dec = q * jnp.exp(gc)[..., None]
    g_last = gc[..., -1]
    k_dec = k * jnp.exp(g_last[..., None] - gc)[..., None]

    def step(state, inp):
        qd, kd, ui, wi, ai, gl = inp
        v_new = ui - jnp.einsum("bhcd,bhde->bhce", wi, state)
        o = jnp.einsum("bhcd,bhde->bhce", qd, state) + jnp.einsum("bhce,bhef->bhcf", ai, v_new)
        state = state * jnp.exp(gl)[..., None, None] + jnp.einsum("bhcd,bhce->bhde", kd, v_new)
        return state, o

    s0 = jnp.zeros((B, H, D, D), jnp.float32)
    _, o = lax.scan(step, s0, (q_dec, k_dec, u, w, attn, g_last))
    return o.transpose(1, 0, 3, 2, 4).reshape(B, L, H, D)

def _multiscale_pool(p, pool_w, pool_scale):
    B, L, _ = p.shape
    pf = p.astype(jnp.float32).reshape(B, L, POOL_GROUPS, POOL_GROUP_DIM)
    csum = jnp.cumsum(pf, axis=1)
    t = (jnp.arange(L, dtype=jnp.int32) + 1).astype(jnp.float32)
    means = []
    for gi, win in enumerate(POOL_WINDOWS):
        c = csum[:, :, gi]
        lag = jnp.pad(c, ((0, 0), (win, 0), (0, 0)))[:, :L]
        cnt = jnp.minimum(t, float(win))[None, :, None]
        means.append((c - lag) / cnt)
    mixed = jnp.stack(means, axis=2) - pf
    y = jnp.einsum("blgc,gcd->blgd", mixed, pool_w.astype(jnp.float32)).reshape(B, L, POOL_WIDTH)
    return (y * pool_scale.astype(jnp.float32)).astype(p.dtype)

def _hybrid_mixer(h, w_in, conv_w, a_log, dt_bias, dn_norm_w, w_dn_branch,
                  pool_w, pool_scale, w_pool_branch, w_mix_out):
    B, L, _ = h.shape
    proj = h @ w_in
    qkv, z, a, b, p, gate_dn, gate_pool = jnp.split(proj, IN_SPLITS, axis=-1)

    qkv = jax.nn.silu(_causal_dwconv(qkv, conv_w)).astype(jnp.float32)
    q, k, v = jnp.split(qkv, 3, axis=-1)
    hs = (B, L, DN_HEADS, DN_HEAD_DIM)
    q = _l2norm(q.reshape(hs)) * (DN_HEAD_DIM ** -0.5)
    k = _l2norm(k.reshape(hs))
    v = v.reshape(hs)
    beta = jax.nn.sigmoid(b.astype(jnp.float32))
    g = -jnp.exp(a_log.astype(jnp.float32)) * jax.nn.softplus(
        a.astype(jnp.float32) + dt_bias.astype(jnp.float32))
    o = _gated_delta_rule(q, k, v, g, beta)
    o = o * lax.rsqrt(jnp.mean(jnp.square(o), axis=-1, keepdims=True) + RMS_EPS)
    o = o * dn_norm_w.astype(jnp.float32) * jax.nn.silu(z.astype(jnp.float32).reshape(hs))
    y_dn = o.reshape(B, L, DN_WIDTH).astype(h.dtype) @ w_dn_branch

    y_pool = _multiscale_pool(p, pool_w, pool_scale) @ w_pool_branch

    merged = jax.nn.sigmoid(gate_dn) * y_dn + jax.nn.sigmoid(gate_pool) * y_pool
    return merged @ w_mix_out

def _cross_attention(h, m, wq, wk, wv, wo):
    B, L, _ = h.shape
    q = (h @ wq).reshape(B, L, XA_HEADS, XA_HEAD_DIM)
    k = (m @ wk).reshape(B, N_MEM, XA_HEADS, XA_HEAD_DIM)
    v = (m @ wv).reshape(B, N_MEM, XA_HEADS, XA_HEAD_DIM)
    s = jnp.einsum("bqhd,bkhd->bhqk", q, k).astype(jnp.float32) * (XA_HEAD_DIM ** -0.5)
    pr = jax.nn.softmax(s, axis=-1).astype(h.dtype)
    o = jnp.einsum("bhqk,bkhd->bqhd", pr, v).reshape(B, L, D_MODEL)
    return o @ wo

def setup_inputs(seed: int = 0) -> dict:
    key = jax.random.key(seed)
    ks = iter(jax.random.split(key, 40))
    f32 = jnp.float32

    def nrm(shape, scale):
        return jax.random.normal(next(ks), shape, f32) * scale

    def gain(shape):
        return 1.0 + 0.02 * jax.random.normal(next(ks), shape, f32)

    def bias(shape):
        return 0.02 * jax.random.normal(next(ks), shape, f32)

    Dp = DEPTH
    d = D_MODEL
    x = jax.random.normal(next(ks), (BATCH, SEQ, d), f32)
    mem = jax.random.normal(next(ks), (BATCH, N_MEM, d), f32)

    ffn1_w_gate = nrm((Dp, d, D_FF), d ** -0.5)
    ffn1_w_up = nrm((Dp, d, D_FF), d ** -0.5)
    ffn1_w_down = nrm((Dp, D_FF, d), BETA_INIT * D_FF ** -0.5)
    ln1_g, ln1_b = gain((Dp, d)), bias((Dp, d))

    w_in = nrm((Dp, d, IN_COLS), d ** -0.5)
    conv_w = nrm((Dp, CONV_K, 3 * DN_WIDTH), CONV_K ** -0.5)
    a_log = jnp.log(jax.random.uniform(next(ks), (Dp, DN_HEADS), f32, 1.0, 16.0))
    dt = jnp.exp(jax.random.uniform(next(ks), (Dp, DN_HEADS), f32,
                                    float(np.log(1e-3)), float(np.log(1e-1))))
    dt_bias = dt + jnp.log(-jnp.expm1(-dt))
    dn_norm_w = gain((Dp, DN_HEAD_DIM))
    w_dn_branch = nrm((Dp, DN_WIDTH, d), DN_WIDTH ** -0.5)
    pool_w = nrm((Dp, POOL_GROUPS, POOL_GROUP_DIM, POOL_GROUP_DIM), POOL_GROUP_DIM ** -0.5)
    pool_scale = gain((Dp, POOL_WIDTH))
    w_pool_branch = nrm((Dp, POOL_WIDTH, d), POOL_WIDTH ** -0.5)
    w_mix_out = nrm((Dp, d, d), BETA_INIT * d ** -0.5)
    ln2_g, ln2_b = gain((Dp, d)), bias((Dp, d))

    mem_ln_g, mem_ln_b = gain((Dp, d)), bias((Dp, d))
    xa_wq = nrm((Dp, d, d), d ** -0.5)
    xa_wk = nrm((Dp, d, d), d ** -0.5)
    xa_wv = nrm((Dp, d, d), d ** -0.5)
    xa_wo = nrm((Dp, d, d), BETA_INIT * d ** -0.5)
    ln3_g, ln3_b = gain((Dp, d)), bias((Dp, d))

    ffn2_w_gate = nrm((Dp, d, D_FF), d ** -0.5)
    ffn2_w_up = nrm((Dp, d, D_FF), d ** -0.5)
    ffn2_w_down = nrm((Dp, D_FF, d), BETA_INIT * D_FF ** -0.5)
    ln4_g, ln4_b = gain((Dp, d)), bias((Dp, d))

    return {"x": x, "mem": mem,
            "ffn1_w_gate": ffn1_w_gate, "ffn1_w_up": ffn1_w_up, "ffn1_w_down": ffn1_w_down,
            "ln1_g": ln1_g, "ln1_b": ln1_b,
            "w_in": w_in, "conv_w": conv_w, "a_log": a_log, "dt_bias": dt_bias,
            "dn_norm_w": dn_norm_w, "w_dn_branch": w_dn_branch,
            "pool_w": pool_w, "pool_scale": pool_scale, "w_pool_branch": w_pool_branch,
            "w_mix_out": w_mix_out, "ln2_g": ln2_g, "ln2_b": ln2_b,
            "mem_ln_g": mem_ln_g, "mem_ln_b": mem_ln_b,
            "xa_wq": xa_wq, "xa_wk": xa_wk, "xa_wv": xa_wv, "xa_wo": xa_wo,
            "ln3_g": ln3_g, "ln3_b": ln3_b,
            "ffn2_w_gate": ffn2_w_gate, "ffn2_w_up": ffn2_w_up, "ffn2_w_down": ffn2_w_down,
            "ln4_g": ln4_g, "ln4_b": ln4_b}

def reference(x, mem, ffn1_w_gate, ffn1_w_up, ffn1_w_down, ln1_g, ln1_b,
              w_in, conv_w, a_log, dt_bias, dn_norm_w, w_dn_branch,
              pool_w, pool_scale, w_pool_branch, w_mix_out, ln2_g, ln2_b,
              mem_ln_g, mem_ln_b, xa_wq, xa_wk, xa_wv, xa_wo, ln3_g, ln3_b,
              ffn2_w_gate, ffn2_w_up, ffn2_w_down, ln4_g, ln4_b):
    for l in range(DEPTH):
        x = _layernorm(ALPHA * x + 0.5 * _swiglu(x, ffn1_w_gate[l], ffn1_w_up[l], ffn1_w_down[l]),
                       ln1_g[l], ln1_b[l])
        mix = _hybrid_mixer(x, w_in[l], conv_w[l], a_log[l], dt_bias[l], dn_norm_w[l],
                            w_dn_branch[l], pool_w[l], pool_scale[l], w_pool_branch[l], w_mix_out[l])
        x = _layernorm(ALPHA * x + mix, ln2_g[l], ln2_b[l])
        m = _layernorm(mem, mem_ln_g[l], mem_ln_b[l])
        xa = _cross_attention(x, m, xa_wq[l], xa_wk[l], xa_wv[l], xa_wo[l])
        x = _layernorm(ALPHA * x + xa, ln3_g[l], ln3_b[l])
        x = _layernorm(ALPHA * x + 0.5 * _swiglu(x, ffn2_w_gate[l], ffn2_w_up[l], ffn2_w_down[l]),
                       ln4_g[l], ln4_b[l])
    return x


_drawn_inputs = setup_inputs


def setup_inputs(seed=0):
    import zlib

    import numpy as np

    out = dict(_drawn_inputs(seed))
    spreads = {}
    factors = {'ln1_b': 2.669,
     'dn_norm_w': 8.0,
     'pool_scale': 8.0,
     'ln2_g': 2.854,
     'ln2_b': 2.873,
     'mem_ln_g': 8.0,
     'mem_ln_b': 24.142,
     'ln3_g': 2.777,
     'ln3_b': 2.762,
     'ln4_g': 7.68,
     'ln4_b': 8.042}
    for name, (base, spread) in spreads.items():
        noise = np.random.default_rng([zlib.crc32(name.encode()), seed]).standard_normal(out[name].shape)
        drawn = base * np.exp(spread * noise) if base else spread * noise
        out[name] = __import__('jax').numpy.asarray(drawn.astype(out[name].dtype))
    for name, factor in factors.items():
        out[name] = (out[name] * factor).astype(out[name].dtype)
    return out
```

```python
from contextlib import ExitStack

import numpy as np
import concourse.bass as bass
from concourse import mybir

P = 128
SEQ = 1024
D = 1024
KD = D // P
NT = SEQ // P
HALF = 512
D_FF = 2816
PAIRS = D_FF // (2 * P)
N_MEM = 256
MT = N_MEM // P
HEADS = 4
HD = 128
XD = 256
QKV = 3 * HEADS * HD
CONV_K = 4
GROUPS = 4
HALO = 16
LN_EPS = 1e-5
RMS_EPS = 1e-6
L2_EPS = 1e-6
ALPHA = 2.0 ** 0.25
LEVELS = 6

COL_Z = QKV
COL_AB = COL_Z + HEADS * HD
COL_P = COL_AB + 2 * HEADS
COL_GDN = COL_P + GROUPS * P
COL_GPOOL = COL_GDN + D

CH_Z = QKV // P
CH_GDN = CH_Z + HEADS
CH_GPOOL = CH_GDN + KD
CHUNKS = CH_GPOOL + KD

F32 = mybir.dt.float32
F32R = mybir.dt.float32r
ALU = mybir.AluOpType
ACT = mybir.ActivationFunctionType
AX = mybir.AxisListType

S_KV, S_FFN1 = 0, 8
S_QKV = S_FFN1 + 2 * PAIRS
S_Z = S_QKV + 6
S_GATE = S_Z + 2
S_P = S_GATE + 8
S_MIX = S_P + 2
S_XA = S_MIX + 4
S_FFN2 = S_XA + 4
S_END = S_FFN2 + 2 * PAIRS

U_KV, U_FFN1 = 0, 8
U_QKV = U_FFN1 + 4 * PAIRS
U_Z = U_QKV + 12
U_GATE = U_Z + 4
U_P = U_GATE + 16
U_MIX = U_P + 4
U_XA = U_MIX + 16
U_FFN2 = U_XA + 16
U_END = U_FFN2 + 4 * PAIRS

Q_MEM, Q_X = 0, 2 * MT
Q_FFN1 = Q_X + 2 * NT
Q_LN1 = Q_FFN1 + 16 * PAIRS
Q_AB = Q_LN1 + 2 * NT
Q_POOL = Q_AB + 1
Q_MIX = Q_POOL + 2 * GROUPS
Q_LN2 = Q_MIX + 16 * 4
Q_XA = Q_LN2 + 2 * NT
Q_LN3 = Q_XA + 16 * 4
Q_FFN2 = Q_LN3 + 2 * NT

D_FFN1, D_MIX = 0, PAIRS
D_XA = D_MIX + 4
D_FFN2 = D_XA + 4

H_FFN1, H_MIX = 0, 4 * PAIRS
H_FFN2 = H_MIX + 16

M_ID, M_UP, M_ONE, M_LOW, M_NEG1, M_LEV = 0, 1, 2, 3, 4, 5
N_MASKS = M_LEV + LEVELS


def host_masks():
    i = np.arange(P)[:, None]
    j = np.arange(P)[None, :]
    m = np.zeros((P, N_MASKS, P), np.float32)
    m[:, M_ID] = i == j
    m[:, M_UP] = i <= j
    m[:, M_ONE] = 1.0
    m[:, M_LOW] = i > j

    def level(b):
        return (i // (2 * b) == j // (2 * b)) & (i // b % 2 == 1) & (j // b % 2 == 0)

    m[:, M_NEG1] = -1.0 * level(1)
    for n in range(LEVELS):
        m[:, M_LEV + n] = level(2 << n)
    return m


def host_counts():
    c = np.zeros((P, 32), np.float32)
    c[:, 0:HALO] = 1.0 / (np.arange(HALO) + 1.0)
    c[:, HALO:] = -0.5
    return c


def build(nc, a):
    with ExitStack() as ctx:
        base = 16512
        place = {}

        def at(name, shape, dtype, where=None, offset=0):
            nonlocal base
            size = int(np.prod(shape[1:])) * 4
            if where is None:
                address = base
                base += (size + 31) // 32 * 32
            else:
                address = place[where] + offset
            place[name] = address
            return nc.alloc_sbuf_tensor_at(name, shape, dtype, offset=address)

        X = at("X", [P, NT, D], F32)
        XTh = at("XTh", [P, KD, SEQ], F32R)
        XTl = at("XTl", [P, KD, SEQ], F32R)
        GUraw = at("GUraw", [P, KD, 256], F32)
        GUh = at("GUh", [P, 2, KD, 256], F32R)
        GUl = at("GUl", [P, 2, KD, 256], F32R)
        DWraw = at("DWraw", [P, 2, D], F32)
        DWh = at("DWh", [P, 2, D], F32R)
        DWl = at("DWl", [P, 2, D], F32R)
        HTh = at("HTh", [P, 2, SEQ], F32R)
        HTl = at("HTl", [P, 2, SEQ], F32R)
        SIG = at("SIG", [P, 2, HALF], F32)
        H32 = at("H32", [P, 2, HALF], F32)
        PTh = at("PTh", [P, 2, HALF], F32R)
        PTl = at("PTl", [P, 2, HALF], F32R)
        LNG = at("LNG", [P, D], F32)
        LNB = at("LNB", [P, D], F32)
        MASK = at("MASK", [P, N_MASKS, P], F32)
        COUNT = at("COUNT", [P, 32], F32)
        BNS = at("BNS", [P, 2, 6], F32)
        MV = at("MV", [P, NT, 2], F32)
        VE = at("VE", [P, NT], F32)
        RSTD = at("RSTD", [P, NT], F32)
        NMR = at("NMR", [P, NT], F32)
        CONVW = at("CONVW", [P, CH_Z, CONV_K], F32)
        PSCALE = at("PSCALE", [P, GROUPS], F32)
        DNW = at("DNW", [P, 1], F32)
        HPAR = at("HPAR", [P, 2, HEADS], F32)
        G_G, G_CUM, G_ECUM, G_ETAIL, G_ELAST, G_BETA, G_NBE = range(7)
        GT = at("GT", [P, NT, 7, HEADS], F32)
        GTN = at("GTN", [P, 7, HEADS], F32)
        SS = at("SS", [P, 4, HEADS], F32)
        RN = at("RN", [P, 3, HEADS], F32)
        assert base <= 229368, base

        KV = at("KV", [P, 2, 2, 2, XD], F32R, "LNG")
        PR = at("PR", [P, 4, N_MEM], F32, "SIG")
        NEGMAX = at("NEGMAX", [P, 8], F32, "H32")
        RSUM = at("RSUM", [P, 8], F32, "H32", 32)
        RINV = at("RINV", [P, 8], F32, "H32", 64)
        KVO = at("KVO", [P, 2, 2, 2 * N_MEM], F32R, "DWh")
        RAW = at("RAW", [P, 2, HALO + SEQ], F32, "DWh")
        CACC = at("CACC", [P, 2, 2, HALF], F32, "HTh")
        WSUM = at("WSUM", [P, 2, HALO + SEQ], F32, "HTh")
        COUT = at("COUT", [P, 2, 2, HALF], F32, "SIG")
        MIXED = at("MIXED", [P, GROUPS, SEQ], F32, "PTh")
        POOLW = at("POOLW", [P, GROUPS, P], F32, "DWh", 12288)
        ABRAW = at("ABRAW", [P, KD, 8], F32, "PTh")
        ABh = at("ABh", [P, KD, 8], F32R, "PTh", 256)
        ABl = at("ABl", [P, KD, 8], F32R, "PTh", 512)
        ABT = at("ABT", [P, NT, 8], F32, "PTh", 768)
        AB1 = at("AB1", [P, NT, HEADS], F32, "PTh", 1024)
        AB2 = at("AB2", [P, NT, HEADS], F32, "PTh", 1152)
        AB3 = at("AB3", [P, NT, HEADS], F32, "PTh", 1280)
        AB4 = at("AB4", [P, HEADS], F32, "PTh", 1408)
        GATE = at("GATE", [P, 2, 2, HALF], F32, "PTh")
        spot = [0]

        def delta(name, shape=(P, HEADS, P)):
            t = at(name, list(shape), F32, "DWh", spot[0])
            spot[0] += int(np.prod(shape[1:])) * 4
            return t

        QKVS = delta("QKVS", (P, 3 * HEADS, P))
        ZS, K0, Q0, V0, SQ = map(delta, ("ZS", "K0", "Q0", "V0", "SQ"))
        KN, QN, KDEC, VB, KT, QT = map(delta, ("KN", "QN", "KDEC", "VB", "KT", "QT"))
        DIF, E1, E2, L, LT, T, TT, MM = map(delta, ("DIF", "E1", "E2", "L", "LT", "T", "TT", "MM"))
        ATT, R, VN, ST, O, = map(delta, ("ATT", "R", "VN", "ST", "O"))
        assert place["DWh"] + spot[0] <= place["MASK"]
        SQ2, QS, ON, OZ = E1, Q0, SQ, K0

        PS = ctx.enter_context(nc.psum_tensor("PS", [P, 8, 512], F32))
        ident = MASK[:, M_ID, :]

        proj_scratch = nc.dram_tensor("proj_scratch", [CHUNKS, P, SEQ], F32, kind="Internal").ap()
        kv_scratch = nc.dram_tensor("kv_scratch", [HEADS, P, 2, 2, 2 * N_MEM], F32, kind="Internal").ap()
        proj_v = proj_scratch.rearrange("c p t -> p c t")
        gate_v = proj_scratch[CH_GDN:CHUNKS].rearrange("(g c) p t -> p g c t", g=2)
        rows = lambda w: w.rearrange("o (k p) n -> p (o k) n", p=P)
        col = lambda v: v.rearrange("o n -> (o n)")
        w_in = rows(a["w_in"])
        x_v = a["x"].rearrange("b (t p) d -> p (b t) d", p=P)
        out_v = a["out"].rearrange("b (t p) d -> p (b t) d", p=P)
        mem_v = a["mem"].rearrange("b (t p) d -> p (b t) d", p=P)

        sems = {}

        def sem(name):
            if name not in sems:
                sems[name] = ctx.enter_context(nc.semaphore(name))
            return sems[name]

        gu_in, gu_hi, gu_lo = sem("gu_in"), sem("gu_hi"), sem("gu_lo")
        dw_in, dw_hi, dw_lo = sem("dw_in"), sem("dw_hi"), sem("dw_lo")
        unit_ready, unit_read = sem("unit_ready"), sem("unit_read")
        tile_ready, tile_read = sem("tile_ready"), sem("tile_read")
        act_out, h_hi, h_lo = sem("act_out"), sem("h_hi"), sem("h_lo")
        const_in, x_in, mem_in = sem("const_in"), sem("x_in"), sem("mem_in")
        ln_par_in, ln_par_used = sem("ln_par_in"), sem("ln_par_used")
        ln_var, ln_rstd, ln_nmr, ln_hat = sem("ln_var"), sem("ln_rstd"), sem("ln_nmr"), sem("ln_hat")
        ln_scaled, ln_done, bn_step = sem("ln_scaled"), sem("ln_done"), sem("bn_step")
        xt_hi, xt_lo, x_scaled = sem("xt_hi"), sem("xt_lo"), sem("x_scaled")
        kv_hi, kv_lo = sem("kv_hi"), sem("kv_lo")
        kv_stored = [sem("kv_stored0"), sem("kv_stored1")]
        small_step = sem("small_step")
        ab_in, ab_split, ab_done = sem("ab_in"), sem("ab_split"), sem("ab_done")
        halo_zero, tap, conv_done = sem("halo_zero"), sem("tap"), sem("conv_done")
        cout_done = sem("cout_done")
        stored = [sem("stored0"), sem("stored1")]
        pooled, pool_step, pool_hi, pool_w_in = sem("pooled"), sem("pool_step"), sem("pool_hi"), sem("pool_w_in")
        state_zero, delta_done = sem("state_zero"), sem("delta_done")
        gate_in = [sem("gate_in0"), sem("gate_in1")]
        gated_a, gated_b = sem("gated_a"), sem("gated_b")
        kvh_in, kvh_used = sem("kvh_in"), sem("kvh_used")
        q_hi, q_lo, o_hi, o_lo = sem("q_hi"), sem("q_lo"), sem("o_hi"), sem("o_lo")
        s_ready, s_read, neg_max = sem("s_ready"), sem("s_read"), sem("neg_max")
        r_inv, p_norm = sem("r_inv"), sem("p_norm")
        pt_ready, pt_hi, pt_lo = sem("pt_ready"), sem("pt_hi"), sem("pt_lo")
        out_stored = sem("out_stored")

        LN_ORDER = {"mem": 0, "ln1": 1, "ln2": 2, "ln3": 3, "ln4": 4}
        LN_TILES = {"mem": MT, "ln1": NT, "ln2": NT, "ln3": NT, "ln4": NT}
        LN_BASE = {"mem": 0, "ln1": MT, "ln2": MT + NT, "ln3": MT + 2 * NT, "ln4": MT + 3 * NT}
        XT_BASE = {"mem": 0, "x": 2 * MT, "ln1": 2 * MT + 2 * NT, "ln2": 2 * MT + 4 * NT, "ln3": 2 * MT + 6 * NT}
        Q_BASE = {"mem": Q_MEM, "x": Q_X, "ln1": Q_LN1, "ln2": Q_LN2, "ln3": Q_LN3}

        block = ctx.enter_context(nc.Block())

        @block.sync
        def _(sp):
            def load_gu(n, src_a, src_b):
                sp.wait_ge(gu_lo, n + 1)
                for dst, src in (src_a, src_b):
                    sp.dma_start(dst, src).then_inc(gu_in, 16)

            def load_cols(n, w, c):
                load_gu(n, (GUraw[:, 0:4, :], w[:, 0:4, bass.ds(c, 256)]),
                        (GUraw[:, 4:8, :], w[:, 4:8, bass.ds(c, 256)]))

            def load_gate_up(n, wg, wu, c):
                load_gu(n, (GUraw[:, :, 0:P], wg[:, :, bass.ds(c, P)]),
                        (GUraw[:, :, P:256], wu[:, :, bass.ds(c, P)]))

            def load_dw(m, w, row):
                sp.wait_ge(dw_lo, m + 1)
                for c in range(2):
                    sp.dma_start(DWraw[:, c, :], w[bass.ds(row + c * P, P), :]).then_inc(dw_in, 16)

            def load_ln(name, g, b):
                k = LN_ORDER[name]
                if k:
                    sp.wait_ge(ln_par_used, k)
                for dst, src in ((LNG, g), (LNB, b)):
                    sp.dma_start(dst[:, :], src.broadcast_to([P, D])).then_inc(ln_par_in, 16)

            def ffn_loads(s0, d0, wg, wu, wd, next_slots):
                with sp.Fori(0, PAIRS - 1) as j:
                    load_dw(d0 + j, wd, j * 256)
                    for c in range(2):
                        load_gate_up(s0 + 2 + 2 * j + c, wg, wu, j * 256 + 256 + c * P)
                load_dw(d0 + PAIRS - 1, wd, (PAIRS - 1) * 256)
                for f in next_slots:
                    f()

            sp.dma_start(X[:, 0:MT, :], mem_v).then_inc(mem_in, 16)
            load_ln("mem", a["mem_ln_g"], a["mem_ln_b"])
            sp.dma_start(MASK[:, :, :], a["masks"]).then_inc(const_in, 16)
            sp.dma_start(COUNT[:, :], a["counts"]).then_inc(const_in, 16)
            sp.dma_start(CONVW[:, :, :], a["conv_w"]).then_inc(const_in, 16)
            sp.dma_start(PSCALE[:, :], a["pool_scale"]).then_inc(const_in, 16)
            sp.dma_start(DNW[:, :], a["dn_norm_w"]).then_inc(const_in, 16)
            sp.dma_start(HPAR[:, 0, :], a["dt_bias"].broadcast_to([P, HEADS])).then_inc(const_in, 16)
            sp.dma_start(HPAR[:, 1, :], a["a_log"].broadcast_to([P, HEADS])).then_inc(const_in, 16)
            wk, wv = rows(a["xa_wk"]), rows(a["xa_wv"])
            for n in range(4):
                load_cols(n, wk, n * 256)
            for n in range(4):
                load_cols(4 + n, wv, n * 256)
            sp.wait_ge(xt_lo, 2 * MT)
            sp.dma_start(X[:, :, :], x_v).then_inc(x_in, 16)
            wg, wu = rows(a["ffn1_w_gate"]), rows(a["ffn1_w_up"])
            for c in range(2):
                load_gate_up(S_FFN1 + c, wg, wu, c * P)
            load_ln("ln1", a["ln1_g"], a["ln1_b"])
            ffn_loads(S_FFN1, D_FFN1, wg, wu, a["ffn1_w_down"][0],
                      [lambda c=c: load_cols(S_QKV + c, w_in, c * 256) for c in range(2)])
            sp.wait_ge(ln_par_used, 2)
            sp.dma_start(ABRAW[:, :, :], w_in[:, :, COL_AB:COL_AB + 8]).then_inc(ab_in, 16)
            with sp.Fori(0, 6) as j:
                load_cols(S_QKV + 2 + j, w_in, j * 256 + 512)
            for c in range(2):
                load_cols(S_GATE + c, w_in, COL_GDN + c * 256)
            with sp.Fori(0, 6) as j:
                load_cols(S_GATE + 2 + j, w_in, j * 256 + COL_GDN + 512)
            for c in range(2):
                load_cols(S_P + c, w_in, COL_P + c * 256)
            wdn, wpo = rows(a["w_dn_branch"]), rows(a["w_pool_branch"])

            def load_branch(n, c):
                load_gu(n, (GUraw[:, 0:4, :], wdn[:, :, bass.ds(c, 256)]),
                        (GUraw[:, 4:8, :], wpo[:, :, bass.ds(c, 256)]))

            for c in range(2):
                load_branch(S_MIX + c, c * 256)
            sp.wait_ge(cout_done, 34)
            sp.dma_start(POOLW[:, :, :], a["pool_w"].rearrange("o g c e -> c (o g) e")).then_inc(pool_w_in, 16)
            for b in range(2):
                sp.wait_ge(stored[b], 16 * 17)
            sp.wait_ge(tile_read, Q_POOL + 2 * GROUPS + 4)
            with sp.Fori(0, NT) as n:
                sp.wait_ge(delta_done, n + 1)
                sp.dma_start(QKVS[:, :, :], proj_v[:, 0:CH_Z, bass.ds(n * P, P)]).then_inc(sem("qkv_in"), 16)
                sp.dma_start(ZS[:, :, :], proj_v[:, CH_Z:CH_GDN, bass.ds(n * P, P)]).then_inc(sem("z_in"), 16)
            sp.wait_ge(delta_done, NT + 1)
            wmo = a["w_mix_out"][0]

            def load_gate(j, s, c, h):
                u = 4 * s + 2 * c + h
                sp.wait_ge(gated_b, j * 8 + u + 1)
                sp.dma_start(GATE[:, u % 2, :, :], gate_v[:, :, j * 4 + 2 * s + c, h * HALF:(h + 1) * HALF])\
                    .then_inc(gate_in[u % 2], 16)

            for j in range(2):
                for s in range(2):
                    load_dw(D_MIX + 2 * j + s, wmo, (2 * j + s) * 256)
                    for c in range(2):
                        for h in range(2):
                            load_gate(j, s, c, h)
                    if j == 0:
                        load_branch(S_MIX + 2 + s, (2 + s) * 256)
                    else:
                        load_cols(S_XA + s, rows(a["xa_wq"]), s * 256)
            load_ln("ln2", a["ln2_g"], a["ln2_b"])
            sp.wait_ge(ln_par_used, 3)
            wo = a["xa_wo"][0]
            wg, wu = rows(a["ffn2_w_gate"]), rows(a["ffn2_w_up"])
            for s in range(4):
                sp.wait_ge(kvh_used, s + 1)
                for b in range(2):
                    sp.wait_ge(kv_stored[b], 16 * 5)
                sp.dma_start(KV[:, :, :, :, :].bitcast(F32), kv_scratch[s].rearrange("p v h (c n) -> p v h c n", c=2))\
                    .then_inc(kvh_in, 16)
                load_dw(D_XA + s, wo, s * 256)
                if s < 2:
                    load_cols(S_XA + 2 + s, rows(a["xa_wq"]), (2 + s) * 256)
                else:
                    load_gate_up(S_FFN2 + s - 2, wg, wu, (s - 2) * P)
            sp.wait_ge(kvh_used, 5)
            load_ln("ln3", a["ln3_g"], a["ln3_b"])
            ffn_loads(S_FFN2, D_FFN2, wg, wu, a["ffn2_w_down"][0], [])
            load_ln("ln4", a["ln4_g"], a["ln4_b"])
            for t in range(NT):
                sp.wait_ge(ln_done, LN_BASE["ln4"] + t + 1)
                sp.dma_start(out_v[:, t, :], X[:, t, :]).then_inc(out_stored, 16)
            sp.wait_ge(out_stored, 16 * NT)

        @block.tensor
        def _(pe):
            mm = nc.tensor.matmul

            def split_product(out, terms):
                for i, (lh, ll, rh, rl) in enumerate(terms):
                    mm(out, lh, rh, start=(i == 0), stop=False)
                    mm(out, lh, rl, start=False, stop=False)
                    last = mm(out, ll, rh, start=False, stop=(i == len(terms) - 1))
                return last

            def unit(u, par, products):
                pe.wait_ge(unit_read, u + 1)
                for m, (terms, width) in enumerate(products):
                    last = split_product(PS[:, 2 * par + m, 0:width], terms)
                last.then_inc(unit_ready, 1)

            def feature_terms(s, m, h, ks=range(KD)):
                t = slice(h * HALF, (h + 1) * HALF)
                c = slice(m * P, (m + 1) * P)
                return [(GUh[:, s, k, c], GUl[:, s, k, c], XTh[:, k, t], XTl[:, k, t]) for k in ks]

            def slot_ready(n):
                pe.wait_ge(gu_lo, n + 2)

            def down(m, q0, qp, ready):
                pe.wait_ge(dw_lo, m + 2)
                i = 0
                for h in range(2):
                    ready(h)
                    for t in range(4 * h, 4 * h + 4):
                        for n in range(2):
                            pe.wait_ge(tile_read, q0 + i + 1)
                            tok, cs = slice(t * P, (t + 1) * P), slice(n * 512, (n + 1) * 512)
                            split_product(PS[:, 4 + (qp + i) % 4, :],
                                          [(HTh[:, c, tok], HTl[:, c, tok], DWh[:, c, cs], DWl[:, c, cs])
                                           for c in range(2)]).then_inc(tile_ready, 1)
                            i += 1

            def transposes(q0, t, chunks=KD):
                for g in range(2):
                    q = q0 + 2 * t + g
                    pe.wait_ge(tile_read, q + 1)
                    for k in range(4):
                        c = 4 * g + k
                        last = nc.tensor.transpose(PS[:, 4 + q % 4, k * P:(k + 1) * P],
                                                   X[:, t, c * P:(c + 1) * P], ident)
                    last.then_inc(tile_ready, 1)

            def ffn(s0, u0, d0, q0, h0):
                with pe.Fori(0, PAIRS) as j:
                    for c in range(2):
                        slot_ready(s0 + 2 * j + c)
                        for h in range(2):
                            i = 2 * c + h
                            unit(u0 + 4 * j + i, i % 2,
                                 [(feature_terms(c, m, h), HALF) for m in range(2)])
                    down(d0 + j, q0 + 16 * j, q0,
                         lambda h: pe.wait_ge(h_lo, h0 + 4 * j + 3 + h + 2))

            pe.wait_ge(const_in, 16 * 7)
            for t in range(MT):
                pe.wait_ge(ln_done, LN_BASE["mem"] + t + 1)
                transposes(Q_MEM, t)
            pe.wait_ge(xt_lo, XT_BASE["mem"] + 2 * MT)
            for s in range(4):
                slot_ready(s)
                unit(s, s % 2, [([(GUh[:, s % 2, k, m * P:(m + 1) * P], GUl[:, s % 2, k, m * P:(m + 1) * P],
                                   XTh[:, k, 0:N_MEM], XTl[:, k, 0:N_MEM]) for k in range(KD)], N_MEM)
                                for m in range(2)])
            for s in range(4):
                slot_ready(4 + s)
                unit(4 + s, s % 2, [([(XTh[:, k, m * P:(m + 1) * P], XTl[:, k, m * P:(m + 1) * P],
                                       GUh[:, s % 2, k, :], GUl[:, s % 2, k, :]) for k in range(KD)], XD)
                                    for m in range(2)])
            pe.wait_ge(x_in, 16)
            for t in range(NT):
                transposes(Q_X, t)
            pe.wait_ge(xt_lo, XT_BASE["x"] + 2 * NT)
            ffn(S_FFN1, U_FFN1, D_FFN1, Q_FFN1, H_FFN1)
            for t in range(NT):
                pe.wait_ge(ln_done, LN_BASE["ln1"] + t + 1)
                transposes(Q_LN1, t)
            pe.wait_ge(xt_lo, XT_BASE["ln1"] + 2 * NT)

            pe.wait_ge(ab_split, 2)
            pe.wait_ge(tile_read, Q_AB + 1)
            for t in range(NT):
                tok = slice(t * P, (t + 1) * P)
                last = split_product(PS[:, 4 + Q_AB % 4, 8 * t:8 * t + 8],
                                     [(XTh[:, k, tok], XTl[:, k, tok], ABh[:, k, :], ABl[:, k, :])
                                      for k in range(KD)])
            last.then_inc(tile_ready, 1)
            pe.wait_ge(ab_done, 1)
            g = GT[:, :, G_G, :]
            mm(PS[:, 4, 0:NT * HEADS], MASK[:, M_UP, :], g, start=True, stop=True)
            mm(PS[:, 5, 0:NT * HEADS], MASK[:, M_ONE, :], g, start=True, stop=True).then_inc(sem("cum_ready"), 1)

            def project(n, first_u, count):
                with pe.Fori(0, count) as j:
                    for s in range(2):
                        slot_ready(n + 2 * j + s)
                        for h in range(2):
                            unit(first_u + 4 * j + 2 * s + h, h, [(feature_terms(s, m, h), HALF) for m in range(2)])

            pe.wait_ge(sem("cum_read"), 1)
            project(S_QKV, U_QKV, (S_MIX - S_QKV) // 2)

            pe.wait_ge(pool_w_in, 16)
            for g in range(GROUPS):
                pe.wait_ge(pooled, g + 1)
                for h in range(2):
                    q = Q_POOL + 2 * g + h
                    pe.wait_ge(tile_read, q + 1)
                    mm(PS[:, 4 + q % 4, :], POOLW[:, g, :], MIXED[:, g, h * HALF:(h + 1) * HALF],
                       start=True, stop=True).then_inc(tile_ready, 1)

            pe.wait_ge(state_zero, 1)
            pe.wait_ge(tile_read, Q_MIX + 4)
            pe.wait_ge(unit_read, U_MIX + 2)
            with pe.Fori(0, NT) as n:
                def need(name):
                    pe.wait_ge(sem(name), n + 1)

                def flip(bank, src, name):
                    for h in range(HEADS):
                        last = nc.tensor.transpose(PS[:, bank, h * P:(h + 1) * P], src(h), ident)
                    last.then_inc(sem(name), 1)

                def product(bank, lhsT, rhs, name):
                    for h in range(HEADS):
                        last = mm(PS[:, bank, h * P:(h + 1) * P], lhsT(h), rhs(h), start=True, stop=True)
                    last.then_inc(sem(name), 1)

                of = lambda t: (lambda h: t[:, h, :])
                pe.wait_ge(delta_done, n + 1)
                pe.wait_ge(sem("qkv_in"), n * 16 + 16)
                flip(0, lambda h: QKVS[:, HEADS + h, :], "k_tok")
                flip(1, lambda h: QKVS[:, h, :], "q_tok")
                flip(2, lambda h: QKVS[:, 2 * HEADS + h, :], "v_tok")
                need("scalars")
                product(5, lambda h: GTN[:, G_G, h:h + 1].broadcast_to([P, P]), lambda h: MASK[:, M_UP, :], "cum_rows")
                need("k_unit")
                flip(3, of(KN), "kT_ps")
                need("q_unit")
                flip(4, of(QN), "qT_ps")
                need("kT")
                product(6, of(KT), of(KT), "kk")
                need("qT")
                product(7, of(KT), of(QT), "qk")
                need("low")
                flip(0, of(L), "lowT_ps")
                need("inv0")
                flip(1, of(T), "inv0T_ps")
                need("lowT")
                for lv in range(LEVELS):
                    if lv:
                        pe.wait_ge(sem("inv"), n * (LEVELS - 1) + lv)
                    product(2, of(LT), of(T), "lev_m_ps")
                    pe.wait_ge(sem("lev_m"), n * LEVELS + lv + 1)
                    if lv == 0:
                        need("inv0T")
                    else:
                        pe.wait_ge(sem("invT"), n * LEVELS + lv)
                    if lv < LEVELS - 1:
                        product(3, of(TT), of(MM), "lev_p")
                    product(4, of(MM), of(TT), "lev_pT")
                product(5, of(KT), of(ST), "k_state")
                product(6, of(QT), of(ST), "q_state")
                need("resid")
                pe.wait_ge(sem("invT"), n * LEVELS + LEVELS)
                product(7, of(TT), of(R), "v_new_ps")
                need("v_new")
                need("k_dec")
                product(1, of(KDEC), of(VN), "kv_outer")
                need("att")
                product(0, of(ATT), of(VN), "o_intra")
                need("o_unit")
                flip(2, of(ON), "oT_ps")

            pe.wait_ge(delta_done, NT + 1)
            for s in range(4):
                slot_ready(S_MIX + s)
                for c in range(2):
                    for h in range(2):
                        i = 2 * c + h
                        unit(U_MIX + 4 * s + i, i % 2,
                             [(feature_terms(s % 2, c, h, range(0, 4)), HALF),
                              (feature_terms(s % 2, c, h, range(4, 8)), HALF)])
                down(D_MIX + s, Q_MIX + 16 * s, Q_MIX,
                     lambda h: pe.wait_ge(h_lo, H_MIX + 4 * s + 3 + h + 2))
            for t in range(NT):
                pe.wait_ge(ln_done, LN_BASE["ln2"] + t + 1)
                transposes(Q_LN2, t)
            pe.wait_ge(xt_lo, XT_BASE["ln2"] + 2 * NT)

            for s in range(4):
                slot_ready(S_XA + s)
                for h in range(2):
                    unit(U_XA + 4 * s + h, h, [(feature_terms(s % 2, m, h), HALF) for m in range(2)])
                pe.wait_ge(kvh_in, 16 * (s + 1))
                pe.wait_ge(tile_read, Q_XA + 16 * s + 4)
                for i in range(NT + 2):
                    if i < NT:
                        if i % 4 == 0:
                            pe.wait_ge(q_lo, 2 * s + i // 4 + 1)
                        pe.wait_ge(s_read, 8 * s + i + 1)
                        tok = slice(i * P, (i + 1) * P)
                        split_product(PS[:, 4 + i % 2, 0:N_MEM],
                                      [(HTh[:, c, tok], HTl[:, c, tok], KV[:, 0, 0, c, :], KV[:, 0, 1, c, :])
                                       for c in range(2)]).then_inc(s_ready, 1)
                    if i >= 2:
                        t = i - 2
                        pe.wait_ge(p_norm, 8 * s + t + 1)
                        pe.wait_ge(pt_lo, 8 * s + t + 1)
                        for m in range(MT):
                            last = nc.tensor.transpose(PS[:, 6 + t % 2, m * P:(m + 1) * P],
                                                       PR[:, t % 4, m * P:(m + 1) * P], ident)
                        last.then_inc(pt_ready, 1)
                    if i in (NT // 2 + 1, NT + 1):
                        h = i // (NT + 1)
                        pe.wait_ge(pt_lo, 8 * s + 4 * h + 4 + 2)
                        unit(U_XA + 4 * s + 2 + h, h,
                             [([(KV[:, 1, 0, m, c * P:(c + 1) * P], KV[:, 1, 1, m, c * P:(c + 1) * P],
                                 PTh[:, m, :], PTl[:, m, :]) for m in range(MT)], HALF) for c in range(2)])
                down(D_XA + s, Q_XA + 16 * s, Q_XA, lambda h: pe.wait_ge(o_lo, 2 * s + h + 1))
            for t in range(NT):
                pe.wait_ge(ln_done, LN_BASE["ln3"] + t + 1)
                transposes(Q_LN3, t)
            pe.wait_ge(xt_lo, XT_BASE["ln3"] + 2 * NT)
            ffn(S_FFN2, U_FFN2, D_FFN2, Q_FFN2, H_FFN2)

        @block.scalar
        def _(act):
            op = nc.scalar.activation

            def split_gu(n, par):
                act.wait_ge(gu_in, n * 32 + 32)
                op(GUh[:, par, :, :], GUraw[:, :, :], ACT.Copy).then_inc(gu_hi, 1)

            def split_dw(m, q):
                act.wait_ge(dw_in, m * 32 + 32)
                act.wait_ge(tile_ready, q)
                op(DWh[:, :, :], DWraw[:, :, :], ACT.Copy).then_inc(dw_hi, 1)

            def unit_wait(u):
                act.wait_ge(unit_ready, u + 1)

            def transposed_hi(base, q0, t, off=0):
                for g in range(2):
                    q = q0 + 2 * t + g
                    act.wait_ge(tile_ready, q + 1)
                    op(XTh[:, 4 * g:4 * g + 4, t * P:(t + 1) * P],
                       PS[:, 4 + q % 4, :].rearrange("p (k t) -> p k t", k=4), ACT.Copy).then_inc(xt_hi, 1)

            def normalise(name, half):
                b = LN_BASE[name]
                n = min(4, LN_TILES[name])
                act.wait_ge(ln_nmr, LN_ORDER_HALF[name] + half + 1)
                for t in range(n * half, n * half + n):
                    op(X[:, t, :], X[:, t, :], ACT.Identity, bias=NMR[:, t:t + 1],
                       scale=RSTD[:, t:t + 1]).then_inc(ln_hat, 1)

            def layer_norm(name):
                for half in range(2 if LN_TILES[name] > 4 else 1):
                    normalise(name, half)
                if name in Q_BASE:
                    for t in range(LN_TILES[name]):
                        transposed_hi(XT_BASE[name], Q_BASE[name], t)

            def ffn(s0, u0, d0, q0, h0, last_phase):
                def pair(j, more):
                    split_dw(d0 + j, q0 + 16 * j)
                    for c in range(2):
                        for h in range(2):
                            i = 2 * c + h
                            u = u0 + 4 * j + i
                            unit_wait(u)
                            op(SIG[:, i % 2, :], PS[:, 2 * (i % 2), :], ACT.Silu).then_inc(act_out, 1)
                            act.wait_ge(unit_read, u + 3)
                            op(HTh[:, c, h * HALF:(h + 1) * HALF], H32[:, i % 2, :], ACT.Copy).then_inc(h_hi, 1)
                        if more:
                            split_gu(s0 + 2 + 2 * j + c, c)
                if last_phase:
                    with act.Fori(0, PAIRS - 1) as j:
                        pair(j, True)
                    pair(PAIRS - 1, False)
                else:
                    with act.Fori(0, PAIRS) as j:
                        pair(j, True)

            for n in range(2):
                split_gu(n, n)
            layer_norm("mem")
            for s in range(8):
                unit_wait(s)
                act.wait_ge(kv_stored[s % 2], 16 * (s // 2 + 1))
                v = KVO[:, s % 2, 0, :].rearrange("p (c n) -> p c n", c=2)
                op(v, PS[:, 2 * (s % 2):2 * (s % 2) + 2, 0:256], ACT.Copy).then_inc(kv_hi, 1)
                split_gu(s + 2, s % 2)
                act.wait_ge(kv_lo, s + 1)
                act.dma_start(kv_scratch[s % 4, :, s // 4, :, :], KVO[:, s % 2, :, :].bitcast(F32))\
                    .then_inc(kv_stored[s % 2], 16)
            for b in range(2):
                act.wait_ge(kv_stored[b], 16 * 5)
            for t in range(NT):
                transposed_hi(XT_BASE["x"], Q_X, t)
            ffn(S_FFN1, U_FFN1, D_FFN1, Q_FFN1, H_FFN1, False)
            layer_norm("ln1")

            act.wait_ge(ab_in, 16)
            op(ABh[:, :, :], ABRAW[:, :, :], ACT.Copy).then_inc(ab_split, 1)
            act.wait_ge(sem("ab_sum"), 1)
            op(GT[:, :, G_BETA, :], ABT[:, :, HEADS:], ACT.Sigmoid).then_inc(sem("beta"), 1)
            op(AB2[:, :, :], AB1[:, :, :], ACT.Abs).then_inc(sem("ab_abs"), 1)
            act.wait_ge(sem("ab_abs"), 1)
            op(AB2[:, :, :], AB2[:, :, :], ACT.Exp, scale=-1.0).then_inc(sem("ab_abs"), 1)
            op(AB4[:, :], HPAR[:, 1, :], ACT.Exp).then_inc(sem("a_exp"), 1)
            act.wait_ge(sem("ab_abs"), 2)
            op(AB2[:, :, :], AB2[:, :, :], ACT.Ln, bias=1.0).then_inc(sem("ab_ln"), 1)
            act.wait_ge(sem("cum_read"), 1)
            op(GT[:, :, G_ECUM:G_ELAST + 1, :], GT[:, :, G_ECUM:G_ELAST + 1, :], ACT.Exp).then_inc(sem("g_exp"), 1)

            def store(j, par, chunks, h):
                act.wait_ge(cout_done, j + 3)
                act.dma_start(chunks[:, :, h * HALF:(h + 1) * HALF], COUT[:, par, :, :]).then_inc(stored[par], 16)

            with act.Fori(0, 3) as j:
                for s in range(2):
                    for h in range(2):
                        v = 4 * j + 2 * s + h
                        act.wait_ge(unit_ready, v + U_QKV + 1)
                        act.wait_ge(conv_done, v + 1 if h == 0 else v)
                        op(RAW[:, :, HALO + h * HALF:HALO + (h + 1) * HALF], PS[:, 2 * h:2 * h + 2, :],
                           ACT.Copy).then_inc(unit_read, 1)
                        act.wait_ge(conv_done, v + 2)
                        act.wait_ge(stored[h], j * 32 + 16 * s + 16)
                        op(COUT[:, h, :, :], CACC[:, h, :, :], ACT.Silu).then_inc(cout_done, 1)
                        store(v, h, proj_v[:, bass.ds(4 * j + 2 * s, 2), :], h)
                    split_gu(S_QKV + 2 + 2 * j + s, s)
            for s in range(2):
                for h in range(2):
                    v = 12 + 2 * s + h
                    act.wait_ge(unit_ready, v + U_QKV + 1)
                    act.wait_ge(stored[h], 16 * (v // 2 + 1))
                    op(COUT[:, h, :, :], PS[:, 2 * h:2 * h + 2, :], ACT.Silu).then_inc(cout_done, 1)
                    act.wait_ge(cout_done, v + 3)
                    nc.scalar.sem_inc(unit_read, 1)
                    store(v, h, proj_v[:, CH_Z + 2 * s:CH_Z + 2 * s + 2, :], h)
                split_gu(S_Z + 2 + s, s)
            with act.Fori(0, 4) as j:
                for s in range(2):
                    for h in range(2):
                        v = 4 * j + 16 + 2 * s + h
                        act.wait_ge(unit_ready, v + U_QKV + 1)
                        act.wait_ge(stored[h], j * 32 + 16 * (8 + s + 1))
                        op(COUT[:, h, :, :], PS[:, 2 * h:2 * h + 2, :], ACT.Sigmoid).then_inc(cout_done, 1)
                        act.wait_ge(cout_done, v + 3)
                        nc.scalar.sem_inc(unit_read, 1)
                        store(v, h, proj_v[:, bass.ds(4 * j + CH_GDN + 2 * s, 2), :], h)
                    split_gu(S_GATE + 2 + 2 * j + s, s)
            for s in range(2):
                for h in range(2):
                    act.wait_ge(unit_ready, U_P + 2 * s + h + 1)
                    if s == 1 and h == 0:
                        act.wait_ge(pooled, 2)
                    op(RAW[:, :, HALO + h * HALF:HALO + (h + 1) * HALF], PS[:, 2 * h:2 * h + 2, :],
                       ACT.Copy).then_inc(unit_read, 1)
                split_gu(S_P + 2 + s, s)
            for g in range(GROUPS):
                for h in range(2):
                    q = Q_POOL + 2 * g + h
                    act.wait_ge(tile_ready, q + 1)
                    op(XTh[:, 4 + g, h * HALF:(h + 1) * HALF], PS[:, 4 + q % 4, :], ACT.Copy,
                       scale=PSCALE[:, g:g + 1]).then_inc(pool_hi, 1)

            with act.Fori(0, NT) as n:
                def need(name):
                    act.wait_ge(sem(name), n + 1)

                def copy(dst, bank, name):
                    op(dst[:, :, :], PS[:, bank, :].rearrange("p (h t) -> p h t", h=HEADS), ACT.Copy)\
                        .then_inc(sem(name), 1)

                act.wait_ge(delta_done, n + 1)
                for src, dst, bank, name in (("k_tok", K0, 0, "k0"), ("q_tok", Q0, 1, "q0"), ("v_tok", V0, 2, "v0"),
                                             ("kT_ps", KT, 3, "kT"), ("qT_ps", QT, 4, "qT")):
                    need(src)
                    copy(dst, bank, name)
                need("dif_pos")
                op(E1[:, :, :], E1[:, :, :], ACT.Exp, scale=-1.0).then_inc(sem("decay"), 1)
                need("dif_neg")
                op(E2[:, :, :], E2[:, :, :], ACT.Exp).then_inc(sem("decayT"), 1)
                need("lowT_ps")
                copy(LT, 0, "lowT")
                need("inv0T_ps")
                copy(TT, 1, "inv0T")
                need("q_state")
                for h in range(HEADS):
                    last = op(QS[:, h, :], PS[:, 6, h * P:(h + 1) * P], ACT.Copy, scale=GTN[:, G_ECUM, h:h + 1])
                last.then_inc(sem("q_state_dec"), 1)
                need("v_new_ps")
                copy(VN, 7, "v_new")
                need("oT")
                op(XTh[:, 0:HEADS, bass.ds(n * P, P)], OZ[:, :, :], ACT.Copy).then_inc(sem("oT_hi"), 1)

            for s in range(4):
                if s == 0:
                    act.wait_ge(delta_done, NT + 1)
                split_dw(D_MIX + s, Q_MIX + 16 * s)
                for i in range(4):
                    u = U_MIX + 4 * s + i
                    unit_wait(u)
                    act.wait_ge(sem("merged"), 4 * s + i + 1)
                    op(HTh[:, i // 2, i % 2 * HALF:(i % 2 + 1) * HALF], H32[:, i % 2, :], ACT.Copy)\
                        .then_inc(h_hi, 1)
                split_gu(S_MIX + 2 + s, s % 2)
            layer_norm("ln2")

            for s in range(4):
                for h in range(2):
                    unit_wait(U_XA + 4 * s + h)
                    if s:
                        act.wait_ge(tile_ready, Q_XA + 16 * s)
                    op(HTh[:, :, h * HALF:(h + 1) * HALF], PS[:, 2 * h:2 * h + 2, :], ACT.Copy,
                       scale=XD ** -0.5).then_inc(q_hi, 1)
                split_gu(S_XA + 2 + s, s % 2)
                split_dw(D_XA + s, Q_XA + 16 * s)
                for i in range(NT + 2):
                    if i < NT:
                        act.wait_ge(neg_max, 8 * s + i + 1)
                        if 8 * s + i >= 4:
                            act.wait_ge(pt_ready, 8 * s + i - 3)
                        op(PR[:, i % 4, :], PS[:, 4 + i % 2, 0:N_MEM], ACT.Exp, bias=NEGMAX[:, i:i + 1],
                           accum_out=RSUM[:, i:i + 1]).then_inc(s_read, 1)
                    if i >= 2:
                        t = i - 2
                        act.wait_ge(pt_ready, 8 * s + t + 1)
                        if t % 4 == 0 and 2 * s + t // 4 >= 1:
                            act.wait_ge(unit_ready, U_XA + 4 * s + 3 if t else U_XA + 4 * s)
                        op(PTh[:, :, t % 4 * P:(t % 4 + 1) * P],
                           PS[:, 6 + t % 2, 0:N_MEM].rearrange("p (m t) -> p m t", m=MT), ACT.Copy)\
                            .then_inc(pt_hi, 1)
                    if i in (NT // 2 + 1, NT + 1):
                        h = i // (NT + 1)
                        unit_wait(U_XA + 4 * s + 2 + h)
                        op(HTh[:, :, h * HALF:(h + 1) * HALF], PS[:, 2 * h:2 * h + 2, :], ACT.Copy)\
                            .then_inc(o_hi, 1)
            layer_norm("ln3")
            ffn(S_FFN2, U_FFN2, D_FFN2, Q_FFN2, H_FFN2, True)
            layer_norm("ln4")

        @block.gpsimd
        def _(pool):
            tt = nc.gpsimd.tensor_tensor

            def split_gu(n, par):
                pool.wait_ge(gu_hi, n + 1)
                tt(GUl[:, par, :, :], GUraw[:, :, :], GUh[:, par, :, :].bitcast(F32), ALU.subtract)\
                    .then_inc(gu_lo, 1)

            def split_dw(m):
                pool.wait_ge(dw_hi, m + 1)
                tt(DWl[:, :, :], DWraw[:, :, :], DWh[:, :, :].bitcast(F32), ALU.subtract).then_inc(dw_lo, 1)

            def split_half(v, i):
                pool.wait_ge(h_hi, v + 1)
                to = (slice(None), i // 2, slice(i % 2 * HALF, (i % 2 + 1) * HALF))
                tt(HTl[to], H32[:, i % 2, :], HTh[to].bitcast(F32), ALU.subtract).then_inc(h_lo, 1)

            def layer_norm(name):
                n = min(4, LN_TILES[name])
                for half in range(2 if LN_TILES[name] > 4 else 1):
                    pool.wait_ge(ln_var, LN_ORDER_HALF[name] + half + 1)
                    c = slice(n * half, n * half + n)
                    tt(RSTD[:, c], VE[:, c], COUNT[:, HALO:HALO + n], ALU.pow).then_inc(ln_rstd, 1)

            def ffn(s0, d0, h0, last_phase):
                def pair(j, more):
                    split_dw(d0 + j)
                    for c in range(2):
                        for h in range(2):
                            split_half(h0 + 4 * j + 2 * c + h, 2 * c + h)
                        if more:
                            split_gu(s0 + 2 + 2 * j + c, c)
                if last_phase:
                    with pool.Fori(0, PAIRS - 1) as j:
                        pair(j, True)
                    pair(PAIRS - 1, False)
                else:
                    with pool.Fori(0, PAIRS) as j:
                        pair(j, True)

            pool.sem_inc(gu_lo, 1)
            pool.sem_inc(dw_lo, 1)
            pool.sem_inc(h_lo, 2)
            pool.sem_inc(delta_done, 1)
            pool.wait_ge(const_in, 16 * 7)
            for n in range(2):
                split_gu(n, n)
            layer_norm("mem")
            for s in range(8):
                split_gu(s + 2, s % 2)
            ffn(S_FFN1, D_FFN1, H_FFN1, False)
            layer_norm("ln1")
            pool.wait_ge(ab_split, 1)
            tt(ABl[:, :, :], ABRAW[:, :, :], ABh[:, :, :].bitcast(F32), ALU.subtract).then_inc(ab_split, 1)
            with pool.Fori(0, (S_MIX - S_QKV) // 2) as j:
                for s in range(2):
                    split_gu(S_QKV + 2 + 2 * j + s, s)

            with pool.Fori(0, NT) as n:
                def need(name):
                    pool.wait_ge(sem(name), n + 1)

                over = lambda kind: GTN[:, kind, :].unsqueeze(2).broadcast_to([P, HEADS, P])
                mask = lambda m: MASK[:, m, :].unsqueeze(1).broadcast_to([P, HEADS, P])
                pool.wait_ge(delta_done, n + 1)
                need("norm_arg")
                tt(RN[:, 0:2, :], SS[:, 0:2, :], COUNT[:, HALO:HALO + 8].rearrange("p (a h) -> p a h", a=2),
                   ALU.pow).then_inc(sem("norm_inv"), 1)
                need("v0")
                tt(VB[:, :, :], V0[:, :, :], over(G_BETA), ALU.mult).then_inc(sem("v_beta"), 1)
                need("decay")
                tt(E1[:, :, :], E1[:, :, :], mask(M_LOW), ALU.mult).then_inc(sem("decay_low"), 1)
                need("decay_low")
                tt(E1[:, :, :], E1[:, :, :], over(G_BETA), ALU.mult).then_inc(sem("decay_beta"), 1)
                need("decayT")
                tt(E2[:, :, :], E2[:, :, :], mask(M_UP), ALU.mult).then_inc(sem("decayT_up"), 1)
                need("low")
                tt(T[:, :, :], L[:, :, :], mask(M_NEG1), ALU.mult).then_inc(sem("inv_part"), 1)
                need("inv_part")
                tt(T[:, :, :], T[:, :, :], mask(M_ID), ALU.add).then_inc(sem("inv0"), 1)
                need("k_unit")
                tt(KDEC[:, :, :], KN[:, :, :], over(G_ETAIL), ALU.mult).then_inc(sem("k_dec"), 1)
                need("rms_arg")
                tt(RN[:, 2, :], SS[:, 3, :], COUNT[:, HALO:HALO + HEADS], ALU.pow).then_inc(sem("rms_inv"), 1)
                need("oT_hi")
                to = XTl[:, 0:HEADS, bass.ds(n * P, P)]
                hi = XTh[:, 0:HEADS, bass.ds(n * P, P)].bitcast(F32)
                tt(to, OZ[:, :, :], hi, ALU.subtract).then_inc(delta_done, 1)

            for s in range(4):
                split_dw(D_MIX + s)
                for i in range(4):
                    v = 4 * s + i
                    pool.wait_ge(gated_b, v + 3)
                    tt(H32[:, i % 2, :], H32[:, i % 2, :], SIG[:, i % 2, :], ALU.add).then_inc(sem("merged"), 1)
                    split_half(H_MIX + v, i)
                split_gu(S_MIX + 2 + s, s % 2)
            layer_norm("ln2")
            for s in range(4):
                split_gu(S_XA + 2 + s, s % 2)
                split_dw(D_XA + s)
            layer_norm("ln3")
            ffn(S_FFN2, D_FFN2, H_FFN2, True)
            layer_norm("ln4")

        @block.vector
        def _(dve):
            v = nc.vector

            steps = [0]

            def chain(ins):
                steps[0] += 1
                ins.then_inc(small_step, 1)
                dve.wait_ge(small_step, steps[0])

            def stats(t):
                for i in range(2):
                    chain(v.bn_stats(BNS[:, i, :], X[:, t, i * 512:(i + 1) * 512]))
                chain(v.bn_aggr(MV[:, t, :], BNS[:, :, :]))

            def layer_norm(name):
                tiles = LN_TILES[name]
                n = min(4, tiles)
                k = LN_ORDER[name]
                for half in range(2 if tiles > 4 else 1):
                    for t in range(n * half, n * half + n):
                        stats(t)
                    c = slice(n * half, n * half + n)
                    v.tensor_scalar(VE[:, c], MV[:, c, 1], LN_EPS, None, ALU.add).then_inc(ln_var, 1)
                    dve.wait_ge(ln_rstd, LN_ORDER_HALF[name] + half + 1)
                    v.scalar_tensor_tensor(NMR[:, c], MV[:, c, 0], -1.0, RSTD[:, c], ALU.mult, ALU.mult)\
                        .then_inc(ln_nmr, 1)
                dve.wait_ge(ln_par_in, 32 * (k + 1))
                for t in range(tiles):
                    dve.wait_ge(ln_hat, LN_BASE[name] + t + 1)
                    v.tensor_tensor(X[:, t, :], X[:, t, :], LNG[:, :], ALU.mult).then_inc(ln_scaled, 1)
                    dve.wait_ge(ln_scaled, LN_BASE[name] + t + 1)
                    v.tensor_tensor(X[:, t, :], X[:, t, :], LNB[:, :], ALU.add).then_inc(ln_done, 1)
                dve.wait_ge(ln_done, LN_BASE[name] + tiles)
                dve.sem_inc(ln_par_used, 1)
                if name in Q_BASE:
                    transposed_lo(name, tiles)

            def transposed_lo(name, tiles):
                for t in range(tiles):
                    for g in range(2):
                        i = 2 * t + g
                        q = Q_BASE[name] + i
                        dve.wait_ge(xt_hi, XT_BASE[name] + i + 1)
                        to = (slice(None), slice(4 * g, 4 * g + 4), slice(t * P, (t + 1) * P))
                        v.tensor_tensor(XTl[to], PS[:, 4 + q % 4, :].rearrange("p (k t) -> p k t", k=4),
                                        XTh[to].bitcast(F32), ALU.subtract).then_inc(xt_lo, 1)
                        dve.wait_ge(xt_lo, XT_BASE[name] + i + 1)
                        dve.sem_inc(tile_read, 1)
                    if name != "mem":
                        v.tensor_scalar(X[:, t, :], X[:, t, :], ALPHA, None, ALU.mult).then_inc(x_scaled, 1)

            def residual_add(q0, qp):
                i = 0
                for t in range(NT):
                    for n in range(2):
                        dve.wait_ge(tile_ready, q0 + i + 1)
                        c = slice(n * 512, (n + 1) * 512)
                        v.tensor_tensor(X[:, t, c], X[:, t, c], PS[:, 4 + (qp + i) % 4, :], ALU.add)\
                            .then_inc(tile_read, 1)
                        i += 1

            def ffn(u0, q0, h0):
                with dve.Fori(0, PAIRS) as j:
                    for i in range(4):
                        dve.wait_ge(act_out, j * 4 + (h0 if h0 == 0 else 4 * PAIRS) + i + 1)
                        dve.wait_ge(h_lo, j * 4 + h0 + i + 1)
                        v.scalar_tensor_tensor(H32[:, i % 2, :], SIG[:, i % 2, :], 0.5,
                                               PS[:, 2 * (i % 2) + 1, :], ALU.mult, ALU.mult)\
                            .then_inc(unit_read, 1)
                    residual_add(q0 + 16 * j, q0)

            dve.sem_inc(unit_read, 2)
            dve.sem_inc(tile_read, 4)
            dve.sem_inc(kv_stored[0], 16)
            dve.sem_inc(kv_stored[1], 16)
            dve.sem_inc(stored[0], 16)
            dve.sem_inc(stored[1], 16)
            dve.sem_inc(conv_done, 1)
            dve.sem_inc(cout_done, 2)
            dve.sem_inc(gated_b, 2)
            dve.sem_inc(kvh_used, 1)
            dve.sem_inc(s_read, 2)
            dve.sem_inc(pt_lo, 2)

            dve.wait_ge(mem_in, 16)
            layer_norm("mem")
            for s in range(8):
                dve.wait_ge(kv_hi, s + 1)
                r = lambda i: KVO[:, s % 2, i, :].rearrange("p (c n) -> p c n", c=2)
                v.tensor_tensor(r(1), PS[:, 2 * (s % 2):2 * (s % 2) + 2, 0:256], r(0).bitcast(F32),
                                ALU.subtract).then_inc(kv_lo, 1)
                dve.wait_ge(kv_lo, s + 1)
                dve.sem_inc(unit_read, 1)
            transposed_lo("x", NT)
            dve.wait_ge(x_scaled, NT)
            ffn(U_FFN1, Q_FFN1, H_FFN1)
            dve.wait_ge(tile_read, Q_LN1 + 4)
            layer_norm("ln1")

            dve.wait_ge(tile_ready, Q_AB + 1)
            v.tensor_copy(ABT[:, :, :], PS[:, 4 + Q_AB % 4, 0:8 * NT].rearrange("p (t c) -> p t c", t=NT))\
                .then_inc(tile_read, 1)
            dve.wait_ge(tile_read, Q_AB + 5)
            v.tensor_tensor(AB1[:, :, :], ABT[:, :, 0:HEADS],
                            HPAR[:, 0, :].unsqueeze(1).broadcast_to([P, NT, HEADS]), ALU.add)\
                .then_inc(sem("ab_sum"), 1)
            dve.wait_ge(sem("ab_sum"), 1)
            chain(v.tensor_scalar(AB3[:, :, :], AB1[:, :, :], 0.0, None, ALU.max))
            dve.wait_ge(sem("ab_ln"), 1)
            chain(v.tensor_tensor(AB3[:, :, :], AB3[:, :, :], AB2[:, :, :], ALU.add))
            dve.wait_ge(sem("a_exp"), 1)
            v.scalar_tensor_tensor(GT[:, :, G_G, :], AB3[:, :, :], -1.0,
                                   AB4[:, :].unsqueeze(1).broadcast_to([P, NT, HEADS]), ALU.mult, ALU.mult)\
                .then_inc(ab_done, 1)
            dve.wait_ge(sem("cum_ready"), 1)
            cum = PS[:, 4, 0:NT * HEADS].rearrange("p (t h) -> p t h", h=HEADS)
            total = PS[:, 5, 0:NT * HEADS].rearrange("p (t h) -> p t h", h=HEADS)
            chain(v.tensor_copy(GT[:, :, G_CUM, :], cum))
            v.tensor_copy(GT[:, :, G_ECUM, :], cum)
            v.tensor_tensor(GT[:, :, G_ETAIL, :], total, GT[:, :, G_CUM, :], ALU.subtract)
            v.tensor_copy(GT[:, :, G_ELAST, :], total).then_inc(sem("cum_read"), 1)
            dve.wait_ge(sem("g_exp"), 1)
            dve.wait_ge(sem("beta"), 1)
            chain(v.scalar_tensor_tensor(GT[:, :, G_NBE, :], GT[:, :, G_BETA, :], -1.0, GT[:, :, G_ECUM, :],
                                         ALU.mult, ALU.mult))

            chain(v.memset(RAW[:, :, 0:HALO], 0.0))
            with dve.Fori(0, 3) as j:
                for s in range(2):
                    for h in range(2):
                        w = 4 * j + 2 * s + h
                        dve.wait_ge(unit_read, w + U_QKV + 3)
                        dve.wait_ge(cout_done, w + 1)
                        for k in range(CONV_K):
                            if k:
                                dve.wait_ge(tap, w * (2 * CONV_K - 2) + 2 * k)
                            for c in range(2):
                                src = RAW[:, c, HALO - CONV_K + 1 + k + h * HALF:HALO - CONV_K + 1 + k + (h + 1) * HALF]
                                wt = CONVW[:, bass.ds(4 * j + 2 * s + c, 1), k]
                                if k == 0:
                                    ins = v.tensor_scalar(CACC[:, h, c, :], src, wt, None, ALU.mult)
                                else:
                                    ins = v.scalar_tensor_tensor(CACC[:, h, c, :], src, wt, CACC[:, h, c, :],
                                                                 ALU.mult, ALU.add)
                                if k < CONV_K - 1:
                                    ins.then_inc(tap, 1)
                        ins.then_inc(conv_done, 1)
            dve.wait_ge(cout_done, 12 + 2)
            chain(v.memset(WSUM[:, :, 0:HALO], 0.0))
            for g in range(GROUPS):
                if g % 2 == 0:
                    dve.wait_ge(unit_read, U_P + g + 2 + 2)
                src = RAW[:, g % 2, :]
                for i in range(g + 1):
                    dst = WSUM[:, i % 2, :]
                    lag = 1 << i
                    chain(v.tensor_tensor(dst[:, HALO:], src[:, HALO:], src[:, HALO - lag:HALO + SEQ - lag],
                                          ALU.add))
                    src = dst
                win = 2 << g
                frame = RAW[:, g % 2, HALO:]
                chain(v.scalar_tensor_tensor(MIXED[:, g, :], src[:, HALO:], 1.0 / win, frame, ALU.mult,
                                             ALU.subtract))
                chain(v.tensor_tensor(MIXED[:, g, 0:win], src[:, HALO:HALO + win], COUNT[:, 0:win], ALU.mult))
                v.tensor_tensor(MIXED[:, g, 0:win], MIXED[:, g, 0:win], frame[:, 0:win], ALU.subtract)\
                    .then_inc(pooled, 1)
            for g in range(GROUPS):
                for h in range(2):
                    i = 2 * g + h
                    dve.wait_ge(pool_hi, i + 1)
                    to = (slice(None), 4 + g, slice(h * HALF, (h + 1) * HALF))
                    v.scalar_tensor_tensor(XTl[to], PS[:, 4 + (Q_POOL + i) % 4, :], PSCALE[:, g:g + 1],
                                           XTh[to].bitcast(F32), ALU.mult, ALU.subtract).then_inc(tile_read, 1)
            dve.wait_ge(tile_read, Q_MIX + 4)
            v.memset(ST[:, :, :], 0.0).then_inc(state_zero, 1)

            with dve.Fori(0, NT) as n:
                def need(name):
                    dve.wait_ge(sem(name), n + 1)

                def bank(b):
                    return PS[:, b, :].rearrange("p (h t) -> p h t", h=HEADS)

                def signal(ins, name):
                    ins.then_inc(sem(name), 1)

                over = lambda t: t.unsqueeze(2).broadcast_to([P, HEADS, P])
                mask = lambda m: MASK[:, m, :].unsqueeze(1).broadcast_to([P, HEADS, P])
                dve.wait_ge(delta_done, n + 1)
                signal(v.tensor_copy(GTN[:, :, :], GT[:, bass.ds(n, 1), :, :].squeeze(1)), "scalars")
                for name, src, sq, row, (mul, add) in (("k0", K0, SQ, 0, (1.0, L2_EPS)),
                                                      ("q0", Q0, SQ2, 1, (float(HD), HD * L2_EPS))):
                    need(name)
                    signal(v.tensor_tensor(sq[:, :, :], src[:, :, :], src[:, :, :], ALU.mult), name + "_sq")
                    need(name + "_sq")
                    signal(v.tensor_reduce(SS[:, 2, :] if row else SS[:, 3, :], sq[:, :, :], AX.X, ALU.add), name + "_ss")
                    need(name + "_ss")
                    ins = v.tensor_scalar(SS[:, row, :], SS[:, 2, :] if row else SS[:, 3, :], mul, add, ALU.mult, ALU.add)
                signal(ins, "norm_arg")
                need("norm_inv")
                signal(v.tensor_tensor(KN[:, :, :], K0[:, :, :], over(RN[:, 0, :]), ALU.mult), "k_unit")
                signal(v.tensor_tensor(QN[:, :, :], Q0[:, :, :], over(RN[:, 1, :]), ALU.mult), "q_unit")
                need("cum_rows")
                need("scalars")
                signal(v.tensor_tensor(DIF[:, :, :], bank(5), over(GTN[:, G_CUM, :]), ALU.subtract), "dif")
                need("dif")
                signal(v.tensor_scalar(E1[:, :, :], DIF[:, :, :], 0.0, None, ALU.max), "dif_pos")
                signal(v.tensor_scalar(E2[:, :, :], DIF[:, :, :], 0.0, None, ALU.min), "dif_neg")
                need("kk")
                need("decay_beta")
                signal(v.tensor_tensor(L[:, :, :], bank(6), E1[:, :, :], ALU.mult), "low")
                need("qk")
                need("decayT_up")
                signal(v.tensor_tensor(ATT[:, :, :], bank(7), E2[:, :, :], ALU.mult), "att")
                for lv in range(LEVELS):
                    dve.wait_ge(sem("lev_m_ps"), n * LEVELS + lv + 1)
                    v.tensor_tensor(MM[:, :, :], bank(2), mask(M_LEV + lv), ALU.mult).then_inc(sem("lev_m"), 1)
                    if lv < LEVELS - 1:
                        dve.wait_ge(sem("lev_p"), n * (LEVELS - 1) + lv + 1)
                        if lv:
                            dve.wait_ge(sem("inv"), n * (LEVELS - 1) + lv)
                        v.tensor_tensor(T[:, :, :], T[:, :, :], bank(3), ALU.subtract).then_inc(sem("inv"), 1)
                    dve.wait_ge(sem("lev_pT"), n * LEVELS + lv + 1)
                    if lv:
                        dve.wait_ge(sem("invT"), n * LEVELS + lv)
                    v.tensor_tensor(TT[:, :, :], TT[:, :, :], bank(4), ALU.subtract).then_inc(sem("invT"), 1)
                need("k_state")
                need("v_beta")
                for h in range(HEADS):
                    ins = v.scalar_tensor_tensor(R[:, h, :], PS[:, 5, h * P:(h + 1) * P], GTN[:, G_NBE, h:h + 1],
                                                 VB[:, h, :], ALU.mult, ALU.add)
                signal(ins, "resid")
                need("kv_outer")
                for h in range(HEADS):
                    ins = v.scalar_tensor_tensor(ST[:, h, :], ST[:, h, :], GTN[:, G_ELAST, h:h + 1],
                                                 PS[:, 1, h * P:(h + 1) * P], ALU.mult, ALU.add)
                signal(ins, "state")
                need("o_intra")
                need("q_state_dec")
                signal(v.tensor_tensor(O[:, :, :], QS[:, :, :], bank(0), ALU.add), "o")
                need("o")
                signal(v.tensor_tensor(SQ[:, :, :], O[:, :, :], O[:, :, :], ALU.mult), "o_sq")
                need("o_sq")
                signal(v.tensor_reduce(SS[:, 2, :], SQ[:, :, :], AX.X, ALU.add), "o_ss")
                need("o_ss")
                signal(v.tensor_scalar(SS[:, 3, :], SS[:, 2, :], 1.0 / HD, RMS_EPS, ALU.mult, ALU.add), "rms_arg")
                need("rms_inv")
                signal(v.tensor_tensor(ON[:, :, :], O[:, :, :], over(RN[:, 2, :]), ALU.mult), "o_unit")
                need("oT_ps")
                dve.wait_ge(sem("z_in"), n * 16 + 16)
                signal(v.scalar_tensor_tensor(OZ[:, :, :], bank(2), DNW[:, 0:1], ZS[:, :, :], ALU.mult, ALU.mult), "oT")

            dve.wait_ge(delta_done, NT + 1)
            for s in range(4):
                for i in range(4):
                    w = 4 * s + i
                    dve.wait_ge(unit_ready, U_MIX + w + 1)
                    dve.wait_ge(gate_in[i % 2], 16 * (w // 2 + 1))
                    dve.wait_ge(h_lo, H_MIX + w + 1)
                    v.tensor_tensor(H32[:, i % 2, :], GATE[:, i % 2, 0, :], PS[:, 2 * (i % 2), :], ALU.mult)
                    v.tensor_tensor(SIG[:, i % 2, :], GATE[:, i % 2, 1, :], PS[:, 2 * (i % 2) + 1, :], ALU.mult)\
                        .then_inc(gated_b, 1)
                    dve.wait_ge(gated_b, w + 3)
                    dve.sem_inc(unit_read, 1)
                residual_add(Q_MIX + 16 * s, Q_MIX)
            dve.wait_ge(tile_read, Q_LN2 + 4)
            layer_norm("ln2")

            for s in range(4):
                for h in range(2):
                    dve.wait_ge(q_hi, 2 * s + h + 1)
                    to = (slice(None), slice(None), slice(h * HALF, (h + 1) * HALF))
                    v.scalar_tensor_tensor(HTl[to], PS[:, 2 * h:2 * h + 2, :], XD ** -0.5, HTh[to].bitcast(F32),
                                           ALU.mult, ALU.subtract).then_inc(q_lo, 1)
                    dve.wait_ge(q_lo, 2 * s + h + 1)
                    dve.sem_inc(unit_read, 1)
                for i in range(NT + 2):
                    if i < NT:
                        dve.wait_ge(s_ready, 8 * s + i + 1)
                        v.tensor_reduce(NEGMAX[:, i:i + 1], PS[:, 4 + i % 2, 0:N_MEM], AX.X, ALU.max, negate=True)\
                            .then_inc(neg_max, 1)
                        dve.wait_ge(s_read, 8 * s + i + 3)
                        v.reciprocal(RINV[:, i:i + 1], RSUM[:, i:i + 1]).then_inc(r_inv, 1)
                        dve.wait_ge(r_inv, 8 * s + i + 1)
                        v.tensor_scalar(PR[:, i % 4, :], PR[:, i % 4, :], RINV[:, i:i + 1], None, ALU.mult)\
                            .then_inc(p_norm, 1)
                    if i >= 2:
                        t = i - 2
                        dve.wait_ge(pt_hi, 8 * s + t + 1)
                        to = (slice(None), slice(None), slice(t % 4 * P, (t % 4 + 1) * P))
                        v.tensor_tensor(PTl[to], PS[:, 6 + t % 2, 0:N_MEM].rearrange("p (m t) -> p m t", m=MT),
                                        PTh[to].bitcast(F32), ALU.subtract).then_inc(pt_lo, 1)
                    if i in (NT // 2 + 1, NT + 1):
                        h = i // (NT + 1)
                        dve.wait_ge(o_hi, 2 * s + h + 1)
                        to = (slice(None), slice(None), slice(h * HALF, (h + 1) * HALF))
                        v.tensor_tensor(HTl[to], PS[:, 2 * h:2 * h + 2, :], HTh[to].bitcast(F32), ALU.subtract)\
                            .then_inc(o_lo, 1)
                        dve.wait_ge(o_lo, 2 * s + h + 1)
                        dve.sem_inc(unit_read, 1)
                dve.sem_inc(kvh_used, 1)
                residual_add(Q_XA + 16 * s, Q_XA)
            dve.wait_ge(tile_read, Q_LN3 + 4)
            layer_norm("ln3")
            dve.wait_ge(x_scaled, 4 * NT)
            ffn(U_FFN2, Q_FFN2, H_FFN2)
            dve.wait_ge(tile_read, Q_FFN2 + 16 * PAIRS + 4)
            layer_norm("ln4")


LN_ORDER_HALF = {"mem": 0, "ln1": 1, "ln2": 3, "ln3": 5, "ln4": 7}

_INS = ["x", "mem", "ffn1_w_gate", "ffn1_w_up", "ffn1_w_down", "ln1_g", "ln1_b", "w_in", "conv_w", "a_log",
        "dt_bias", "dn_norm_w", "w_dn_branch", "pool_w", "pool_scale", "w_pool_branch", "w_mix_out", "ln2_g",
        "ln2_b", "mem_ln_g", "mem_ln_b", "xa_wq", "xa_wk", "xa_wv", "xa_wo", "ln3_g", "ln3_b",
        "ffn2_w_gate", "ffn2_w_up", "ffn2_w_down", "ln4_g", "ln4_b"]


def kernel(**inputs):
    import concourse.bacc as bacc
    from concourse.bass_utils import run_bass_kernel_spmd

    nc = bacc.Bacc("TRN2", target_bir_lowering=False, num_devices=1)
    arrays, args = {}, {}
    given = {name: np.ascontiguousarray(inputs[name]) for name in _INS}
    given["conv_w"] = np.ascontiguousarray(given["conv_w"][0].reshape(CONV_K, CH_Z, P).transpose(2, 1, 0))
    given["pool_scale"] = np.ascontiguousarray(given["pool_scale"].reshape(GROUPS, P).T)
    given["dn_norm_w"] = given["dn_norm_w"].reshape(P, 1)
    given["masks"] = host_masks()
    given["counts"] = host_counts()
    for name, v in given.items():
        arrays[f"in_{name}"] = v
        args[name] = nc.dram_tensor(f"in_{name}", v.shape, F32, kind="ExternalInput").ap()
    args["out"] = nc.dram_tensor("out_x", (1, SEQ, D), F32, kind="ExternalOutput").ap()
    build(nc, args)
    r = run_bass_kernel_spmd(nc, [arrays], core_ids=[0])
    return r.results[0]["out_x"]
```

```python
from contextlib import ExitStack

import numpy as np
import concourse.bass as bass
from concourse import mybir

P = 128
SEQ = 1024
D = 1024
KD = D // P
NT = SEQ // P
HALF = 512
D_FF = 2816
PAIRS = D_FF // (2 * P)
N_MEM = 256
MT = N_MEM // P
HEADS = 4
HD = 128
XD = 256
QKV = 3 * HEADS * HD
CONV_K = 4
GROUPS = 4
HALO = 16
LN_EPS = 1e-5
RMS_EPS = 1e-6
L2_EPS = 1e-6
ALPHA = 2.0 ** 0.25
LEVELS = 6

COL_Z = QKV
COL_AB = COL_Z + HEADS * HD
COL_P = COL_AB + 2 * HEADS
COL_GDN = COL_P + GROUPS * P
COL_GPOOL = COL_GDN + D

CH_Z = QKV // P
CH_GDN = CH_Z + HEADS
CH_GPOOL = CH_GDN + KD
CHUNKS = CH_GPOOL + KD

F32 = mybir.dt.float32
F32R = mybir.dt.float32r
ALU = mybir.AluOpType
ACT = mybir.ActivationFunctionType
AX = mybir.AxisListType

S_KV, S_FFN1 = 0, 8
S_P = S_FFN1 + 2 * PAIRS
S_QKV = S_P + 2
S_Z = S_QKV + 6
S_GATE = S_Z + 2
S_MIX = S_GATE + NT
S_XA = S_MIX + 4
S_FFN2 = S_XA + 4
S_END = S_FFN2 + 2 * PAIRS

U_KV, U_FFN1 = 0, 8
U_P = U_FFN1 + 4 * PAIRS
U_QKV = U_P + 4
U_Z = U_QKV + 12
U_MIX = U_Z + 4
U_XA = U_MIX + 16
U_FFN2 = U_XA + 16
U_END = U_FFN2 + 4 * PAIRS

Q_MEM, Q_X = 0, 2 * MT
Q_FFN1 = Q_X + 2 * NT
Q_LN1 = Q_FFN1 + 16 * PAIRS
Q_AB = Q_LN1 + 2 * NT
Q_POOL = Q_AB + 1
Q_MIX = Q_POOL + 2 * GROUPS
Q_LN2 = Q_MIX + 16 * 4
Q_XA = Q_LN2 + 2 * NT
Q_LN3 = Q_XA + 16 * 4
Q_FFN2 = Q_LN3 + 2 * NT

D_FFN1, D_MIX = 0, PAIRS
D_XA = D_MIX + 4
D_FFN2 = D_XA + 4

H_FFN1, H_MIX = 0, 4 * PAIRS
H_FFN2 = H_MIX + 16

M_ID, M_UP, M_ONE, M_LOW, M_NEG1, M_LEV = 0, 1, 2, 3, 4, 5
N_MASKS = M_LEV + LEVELS


def host_masks():
    i = np.arange(P)[:, None]
    j = np.arange(P)[None, :]
    m = np.zeros((P, N_MASKS, P), np.float32)
    m[:, M_ID] = i == j
    m[:, M_UP] = i <= j
    m[:, M_ONE] = 1.0
    m[:, M_LOW] = i > j

    def level(b):
        return (i // (2 * b) == j // (2 * b)) & (i // b % 2 == 1) & (j // b % 2 == 0)

    m[:, M_NEG1] = -1.0 * level(1)
    for n in range(LEVELS):
        m[:, M_LEV + n] = level(2 << n)
    return m


def host_counts():
    c = np.zeros((P, 32), np.float32)
    c[:, 0:HALO] = 1.0 / (np.arange(HALO) + 1.0)
    c[:, HALO:] = -0.5
    return c


def build(nc, a):
    with ExitStack() as ctx:
        base = 16512
        place = {}

        def at(name, shape, dtype, where=None, offset=0):
            nonlocal base
            size = int(np.prod(shape[1:])) * 4
            if where is None:
                address = base
                base += (size + 31) // 32 * 32
            else:
                address = place[where] + offset
            place[name] = address
            return nc.alloc_sbuf_tensor_at(name, shape, dtype, offset=address)

        X = at("X", [P, NT, D], F32)
        XTh = at("XTh", [P, KD, SEQ], F32R)
        XTl = at("XTl", [P, KD, SEQ], F32R)
        GUraw = at("GUraw", [P, KD, 256], F32)
        GUh = at("GUh", [P, 2, KD, 256], F32R)
        GUl = at("GUl", [P, 2, KD, 256], F32R)
        DWraw = at("DWraw", [P, 2, D], F32)
        DWh = at("DWh", [P, 2, D], F32R)
        DWl = at("DWl", [P, 2, D], F32R)
        HTh = at("HTh", [P, 2, SEQ], F32R)
        HTl = at("HTl", [P, 2, SEQ], F32R)
        SIG = at("SIG", [P, 2, HALF], F32)
        H32 = at("H32", [P, 2, HALF], F32)
        PTh = at("PTh", [P, 2, HALF], F32R)
        PTl = at("PTl", [P, 2, HALF], F32R)
        LNG = at("LNG", [P, D], F32)
        LNB = at("LNB", [P, D], F32)
        MASK = at("MASK", [P, N_MASKS, P], F32)
        COUNT = at("COUNT", [P, 32], F32)
        BNS = at("BNS", [P, 2, 6], F32)
        MV = at("MV", [P, NT, 2], F32)
        VE = at("VE", [P, NT], F32)
        RSTD = at("RSTD", [P, NT], F32)
        NMR = at("NMR", [P, NT], F32)
        CONVW = at("CONVW", [P, CH_Z, CONV_K], F32)
        PSCALE = at("PSCALE", [P, GROUPS], F32)
        DNW = at("DNW", [P, 1], F32)
        HPAR = at("HPAR", [P, 2, HEADS], F32)
        G_G, G_CUM, G_ECUM, G_ETAIL, G_ELAST, G_BETA, G_NBE = range(7)
        GT = at("GT", [P, NT, 7, HEADS], F32)
        GTN = [at("GTN0", [P, 7, HEADS], F32), at("GTN1", [P, 7, HEADS], F32)]
        SS = at("SS", [P, 4, HEADS], F32)
        SSO = at("SSO", [P, 2, HEADS], F32)
        RN = at("RN", [P, 2, HEADS], F32)
        RNO = at("RNO", [P, HEADS], F32)
        assert base <= 229368, base

        KV = at("KV", [P, 2, 2, 2, XD], F32R, "LNG")
        PR = at("PR", [P, 4, N_MEM], F32, "SIG")
        NEGMAX = at("NEGMAX", [P, 8], F32, "H32")
        RSUM = at("RSUM", [P, 8], F32, "H32", 32)
        RINV = at("RINV", [P, 8], F32, "H32", 64)
        KVO = at("KVO", [P, 2, 2, 2 * N_MEM], F32R, "DWh")
        FRAMES = 2 * (HALO + SEQ) * 4
        RAWP = at("RAWP", [P, 2, HALO + SEQ], F32, "DWraw")
        RAW = at("RAW", [P, 2, HALO + SEQ], F32, "DWraw", FRAMES)
        POOLW = at("POOLW", [P, GROUPS, P], F32, "DWraw", 2 * FRAMES)
        CACC = at("CACC", [P, 2, 2, HALF], F32, "HTh")
        WSUM = [at("WSUM0", [P, HALO + SEQ], F32, "DWraw", 2 * FRAMES + GROUPS * P * 4),
                at("WSUM1", [P, HALO + SEQ], F32, "HTl")]
        COUT = at("COUT", [P, 2, 2, HALF], F32, "SIG")
        MIXED = at("MIXED", [P, GROUPS, SEQ], F32, "PTh")
        ABRAW = at("ABRAW", [P, KD, 8], F32, "PTh")
        ABh = at("ABh", [P, KD, 8], F32R, "PTh", 256)
        ABl = at("ABl", [P, KD, 8], F32R, "PTh", 512)
        ABT = at("ABT", [P, NT, 8], F32, "PTh", 768)
        AB1 = at("AB1", [P, NT, HEADS], F32, "PTh", 1024)
        AB2 = at("AB2", [P, NT, HEADS], F32, "PTh", 1152)
        AB3 = at("AB3", [P, NT, HEADS], F32, "PTh", 1280)
        AB4 = at("AB4", [P, HEADS], F32, "PTh", 1408)
        GATE = at("GATE", [P, 2, 2, HALF], F32, "PTh")
        FEAT = at("FEAT", [P, KD, SEQ], F32, "X")
        GOUT = at("GOUT", [P, 4, HALF], F32, "SIG")
        spots = [place["DWraw"] + i * 2048 for i in range(20)] + [place["PTh"] + i * 2048 for i in range(8)]

        def delta(name, spot, count=1):
            place[name] = spots[spot]
            return nc.alloc_sbuf_tensor_at(name, [P, HEADS * count, P], F32, offset=spots[spot])

        QKVS = delta("QKVS", 0, 3)
        KN, QN, DIF = delta("KN", 0), delta("QN", 1), delta("DIF", 2)
        K0, Q0, V0 = delta("K0", 3), delta("Q0", 4), delta("V0", 5)
        L, LT, T = delta("L", 3), delta("LT", 4), delta("T", 5)
        SQ, SQ2 = delta("SQ", 6), delta("SQ2", 7)
        E1, E2 = delta("E1", 6), delta("E2", 7)
        MM = [delta("MM0", 8), delta("MM1", 9)]
        two = lambda name, spot: [delta(name + str(i), spot + i) for i in range(2)]
        KT, QT, KDEC, VB, TT = two("KT", 10), two("QT", 12), two("KDEC", 14), two("VB", 16), two("TT", 18)
        ATT = two("ATT", 20)
        R, VN, QS, O, ST, ZS = (delta(x, 22 + i) for i, x in enumerate(("R", "VN", "QS", "O", "ST", "ZS")))
        OSQ, ON = R, QS

        PS = ctx.enter_context(nc.psum_tensor("PS", [P, 8, 512], F32))
        ident = MASK[:, M_ID, :]

        proj_scratch = nc.dram_tensor("proj_scratch", [CHUNKS, P, SEQ], F32, kind="Internal").ap()
        kv_scratch = nc.dram_tensor("kv_scratch", [HEADS, P, 2, 2, 2 * N_MEM], F32, kind="Internal").ap()
        proj_v = proj_scratch.rearrange("c p t -> p c t")
        gate_v = proj_scratch[CH_GDN:CHUNKS].rearrange("(g c) p t -> p g c t", g=2)
        x_scratch = nc.dram_tensor("x_scratch", [P, NT, D], F32, kind="Internal").ap()
        rows = lambda w: w.rearrange("o (k p) n -> p (o k) n", p=P)
        col = lambda v: v.rearrange("o n -> (o n)")
        w_in = rows(a["w_in"])
        x_v = a["x"].rearrange("b (t p) d -> p (b t) d", p=P)
        out_v = a["out"].rearrange("b (t p) d -> p (b t) d", p=P)
        mem_v = a["mem"].rearrange("b (t p) d -> p (b t) d", p=P)

        sems = {}

        def sem(name):
            if name not in sems:
                sems[name] = ctx.enter_context(nc.semaphore(name))
            return sems[name]

        gu_in, gu_hi, gu_lo = sem("gu_in"), sem("gu_hi"), sem("gu_lo")
        dw_in, dw_hi, dw_lo = sem("dw_in"), sem("dw_hi"), sem("dw_lo")
        unit_ready, unit_read = sem("unit_ready"), sem("unit_read")
        tile_ready, tile_read = sem("tile_ready"), sem("tile_read")
        act_out, h_hi, h_lo = sem("act_out"), sem("h_hi"), sem("h_lo")
        const_in, x_in, mem_in = sem("const_in"), sem("x_in"), sem("mem_in")
        ln_par_in, ln_par_used = sem("ln_par_in"), sem("ln_par_used")
        ln_var, ln_rstd, ln_nmr, ln_hat = sem("ln_var"), sem("ln_rstd"), sem("ln_nmr"), sem("ln_hat")
        ln_scaled, ln_done, bn_step = sem("ln_scaled"), sem("ln_done"), sem("bn_step")
        xt_hi, xt_lo, x_scaled = sem("xt_hi"), sem("xt_lo"), sem("x_scaled")
        kv_hi, kv_lo = sem("kv_hi"), sem("kv_lo")
        kv_stored = [sem("kv_stored0"), sem("kv_stored1")]
        small_step = sem("small_step")
        ab_in, ab_split, ab_done = sem("ab_in"), sem("ab_split"), sem("ab_done")
        tap, conv_done = sem("tap"), sem("conv_done")
        cout_done = sem("cout_done")
        stored = [sem("stored0"), sem("stored1")]
        pooled, pool_w_in = sem("pooled"), sem("pool_w_in")
        gate_in = [sem("gate_in0"), sem("gate_in1")]
        gated_b = sem("gated_b")
        kvh_in, kvh_used = sem("kvh_in"), sem("kvh_used")
        q_hi, q_lo, o_hi, o_lo = sem("q_hi"), sem("q_lo"), sem("o_hi"), sem("o_lo")
        s_ready, s_read, neg_max = sem("s_ready"), sem("s_read"), sem("neg_max")
        r_inv, p_norm = sem("r_inv"), sem("p_norm")
        pt_ready, pt_hi, pt_lo = sem("pt_ready"), sem("pt_hi"), sem("pt_lo")
        out_stored = sem("out_stored")
        x_spilled, x_back = sem("x_spilled"), sem("x_back")
        gp_ready, gp_read, gate_out = sem("gp_ready"), sem("gp_read"), sem("gate_out")
        gate_stored = [sem(f"gate_stored{i}") for i in range(4)]
        feat_hi, feat_lo, scan_lo = sem("feat_hi"), sem("feat_lo"), sem("scan_lo")

        LN_ORDER = {"mem": 0, "ln1": 1, "ln2": 2, "ln3": 3, "ln4": 4}
        LN_TILES = {"mem": MT, "ln1": NT, "ln2": NT, "ln3": NT, "ln4": NT}
        LN_BASE = {"mem": 0, "ln1": MT, "ln2": MT + NT, "ln3": MT + 2 * NT, "ln4": MT + 3 * NT}
        XT_BASE = {"mem": 0, "x": 2 * MT, "ln1": 2 * MT + 2 * NT, "ln2": 2 * MT + 4 * NT, "ln3": 2 * MT + 6 * NT}
        Q_BASE = {"mem": Q_MEM, "x": Q_X, "ln1": Q_LN1, "ln2": Q_LN2, "ln3": Q_LN3}

        block = ctx.enter_context(nc.Block())

        @block.sync
        def _(sp):
            def load_gu(n, src_a, src_b):
                sp.wait_ge(gu_lo, n + 1)
                for dst, src in (src_a, src_b):
                    sp.dma_start(dst, src).then_inc(gu_in, 16)

            def load_cols(n, w, c):
                load_gu(n, (GUraw[:, 0:4, :], w[:, 0:4, bass.ds(c, 256)]),
                        (GUraw[:, 4:8, :], w[:, 4:8, bass.ds(c, 256)]))

            def load_gate_up(n, wg, wu, c):
                load_gu(n, (GUraw[:, :, 0:P], wg[:, :, bass.ds(c, P)]),
                        (GUraw[:, :, P:256], wu[:, :, bass.ds(c, P)]))

            def load_dw(m, w, row):
                sp.wait_ge(dw_lo, m + 1)
                for c in range(2):
                    sp.dma_start(DWraw[:, c, :], w[bass.ds(row + c * P, P), :]).then_inc(dw_in, 16)

            def load_ln(name, g, b):
                k = LN_ORDER[name]
                if k:
                    sp.wait_ge(ln_par_used, k)
                for dst, src in ((LNG, g), (LNB, b)):
                    sp.dma_start(dst[:, :], src.broadcast_to([P, D])).then_inc(ln_par_in, 16)

            def ffn_loads(s0, d0, wg, wu, wd, next_slots):
                with sp.Fori(0, PAIRS - 1) as j:
                    load_dw(d0 + j, wd, j * 256)
                    for c in range(2):
                        load_gate_up(s0 + 2 + 2 * j + c, wg, wu, j * 256 + 256 + c * P)
                load_dw(d0 + PAIRS - 1, wd, (PAIRS - 1) * 256)
                for f in next_slots:
                    f()

            sp.dma_start(X[:, 0:MT, :], mem_v).then_inc(mem_in, 16)
            load_ln("mem", a["mem_ln_g"], a["mem_ln_b"])
            sp.dma_start(MASK[:, :, :], a["masks"]).then_inc(const_in, 16)
            sp.dma_start(COUNT[:, :], a["counts"]).then_inc(const_in, 16)
            sp.dma_start(CONVW[:, :, :], a["conv_w"]).then_inc(const_in, 16)
            sp.dma_start(PSCALE[:, :], a["pool_scale"]).then_inc(const_in, 16)
            sp.dma_start(DNW[:, :], a["dn_norm_w"]).then_inc(const_in, 16)
            sp.dma_start(HPAR[:, 0, :], a["dt_bias"].broadcast_to([P, HEADS])).then_inc(const_in, 16)
            sp.dma_start(HPAR[:, 1, :], a["a_log"].broadcast_to([P, HEADS])).then_inc(const_in, 16)
            wk, wv = rows(a["xa_wk"]), rows(a["xa_wv"])
            for n in range(4):
                load_cols(n, wk, n * 256)
            for n in range(4):
                load_cols(4 + n, wv, n * 256)
            sp.wait_ge(xt_lo, 2 * MT)
            sp.dma_start(X[:, :, :], x_v).then_inc(x_in, 16)
            wg, wu = rows(a["ffn1_w_gate"]), rows(a["ffn1_w_up"])
            for c in range(2):
                load_gate_up(S_FFN1 + c, wg, wu, c * P)
            load_ln("ln1", a["ln1_g"], a["ln1_b"])
            ffn_loads(S_FFN1, D_FFN1, wg, wu, a["ffn1_w_down"][0],
                      [lambda c=c: load_cols(S_P + c, w_in, COL_P + c * 256) for c in range(2)])
            sp.wait_ge(ln_par_used, 2)
            sp.dma_start(ABRAW[:, :, :], w_in[:, :, COL_AB:COL_AB + 8]).then_inc(ab_in, 16)
            sp.dma_start(POOLW[:, :, :], a["pool_w"].rearrange("o g c e -> c (o g) e")).then_inc(pool_w_in, 16)
            sp.wait_ge(x_scaled, 2 * NT)
            sp.dma_start(x_scratch, X[:, :, :]).then_inc(x_spilled, 16)
            with sp.Fori(0, 8) as j:
                load_cols(S_QKV + j, w_in, j * 256)
            for c in range(2):
                load_cols(S_GATE + c, w_in, COL_GDN + c * 256)
            wdn, wpo = rows(a["w_dn_branch"]), rows(a["w_pool_branch"])

            def load_branch(n, c):
                load_gu(n, (GUraw[:, 0:4, :], wdn[:, :, bass.ds(c, 256)]),
                        (GUraw[:, 4:8, :], wpo[:, :, bass.ds(c, 256)]))

            def load_qkv_tile(m):
                sp.dma_start(QKVS[:, :, :], proj_v[:, 0:CH_Z, bass.ds(m * P, P)]).then_inc(sem("qkv_in"), 16)

            def next_qkv_tile(m):
                for name in ("k_dec", "qT_ps", "dif_neg"):
                    sp.wait_ge(sem(name), m)
                load_qkv_tile(m)

            def load_z_tile(n):
                sp.dma_start(ZS[:, :, :], proj_v[:, CH_Z:CH_GDN, bass.ds(n * P, P)]).then_inc(sem("z_in"), 16)

            sp.wait_ge(tile_read, Q_MIX + 4)
            sp.wait_ge(conv_done, 12 + 1)
            for b in range(2):
                sp.wait_ge(stored[b], 16 * 7)
            load_qkv_tile(0)
            for b in range(2):
                sp.wait_ge(stored[b], 16 * 9)
            load_z_tile(0)
            with sp.Fori(0, NT - 2) as n:
                load_cols(S_GATE + 2 + n, w_in, n * 256 + COL_GDN + 512)
                next_qkv_tile(n + 1)
                sp.wait_ge(sem("oT"), n + 1)
                load_z_tile(n + 1)
            load_branch(S_MIX, 0)
            next_qkv_tile(NT - 1)
            sp.wait_ge(sem("oT"), NT - 1)
            load_z_tile(NT - 1)
            load_branch(S_MIX + 1, 256)
            sp.wait_ge(feat_lo, 4)
            sp.wait_ge(scan_lo, 4)
            sp.wait_ge(x_spilled, 16)
            sp.dma_start(X[:, :, :], x_scratch).then_inc(x_back, 16)
            for i in range(4):
                sp.wait_ge(gate_stored[i], 16 * (NT + 1))
            wmo = a["w_mix_out"][0]

            def load_gate(j, s, c, h):
                u = 4 * s + 2 * c + h
                sp.wait_ge(gated_b, j * 8 + u + 1)
                sp.dma_start(GATE[:, u % 2, :, :], gate_v[:, :, j * 4 + 2 * s + c, h * HALF:(h + 1) * HALF])\
                    .then_inc(gate_in[u % 2], 16)

            for j in range(2):
                for s in range(2):
                    load_dw(D_MIX + 2 * j + s, wmo, (2 * j + s) * 256)
                    for c in range(2):
                        for h in range(2):
                            load_gate(j, s, c, h)
                    if j == 0:
                        load_branch(S_MIX + 2 + s, (2 + s) * 256)
                    else:
                        load_cols(S_XA + s, rows(a["xa_wq"]), s * 256)
            load_ln("ln2", a["ln2_g"], a["ln2_b"])
            sp.wait_ge(ln_par_used, 3)
            wo = a["xa_wo"][0]
            wg, wu = rows(a["ffn2_w_gate"]), rows(a["ffn2_w_up"])
            for s in range(4):
                sp.wait_ge(kvh_used, s + 1)
                for b in range(2):
                    sp.wait_ge(kv_stored[b], 16 * 5)
                sp.dma_start(KV[:, :, :, :, :].bitcast(F32), kv_scratch[s].rearrange("p v h (c n) -> p v h c n", c=2))\
                    .then_inc(kvh_in, 16)
                load_dw(D_XA + s, wo, s * 256)
                if s < 2:
                    load_cols(S_XA + 2 + s, rows(a["xa_wq"]), (2 + s) * 256)
                else:
                    load_gate_up(S_FFN2 + s - 2, wg, wu, (s - 2) * P)
            sp.wait_ge(kvh_used, 5)
            load_ln("ln3", a["ln3_g"], a["ln3_b"])
            ffn_loads(S_FFN2, D_FFN2, wg, wu, a["ffn2_w_down"][0], [])
            load_ln("ln4", a["ln4_g"], a["ln4_b"])
            for t in range(NT):
                sp.wait_ge(ln_done, LN_BASE["ln4"] + t + 1)
                sp.dma_start(out_v[:, t, :], X[:, t, :]).then_inc(out_stored, 16)
            sp.wait_ge(out_stored, 16 * NT)

        @block.tensor
        def _(pe):
            mm = nc.tensor.matmul

            def split_product(out, terms):
                for i, (lh, ll, rh, rl) in enumerate(terms):
                    mm(out, lh, rh, start=(i == 0), stop=False)
                    mm(out, lh, rl, start=False, stop=False)
                    last = mm(out, ll, rh, start=False, stop=(i == len(terms) - 1))
                return last

            def unit(u, par, products):
                pe.wait_ge(unit_read, u + 1)
                for m, (terms, width) in enumerate(products):
                    last = split_product(PS[:, 2 * par + m, 0:width], terms)
                last.then_inc(unit_ready, 1)

            def feature_terms(s, m, h, ks=range(KD)):
                t = slice(h * HALF, (h + 1) * HALF)
                c = slice(m * P, (m + 1) * P)
                return [(GUh[:, s, k, c], GUl[:, s, k, c], XTh[:, k, t], XTl[:, k, t]) for k in ks]

            def slot_ready(n):
                pe.wait_ge(gu_lo, n + 2)

            def down(m, q0, qp, ready):
                pe.wait_ge(dw_lo, m + 2)
                i = 0
                for h in range(2):
                    ready(h)
                    for t in range(4 * h, 4 * h + 4):
                        for n in range(2):
                            pe.wait_ge(tile_read, q0 + i + 1)
                            tok, cs = slice(t * P, (t + 1) * P), slice(n * 512, (n + 1) * 512)
                            split_product(PS[:, 4 + (qp + i) % 4, :],
                                          [(HTh[:, c, tok], HTl[:, c, tok], DWh[:, c, cs], DWl[:, c, cs])
                                           for c in range(2)]).then_inc(tile_ready, 1)
                            i += 1

            def transposes(q0, t, chunks=KD):
                for g in range(2):
                    q = q0 + 2 * t + g
                    pe.wait_ge(tile_read, q + 1)
                    for k in range(4):
                        c = 4 * g + k
                        last = nc.tensor.transpose(PS[:, 4 + q % 4, k * P:(k + 1) * P],
                                                   X[:, t, c * P:(c + 1) * P], ident)
                    last.then_inc(tile_ready, 1)

            def ffn(s0, u0, d0, q0, h0):
                with pe.Fori(0, PAIRS) as j:
                    for c in range(2):
                        slot_ready(s0 + 2 * j + c)
                        for h in range(2):
                            i = 2 * c + h
                            unit(u0 + 4 * j + i, i % 2,
                                 [(feature_terms(c, m, h), HALF) for m in range(2)])
                    down(d0 + j, q0 + 16 * j, q0,
                         lambda h: pe.wait_ge(h_lo, h0 + 4 * j + 3 + h + 2))

            pe.wait_ge(const_in, 16 * 7)
            for t in range(MT):
                pe.wait_ge(ln_done, LN_BASE["mem"] + t + 1)
                transposes(Q_MEM, t)
            pe.wait_ge(xt_lo, XT_BASE["mem"] + 2 * MT)
            for s in range(4):
                slot_ready(s)
                unit(s, s % 2, [([(GUh[:, s % 2, k, m * P:(m + 1) * P], GUl[:, s % 2, k, m * P:(m + 1) * P],
                                   XTh[:, k, 0:N_MEM], XTl[:, k, 0:N_MEM]) for k in range(KD)], N_MEM)
                                for m in range(2)])
            for s in range(4):
                slot_ready(4 + s)
                unit(4 + s, s % 2, [([(XTh[:, k, m * P:(m + 1) * P], XTl[:, k, m * P:(m + 1) * P],
                                       GUh[:, s % 2, k, :], GUl[:, s % 2, k, :]) for k in range(KD)], XD)
                                    for m in range(2)])
            pe.wait_ge(x_in, 16)
            for t in range(NT):
                transposes(Q_X, t)
            pe.wait_ge(xt_lo, XT_BASE["x"] + 2 * NT)
            ffn(S_FFN1, U_FFN1, D_FFN1, Q_FFN1, H_FFN1)
            for t in range(NT):
                pe.wait_ge(ln_done, LN_BASE["ln1"] + t + 1)
                transposes(Q_LN1, t)
            pe.wait_ge(xt_lo, XT_BASE["ln1"] + 2 * NT)

            pe.wait_ge(ab_split, 2)
            pe.wait_ge(tile_read, Q_AB + 1)
            for t in range(NT):
                tok = slice(t * P, (t + 1) * P)
                last = split_product(PS[:, 4 + Q_AB % 4, 8 * t:8 * t + 8],
                                     [(XTh[:, k, tok], XTl[:, k, tok], ABh[:, k, :], ABl[:, k, :])
                                      for k in range(KD)])
            last.then_inc(tile_ready, 1)
            pe.wait_ge(ab_done, 1)
            g = GT[:, :, G_G, :]
            mm(PS[:, 4, 0:NT * HEADS], MASK[:, M_UP, :], g, start=True, stop=True)
            mm(PS[:, 5, 0:NT * HEADS], MASK[:, M_ONE, :], g, start=True, stop=True).then_inc(sem("cum_ready"), 1)

            def project(n, first_u, count):
                with pe.Fori(0, count) as j:
                    for s in range(2):
                        slot_ready(n + 2 * j + s)
                        for h in range(2):
                            unit(first_u + 4 * j + 2 * s + h, h, [(feature_terms(s, m, h), HALF) for m in range(2)])

            pe.wait_ge(sem("cum_read"), 1)
            project(S_P, U_P, 1)
            project(S_QKV, U_QKV, 3)

            pe.wait_ge(pool_w_in, 16)
            for g in range(GROUPS):
                pe.wait_ge(pooled, g + 1)
                for h in range(2):
                    q = Q_POOL + 2 * g + h
                    pe.wait_ge(tile_read, q + 1)
                    mm(PS[:, 4 + q % 4, :], POOLW[:, g, :], MIXED[:, g, h * HALF:(h + 1) * HALF],
                       start=True, stop=True).then_inc(tile_ready, 1)
            project(S_Z, U_Z, 1)

            def flip(bank, src, name):
                for h in range(HEADS):
                    last = nc.tensor.transpose(PS[:, bank, h * P:(h + 1) * P], src(h), ident)
                last.then_inc(sem(name), 1)

            def product(bank, lhsT, rhs, name):
                for h in range(HEADS):
                    last = mm(PS[:, bank, h * P:(h + 1) * P], lhsT(h), rhs(h), start=True, stop=True)
                last.then_inc(sem(name), 1)

            of = lambda t: (lambda h: t[:, h, :])

            def delta_step(n, m, par, scan, prep):
                new = 1 - par
                done = [0]

                def fill(count):
                    if not prep:
                        return
                    if done[0] == 0:
                        slot_ready(S_GATE + m)
                    for i in range(done[0], done[0] + count):
                        g, k3 = i // 24, i % 24
                        k, part = k3 // 3, k3 % 3
                        if k3 == 0:
                            pe.wait_ge(gp_read, m * 4 + g + 1)
                        c = slice(g // 2 * P, (g // 2 + 1) * P)
                        t = slice(g % 2 * HALF, (g % 2 + 1) * HALF)
                        w = (GUh, GUh, GUl)[part][:, new, k, c]
                        x = (XTh, XTl, XTh)[part][:, k, t]
                        ins = mm(PS[:, g % 2, :], w, x, start=(k3 == 0), stop=(k3 == 23))
                        if k3 == 23:
                            ins.then_inc(gp_ready, 1)
                    done[0] += count

                def of_scan(name):
                    pe.wait_ge(sem(name), n + 1)

                def of_prep(name):
                    pe.wait_ge(sem(name), m + 1)

                if prep:
                    pe.wait_ge(sem("qkv_in"), m * 16 + 16)
                    flip(2, lambda h: QKVS[:, HEADS + h, :], "k_tok")
                    flip(3, lambda h: QKVS[:, h, :], "q_tok")
                    flip(4, lambda h: QKVS[:, 2 * HEADS + h, :], "v_tok")
                    of_prep("scalars")
                    product(5, lambda h: GTN[new][:, G_G, h:h + 1].broadcast_to([P, P]),
                            lambda h: MASK[:, M_UP, :], "cum_rows")
                if scan:
                    pe.wait_ge(sem("state"), n + 1)
                    product(6, of(KT[par]), of(ST), "k_state")
                    product(7, of(QT[par]), of(ST), "q_state")
                fill(12)
                if scan:
                    of_scan("resid")
                    product(6, of(TT[par]), of(R), "v_new_ps")
                fill(12)
                if scan:
                    of_scan("v_new")
                    product(6, of(KDEC[par]), of(VN), "kv_outer")
                    of_scan("q_state_dec")
                    product(7, of(ATT[par]), of(VN), "o_intra")
                if prep:
                    of_prep("k_unit")
                    flip(2, of(KN), "kT_ps")
                    of_prep("q_unit")
                    flip(3, of(QN), "qT_ps")
                fill(8)
                if prep:
                    of_prep("kT")
                    of_prep("v0")
                    product(4, of(KT[new]), of(KT[new]), "kk")
                    of_prep("qT")
                    of_prep("dif")
                    product(5, of(KT[new]), of(QT[new]), "qk")
                fill(8)
                if prep:
                    of_prep("low")
                    flip(2, of(L), "lowT_ps")
                    of_prep("inv0")
                    flip(3, of(T), "inv0T_ps")
                if scan:
                    of_scan("o_unit")
                    flip(7, of(ON), "oT_ps")
                fill(8)
                if prep:
                    of_prep("lowT")
                    of_prep("att")
                    for lv in range(LEVELS):
                        b = 2 << lv
                        even = lambda t: t.rearrange("p (c two b) -> p c two b", two=2, b=b)[:, :, 0, :]
                        odd = lambda t: t.rearrange("p (c two b) -> p c two b", two=2, b=b)[:, :, 1, :]
                        if lv:
                            pe.wait_ge(sem("inv"), m * (LEVELS - 1) + lv)
                        for h in range(HEADS):
                            last = mm(PS[:, 4, h * 64:(h + 1) * 64], LT[:, h, :], even(T[:, h, :]),
                                      start=True, stop=True)
                        last.then_inc(sem("lev_m_ps"), 1)
                        fill(3)
                        pe.wait_ge(sem("lev_m"), m * LEVELS + lv + 1)
                        if lv == 0:
                            of_prep("inv0T")
                        for h in range(HEADS):
                            last = mm(PS[:, 5, h * 64:(h + 1) * 64], MM[lv % 2][:, h, :],
                                      odd(TT[new][:, h, :]), start=True, stop=True)
                        last.then_inc(sem("lev_pT"), 1)
                        fill(3)
                        pe.wait_ge(sem("invT"), m * LEVELS + lv + 1)
                        if lv < LEVELS - 1:
                            flip(2, of(TT[new]), "inv_ps")
                            fill(2)
                    fill(96 - done[0])

            pe.wait_ge(unit_read, U_MIX + 2)
            pe.wait_ge(tile_read, Q_MIX + 4)
            delta_step(None, 0, 1, False, True)
            with pe.Fori(0, 3) as j:
                for r in range(2):
                    delta_step(2 * j + r, 2 * j + r + 1, r, True, True)
            delta_step(NT - 2, NT - 1, 0, True, True)
            delta_step(NT - 1, None, 1, True, False)

            pe.wait_ge(gp_read, 4 * NT + 2)
            pe.wait_ge(sem("oT"), NT)
            for s in range(4):
                slot_ready(S_MIX + s)
                for c in range(2):
                    for h in range(2):
                        i = 2 * c + h
                        pe.wait_ge(unit_read, U_MIX + 4 * s + i + 1)
                        if s == 0 and c == 0:
                            pe.wait_ge(feat_lo, 4)
                        split_product(PS[:, 2 * h + 1, :], feature_terms(s % 2, c, h, range(4, 8)))
                        if s == 0 and c == 0:
                            pe.wait_ge(scan_lo, 2 * h + 2)
                        split_product(PS[:, 2 * h, :], feature_terms(s % 2, c, h, range(0, 4)))\
                            .then_inc(unit_ready, 1)
                down(D_MIX + s, Q_MIX + 16 * s, Q_MIX,
                     lambda h: pe.wait_ge(h_lo, H_MIX + 4 * s + 3 + h + 2))
            for t in range(NT):
                pe.wait_ge(ln_done, LN_BASE["ln2"] + t + 1)
                transposes(Q_LN2, t)
            pe.wait_ge(xt_lo, XT_BASE["ln2"] + 2 * NT)

            for s in range(4):
                slot_ready(S_XA + s)
                for h in range(2):
                    unit(U_XA + 4 * s + h, h, [(feature_terms(s % 2, m, h), HALF) for m in range(2)])
                pe.wait_ge(kvh_in, 16 * (s + 1))
                pe.wait_ge(tile_read, Q_XA + 16 * s + 4)
                for i in range(NT + 2):
                    if i < NT:
                        if i % 4 == 0:
                            pe.wait_ge(q_lo, 2 * s + i // 4 + 1)
                        pe.wait_ge(s_read, 8 * s + i + 1)
                        tok = slice(i * P, (i + 1) * P)
                        split_product(PS[:, 4 + i % 2, 0:N_MEM],
                                      [(HTh[:, c, tok], HTl[:, c, tok], KV[:, 0, 0, c, :], KV[:, 0, 1, c, :])
                                       for c in range(2)]).then_inc(s_ready, 1)
                    if i >= 2:
                        t = i - 2
                        pe.wait_ge(p_norm, 8 * s + t + 1)
                        pe.wait_ge(pt_lo, 8 * s + t + 1)
                        for m in range(MT):
                            last = nc.tensor.transpose(PS[:, 6 + t % 2, m * P:(m + 1) * P],
                                                       PR[:, t % 4, m * P:(m + 1) * P], ident)
                        last.then_inc(pt_ready, 1)
                    if i in (NT // 2 + 1, NT + 1):
                        h = i // (NT + 1)
                        pe.wait_ge(pt_lo, 8 * s + 4 * h + 4 + 2)
                        unit(U_XA + 4 * s + 2 + h, h,
                             [([(KV[:, 1, 0, m, c * P:(c + 1) * P], KV[:, 1, 1, m, c * P:(c + 1) * P],
                                 PTh[:, m, :], PTl[:, m, :]) for m in range(MT)], HALF) for c in range(2)])
                down(D_XA + s, Q_XA + 16 * s, Q_XA, lambda h: pe.wait_ge(o_lo, 2 * s + h + 1))
            for t in range(NT):
                pe.wait_ge(ln_done, LN_BASE["ln3"] + t + 1)
                transposes(Q_LN3, t)
            pe.wait_ge(xt_lo, XT_BASE["ln3"] + 2 * NT)
            ffn(S_FFN2, U_FFN2, D_FFN2, Q_FFN2, H_FFN2)

        @block.scalar
        def _(act):
            op = nc.scalar.activation

            def split_gu(n, par):
                act.wait_ge(gu_in, n * 32 + 32)
                op(GUh[:, par, :, :], GUraw[:, :, :], ACT.Copy).then_inc(gu_hi, 1)

            def split_dw(m, q):
                act.wait_ge(dw_in, m * 32 + 32)
                act.wait_ge(tile_ready, q)
                op(DWh[:, :, :], DWraw[:, :, :], ACT.Copy).then_inc(dw_hi, 1)

            def unit_wait(u):
                act.wait_ge(unit_ready, u + 1)

            def transposed_hi(base, q0, t, off=0):
                for g in range(2):
                    q = q0 + 2 * t + g
                    act.wait_ge(tile_ready, q + 1)
                    op(XTh[:, 4 * g:4 * g + 4, t * P:(t + 1) * P],
                       PS[:, 4 + q % 4, :].rearrange("p (k t) -> p k t", k=4), ACT.Copy).then_inc(xt_hi, 1)

            def normalise(name, half):
                b = LN_BASE[name]
                n = min(4, LN_TILES[name])
                act.wait_ge(ln_nmr, LN_ORDER_HALF[name] + half + 1)
                for t in range(n * half, n * half + n):
                    op(X[:, t, :], X[:, t, :], ACT.Identity, bias=NMR[:, t:t + 1],
                       scale=RSTD[:, t:t + 1]).then_inc(ln_hat, 1)

            def layer_norm(name):
                for half in range(2 if LN_TILES[name] > 4 else 1):
                    normalise(name, half)
                if name in Q_BASE:
                    for t in range(LN_TILES[name]):
                        transposed_hi(XT_BASE[name], Q_BASE[name], t)

            def ffn(s0, u0, d0, q0, h0, last_phase):
                def pair(j, more):
                    split_dw(d0 + j, q0 + 16 * j)
                    for c in range(2):
                        for h in range(2):
                            i = 2 * c + h
                            u = u0 + 4 * j + i
                            unit_wait(u)
                            op(SIG[:, i % 2, :], PS[:, 2 * (i % 2), :], ACT.Silu).then_inc(act_out, 1)
                            act.wait_ge(unit_read, u + 3)
                            op(HTh[:, c, h * HALF:(h + 1) * HALF], H32[:, i % 2, :], ACT.Copy).then_inc(h_hi, 1)
                        if more:
                            split_gu(s0 + 2 + 2 * j + c, c)
                if last_phase:
                    with act.Fori(0, PAIRS - 1) as j:
                        pair(j, True)
                    pair(PAIRS - 1, False)
                else:
                    with act.Fori(0, PAIRS) as j:
                        pair(j, True)

            for n in range(2):
                split_gu(n, n)
            layer_norm("mem")
            for s in range(8):
                unit_wait(s)
                act.wait_ge(kv_stored[s % 2], 16 * (s // 2 + 1))
                v = KVO[:, s % 2, 0, :].rearrange("p (c n) -> p c n", c=2)
                op(v, PS[:, 2 * (s % 2):2 * (s % 2) + 2, 0:256], ACT.Copy).then_inc(kv_hi, 1)
                split_gu(s + 2, s % 2)
                act.wait_ge(kv_lo, s + 1)
                act.dma_start(kv_scratch[s % 4, :, s // 4, :, :], KVO[:, s % 2, :, :].bitcast(F32))\
                    .then_inc(kv_stored[s % 2], 16)
            for b in range(2):
                act.wait_ge(kv_stored[b], 16 * 5)
            for t in range(NT):
                transposed_hi(XT_BASE["x"], Q_X, t)
            ffn(S_FFN1, U_FFN1, D_FFN1, Q_FFN1, H_FFN1, False)
            layer_norm("ln1")

            act.wait_ge(ab_in, 16)
            op(ABh[:, :, :], ABRAW[:, :, :], ACT.Copy).then_inc(ab_split, 1)
            act.wait_ge(sem("ab_sum"), 1)
            op(GT[:, :, G_BETA, :], ABT[:, :, HEADS:], ACT.Sigmoid).then_inc(sem("beta"), 1)
            op(AB2[:, :, :], AB1[:, :, :], ACT.Abs).then_inc(sem("ab_abs"), 1)
            act.wait_ge(sem("ab_abs"), 1)
            op(AB2[:, :, :], AB2[:, :, :], ACT.Exp, scale=-1.0).then_inc(sem("ab_abs"), 1)
            op(AB4[:, :], HPAR[:, 1, :], ACT.Exp).then_inc(sem("a_exp"), 1)
            act.wait_ge(sem("ab_abs"), 2)
            op(AB2[:, :, :], AB2[:, :, :], ACT.Ln, bias=1.0).then_inc(sem("ab_ln"), 1)
            act.wait_ge(sem("cum_read"), 1)
            op(GT[:, :, G_ECUM:G_ELAST + 1, :], GT[:, :, G_ECUM:G_ELAST + 1, :], ACT.Exp).then_inc(sem("g_exp"), 1)

            def store(j, par, chunks, h):
                act.wait_ge(cout_done, j + 3)
                act.dma_start(chunks[:, :, h * HALF:(h + 1) * HALF], COUT[:, par, :, :]).then_inc(stored[par], 16)

            def raw_frames(dst, h, u):
                act.wait_ge(unit_ready, u + 1)
                op(dst[:, :, HALO + h * HALF:HALO + (h + 1) * HALF], PS[:, 2 * h:2 * h + 2, :], ACT.Copy)\
                    .then_inc(unit_read, 1)

            for s in range(2):
                for h in range(2):
                    if s == 1 and h == 0:
                        act.wait_ge(pooled, 2)
                    raw_frames(RAWP, h, U_P + 2 * s + h)
                split_gu(S_P + 2 + s, s)
            with act.Fori(0, 3) as j:
                for s in range(2):
                    for h in range(2):
                        v = 4 * j + 2 * s + h
                        act.wait_ge(conv_done, v + 1)
                        raw_frames(RAW, h, v + U_QKV)
                        act.wait_ge(conv_done, v + 2)
                        act.wait_ge(stored[h], j * 32 + 16 * s + 16)
                        op(COUT[:, h, :, :], CACC[:, h, :, :], ACT.Silu).then_inc(cout_done, 1)
                        store(v, h, proj_v[:, bass.ds(4 * j + 2 * s, 2), :], h)
                    split_gu(S_QKV + 2 + 2 * j + s, s)
            act.wait_ge(x_spilled, 16)
            for g in range(GROUPS):
                for h in range(2):
                    q = Q_POOL + 2 * g + h
                    act.wait_ge(tile_ready, q + 1)
                    op(FEAT[:, 4 + g, h * HALF:(h + 1) * HALF], PS[:, 4 + q % 4, :], ACT.Copy,
                       scale=PSCALE[:, g:g + 1]).then_inc(tile_read, 1)
            for s in range(2):
                for h in range(2):
                    v = 12 + 2 * s + h
                    act.wait_ge(unit_ready, v + U_QKV + 1)
                    act.wait_ge(stored[h], 16 * (v // 2 + 1))
                    op(COUT[:, h, :, :], PS[:, 2 * h:2 * h + 2, :], ACT.Silu).then_inc(cout_done, 1)
                    act.wait_ge(cout_done, v + 3)
                    act.sem_inc(unit_read, 1)
                    store(v, h, proj_v[:, CH_Z + 2 * s:CH_Z + 2 * s + 2, :], h)
                if s == 0:
                    split_gu(S_GATE, 0)

            def copy(dst, bank, name):
                op(dst[:, :, :], PS[:, bank, :].rearrange("p (h t) -> p h t", h=HEADS), ACT.Copy)\
                    .then_inc(sem(name), 1)

            def delta_step(n, m, par, scan, prep):
                new = 1 - par

                def of_scan(name):
                    act.wait_ge(sem(name), n + 1)

                def of_prep(name):
                    act.wait_ge(sem(name), m + 1)

                def gate(g):
                    act.wait_ge(gp_ready, m * 4 + g + 1)
                    act.wait_ge(gate_stored[g], m * 16 + 16)
                    op(GOUT[:, g, :], PS[:, g % 2, :], ACT.Sigmoid).then_inc(gp_read, 1)
                    act.wait_ge(gp_read, m * 4 + g + 3)
                    dst = proj_scratch[bass.ds(m * 2 + CH_GDN + g // 2, 1), :, g % 2 * HALF:(g % 2 + 1) * HALF]
                    act.dma_start(dst.rearrange("c p t -> p (c t)"), GOUT[:, g, :]).then_inc(gate_stored[g], 16)

                if prep:
                    for src, dst, bank, name in (("k_tok", K0, 2, "k0"), ("q_tok", Q0, 3, "q0"),
                                                 ("v_tok", V0, 4, "v0")):
                        of_prep(src)
                        copy(dst, bank, name)
                if scan:
                    of_scan("q_state")
                    for h in range(HEADS):
                        last = op(QS[:, h, :], PS[:, 7, h * P:(h + 1) * P], ACT.Copy,
                                  scale=GTN[par][:, G_ECUM, h:h + 1])
                    last.then_inc(sem("q_state_dec"), 1)
                    of_scan("v_new_ps")
                    copy(VN, 6, "v_new")
                if prep:
                    of_prep("dif_pos")
                    op(E1[:, :, :], E1[:, :, :], ACT.Exp, scale=-1.0).then_inc(sem("decay"), 1)
                    of_prep("dif_neg")
                    op(E2[:, :, :], E2[:, :, :], ACT.Exp).then_inc(sem("decayT"), 1)
                    gate(0)
                    of_prep("kT_ps")
                    copy(KT[new], 2, "kT")
                    of_prep("qT_ps")
                    copy(QT[new], 3, "qT")
                    split_gu(S_GATE + 1 + m, par)
                    of_prep("lowT_ps")
                    copy(LT, 2, "lowT")
                    of_prep("inv0T_ps")
                    copy(TT[new], 3, "inv0T")
                    gate(1)
                    for lv in range(LEVELS - 1):
                        act.wait_ge(sem("inv_ps"), m * (LEVELS - 1) + lv + 1)
                        copy(T, 2, "inv")
                        if lv == 2:
                            gate(2)
                    gate(3)
                else:
                    split_gu(S_MIX + 1, 1)
                    for g in range(GROUPS):
                        op(XTh[:, 4 + g, :], FEAT[:, 4 + g, :], ACT.Copy).then_inc(feat_hi, 1)

            for b in range(2):
                act.wait_ge(stored[b], 16 * 9)
            delta_step(None, 0, 1, False, True)
            with act.Fori(0, 3) as j:
                for r in range(2):
                    delta_step(2 * j + r, 2 * j + r + 1, r, True, True)
            delta_step(NT - 2, NT - 1, 0, True, True)
            delta_step(NT - 1, None, 1, True, False)
            act.wait_ge(sem("oT"), NT)
            for h in range(2):
                for k in range(0, 4, 2):
                    to = (slice(None), slice(k, k + 2), slice(h * HALF, (h + 1) * HALF))
                    op(XTh[to], FEAT[to], ACT.Copy).then_inc(feat_hi, 1)

            for s in range(4):
                split_dw(D_MIX + s, Q_MIX + 16 * s)
                for i in range(4):
                    u = U_MIX + 4 * s + i
                    unit_wait(u)
                    act.wait_ge(sem("merged"), 4 * s + i + 1)
                    op(HTh[:, i // 2, i % 2 * HALF:(i % 2 + 1) * HALF], H32[:, i % 2, :], ACT.Copy)\
                        .then_inc(h_hi, 1)
                split_gu(S_MIX + 2 + s, s % 2)
            layer_norm("ln2")

            for s in range(4):
                for h in range(2):
                    unit_wait(U_XA + 4 * s + h)
                    if s:
                        act.wait_ge(tile_ready, Q_XA + 16 * s)
                    op(HTh[:, :, h * HALF:(h + 1) * HALF], PS[:, 2 * h:2 * h + 2, :], ACT.Copy,
                       scale=XD ** -0.5).then_inc(q_hi, 1)
                split_gu(S_XA + 2 + s, s % 2)
                split_dw(D_XA + s, Q_XA + 16 * s)
                for i in range(NT + 2):
                    if i < NT:
                        act.wait_ge(neg_max, 8 * s + i + 1)
                        if 8 * s + i >= 4:
                            act.wait_ge(pt_ready, 8 * s + i - 3)
                        op(PR[:, i % 4, :], PS[:, 4 + i % 2, 0:N_MEM], ACT.Exp, bias=NEGMAX[:, i:i + 1],
                           accum_out=RSUM[:, i:i + 1]).then_inc(s_read, 1)
                    if i >= 2:
                        t = i - 2
                        act.wait_ge(pt_ready, 8 * s + t + 1)
                        if t % 4 == 0 and 2 * s + t // 4 >= 1:
                            act.wait_ge(unit_ready, U_XA + 4 * s + 3 if t else U_XA + 4 * s)
                        op(PTh[:, :, t % 4 * P:(t % 4 + 1) * P],
                           PS[:, 6 + t % 2, 0:N_MEM].rearrange("p (m t) -> p m t", m=MT), ACT.Copy)\
                            .then_inc(pt_hi, 1)
                    if i in (NT // 2 + 1, NT + 1):
                        h = i // (NT + 1)
                        unit_wait(U_XA + 4 * s + 2 + h)
                        op(HTh[:, :, h * HALF:(h + 1) * HALF], PS[:, 2 * h:2 * h + 2, :], ACT.Copy)\
                            .then_inc(o_hi, 1)
            layer_norm("ln3")
            ffn(S_FFN2, U_FFN2, D_FFN2, Q_FFN2, H_FFN2, True)
            layer_norm("ln4")

        @block.gpsimd
        def _(pool):
            tt = nc.gpsimd.tensor_tensor

            def split_gu(n, par):
                pool.wait_ge(gu_hi, n + 1)
                tt(GUl[:, par, :, :], GUraw[:, :, :], GUh[:, par, :, :].bitcast(F32), ALU.subtract)\
                    .then_inc(gu_lo, 1)

            def split_dw(m):
                pool.wait_ge(dw_hi, m + 1)
                tt(DWl[:, :, :], DWraw[:, :, :], DWh[:, :, :].bitcast(F32), ALU.subtract).then_inc(dw_lo, 1)

            def split_half(v, i):
                pool.wait_ge(h_hi, v + 1)
                to = (slice(None), i // 2, slice(i % 2 * HALF, (i % 2 + 1) * HALF))
                tt(HTl[to], H32[:, i % 2, :], HTh[to].bitcast(F32), ALU.subtract).then_inc(h_lo, 1)

            def layer_norm(name):
                n = min(4, LN_TILES[name])
                for half in range(2 if LN_TILES[name] > 4 else 1):
                    pool.wait_ge(ln_var, LN_ORDER_HALF[name] + half + 1)
                    c = slice(n * half, n * half + n)
                    tt(RSTD[:, c], VE[:, c], COUNT[:, HALO:HALO + n], ALU.pow).then_inc(ln_rstd, 1)

            def ffn(s0, d0, h0, last_phase):
                def pair(j, more):
                    split_dw(d0 + j)
                    for c in range(2):
                        for h in range(2):
                            split_half(h0 + 4 * j + 2 * c + h, 2 * c + h)
                        if more:
                            split_gu(s0 + 2 + 2 * j + c, c)
                if last_phase:
                    with pool.Fori(0, PAIRS - 1) as j:
                        pair(j, True)
                    pair(PAIRS - 1, False)
                else:
                    with pool.Fori(0, PAIRS) as j:
                        pair(j, True)

            pool.sem_inc(gu_lo, 1)
            pool.sem_inc(dw_lo, 1)
            pool.sem_inc(h_lo, 2)
            pool.sem_inc(gp_read, 2)
            for i in range(4):
                pool.sem_inc(gate_stored[i], 16)
            pool.wait_ge(const_in, 16 * 7)
            for n in range(2):
                split_gu(n, n)
            layer_norm("mem")
            for s in range(8):
                split_gu(s + 2, s % 2)
            ffn(S_FFN1, D_FFN1, H_FFN1, False)
            layer_norm("ln1")
            pool.wait_ge(ab_split, 1)
            tt(ABl[:, :, :], ABRAW[:, :, :], ABh[:, :, :].bitcast(F32), ALU.subtract).then_inc(ab_split, 1)
            with pool.Fori(0, (S_Z - S_P) // 2) as j:
                for s in range(2):
                    split_gu(S_P + 2 + 2 * j + s, s)
            split_gu(S_GATE, 0)

            def delta_step(n, m, par, scan, prep):
                new = 1 - par

                def of_scan(name):
                    pool.wait_ge(sem(name), n + 1)

                def of_prep(name):
                    pool.wait_ge(sem(name), m + 1)

                over = lambda kind: GTN[new][:, kind, :].unsqueeze(2).broadcast_to([P, HEADS, P])
                mask = lambda i: MASK[:, i, :].unsqueeze(1).broadcast_to([P, HEADS, P])
                if prep:
                    of_prep("norm_arg")
                    tt(RN[:, :, :], SS[:, 0:2, :], COUNT[:, HALO:HALO + 8].rearrange("p (a h) -> p a h", a=2),
                       ALU.pow).then_inc(sem("norm_inv"), 1)
                    of_prep("v0")
                    tt(VB[new][:, :, :], V0[:, :, :], over(G_BETA), ALU.mult).then_inc(sem("v_beta"), 1)
                    of_prep("decay")
                    tt(E1[:, :, :], E1[:, :, :], mask(M_LOW), ALU.mult).then_inc(sem("decay_low"), 1)
                    of_prep("decay_low")
                    tt(E1[:, :, :], E1[:, :, :], over(G_BETA), ALU.mult).then_inc(sem("decay_beta"), 1)
                if scan:
                    of_scan("rms_arg")
                    tt(RNO[:, :], SSO[:, 1, :], COUNT[:, HALO:HALO + HEADS], ALU.pow).then_inc(sem("rms_inv"), 1)
                if prep:
                    of_prep("decayT")
                    tt(E2[:, :, :], E2[:, :, :], mask(M_UP), ALU.mult).then_inc(sem("decayT_up"), 1)
                    of_prep("k_unit")
                    tt(KDEC[new][:, :, :], KN[:, :, :], over(G_ETAIL), ALU.mult).then_inc(sem("k_dec"), 1)
                    for lv in range(LEVELS):
                        if lv >= 2:
                            pool.wait_ge(sem("lev_pT"), m * LEVELS + lv - 1)
                        tt(MM[lv % 2][:, :, :], mask(M_ID), mask(M_ID), ALU.subtract).then_inc(sem("mm_zero"), 1)
                        if lv == 1:
                            split_gu(S_GATE + 1 + m, par)
                else:
                    split_gu(S_MIX + 1, 1)
                    for g in range(GROUPS):
                        pool.wait_ge(feat_hi, g + 1)
                        tt(XTl[:, 4 + g, :], FEAT[:, 4 + g, :], XTh[:, 4 + g, :].bitcast(F32), ALU.subtract)\
                            .then_inc(feat_lo, 1)

            delta_step(None, 0, 1, False, True)
            with pool.Fori(0, 3) as j:
                for r in range(2):
                    delta_step(2 * j + r, 2 * j + r + 1, r, True, True)
            delta_step(NT - 2, NT - 1, 0, True, True)
            delta_step(NT - 1, None, 1, True, False)

            for s in range(4):
                split_dw(D_MIX + s)
                for i in range(4):
                    v = 4 * s + i
                    pool.wait_ge(gated_b, v + 3)
                    tt(H32[:, i % 2, :], H32[:, i % 2, :], SIG[:, i % 2, :], ALU.add).then_inc(sem("merged"), 1)
                    split_half(H_MIX + v, i)
                split_gu(S_MIX + 2 + s, s % 2)
            layer_norm("ln2")
            for s in range(4):
                split_gu(S_XA + 2 + s, s % 2)
                split_dw(D_XA + s)
            layer_norm("ln3")
            ffn(S_FFN2, D_FFN2, H_FFN2, True)
            layer_norm("ln4")

        @block.vector
        def _(dve):
            v = nc.vector

            steps = [0]

            def chain(ins):
                steps[0] += 1
                ins.then_inc(small_step, 1)
                dve.wait_ge(small_step, steps[0])

            def stats(t):
                for i in range(2):
                    chain(v.bn_stats(BNS[:, i, :], X[:, t, i * 512:(i + 1) * 512]))
                chain(v.bn_aggr(MV[:, t, :], BNS[:, :, :]))

            def layer_norm(name):
                tiles = LN_TILES[name]
                n = min(4, tiles)
                k = LN_ORDER[name]
                for half in range(2 if tiles > 4 else 1):
                    for t in range(n * half, n * half + n):
                        stats(t)
                    c = slice(n * half, n * half + n)
                    v.tensor_scalar(VE[:, c], MV[:, c, 1], LN_EPS, None, ALU.add).then_inc(ln_var, 1)
                    dve.wait_ge(ln_rstd, LN_ORDER_HALF[name] + half + 1)
                    v.scalar_tensor_tensor(NMR[:, c], MV[:, c, 0], -1.0, RSTD[:, c], ALU.mult, ALU.mult)\
                        .then_inc(ln_nmr, 1)
                dve.wait_ge(ln_par_in, 32 * (k + 1))
                for t in range(tiles):
                    dve.wait_ge(ln_hat, LN_BASE[name] + t + 1)
                    v.tensor_tensor(X[:, t, :], X[:, t, :], LNG[:, :], ALU.mult).then_inc(ln_scaled, 1)
                    dve.wait_ge(ln_scaled, LN_BASE[name] + t + 1)
                    v.tensor_tensor(X[:, t, :], X[:, t, :], LNB[:, :], ALU.add).then_inc(ln_done, 1)
                dve.wait_ge(ln_done, LN_BASE[name] + tiles)
                dve.sem_inc(ln_par_used, 1)
                if name in Q_BASE:
                    transposed_lo(name, tiles)

            def transposed_lo(name, tiles):
                for t in range(tiles):
                    for g in range(2):
                        i = 2 * t + g
                        q = Q_BASE[name] + i
                        dve.wait_ge(xt_hi, XT_BASE[name] + i + 1)
                        to = (slice(None), slice(4 * g, 4 * g + 4), slice(t * P, (t + 1) * P))
                        v.tensor_tensor(XTl[to], PS[:, 4 + q % 4, :].rearrange("p (k t) -> p k t", k=4),
                                        XTh[to].bitcast(F32), ALU.subtract).then_inc(xt_lo, 1)
                        dve.wait_ge(xt_lo, XT_BASE[name] + i + 1)
                        dve.sem_inc(tile_read, 1)
                    if name != "mem":
                        v.tensor_scalar(X[:, t, :], X[:, t, :], ALPHA, None, ALU.mult).then_inc(x_scaled, 1)

            def residual_add(q0, qp):
                i = 0
                for t in range(NT):
                    for n in range(2):
                        dve.wait_ge(tile_ready, q0 + i + 1)
                        c = slice(n * 512, (n + 1) * 512)
                        v.tensor_tensor(X[:, t, c], X[:, t, c], PS[:, 4 + (qp + i) % 4, :], ALU.add)\
                            .then_inc(tile_read, 1)
                        i += 1

            def ffn(u0, q0, h0):
                with dve.Fori(0, PAIRS) as j:
                    for i in range(4):
                        dve.wait_ge(act_out, j * 4 + (h0 if h0 == 0 else 4 * PAIRS) + i + 1)
                        dve.wait_ge(h_lo, j * 4 + h0 + i + 1)
                        v.scalar_tensor_tensor(H32[:, i % 2, :], SIG[:, i % 2, :], 0.5,
                                               PS[:, 2 * (i % 2) + 1, :], ALU.mult, ALU.mult)\
                            .then_inc(unit_read, 1)
                    residual_add(q0 + 16 * j, q0)

            dve.sem_inc(unit_read, 2)
            dve.sem_inc(tile_read, 4)
            dve.sem_inc(kv_stored[0], 16)
            dve.sem_inc(kv_stored[1], 16)
            dve.sem_inc(stored[0], 16)
            dve.sem_inc(stored[1], 16)
            dve.sem_inc(conv_done, 1)
            dve.sem_inc(cout_done, 2)
            dve.sem_inc(gated_b, 2)
            dve.sem_inc(kvh_used, 1)
            dve.sem_inc(s_read, 2)
            dve.sem_inc(pt_lo, 2)

            dve.wait_ge(mem_in, 16)
            layer_norm("mem")
            for s in range(8):
                dve.wait_ge(kv_hi, s + 1)
                r = lambda i: KVO[:, s % 2, i, :].rearrange("p (c n) -> p c n", c=2)
                v.tensor_tensor(r(1), PS[:, 2 * (s % 2):2 * (s % 2) + 2, 0:256], r(0).bitcast(F32),
                                ALU.subtract).then_inc(kv_lo, 1)
                dve.wait_ge(kv_lo, s + 1)
                dve.sem_inc(unit_read, 1)
            transposed_lo("x", NT)
            dve.wait_ge(x_scaled, NT)
            ffn(U_FFN1, Q_FFN1, H_FFN1)
            dve.wait_ge(tile_read, Q_LN1 + 4)
            layer_norm("ln1")

            dve.wait_ge(tile_ready, Q_AB + 1)
            v.tensor_copy(ABT[:, :, :], PS[:, 4 + Q_AB % 4, 0:8 * NT].rearrange("p (t c) -> p t c", t=NT))\
                .then_inc(tile_read, 1)
            dve.wait_ge(tile_read, Q_AB + 5)
            v.tensor_tensor(AB1[:, :, :], ABT[:, :, 0:HEADS],
                            HPAR[:, 0, :].unsqueeze(1).broadcast_to([P, NT, HEADS]), ALU.add)\
                .then_inc(sem("ab_sum"), 1)
            dve.wait_ge(sem("ab_sum"), 1)
            chain(v.tensor_scalar(AB3[:, :, :], AB1[:, :, :], 0.0, None, ALU.max))
            dve.wait_ge(sem("ab_ln"), 1)
            chain(v.tensor_tensor(AB3[:, :, :], AB3[:, :, :], AB2[:, :, :], ALU.add))
            dve.wait_ge(sem("a_exp"), 1)
            v.scalar_tensor_tensor(GT[:, :, G_G, :], AB3[:, :, :], -1.0,
                                   AB4[:, :].unsqueeze(1).broadcast_to([P, NT, HEADS]), ALU.mult, ALU.mult)\
                .then_inc(ab_done, 1)
            dve.wait_ge(sem("cum_ready"), 1)
            cum = PS[:, 4, 0:NT * HEADS].rearrange("p (t h) -> p t h", h=HEADS)
            total = PS[:, 5, 0:NT * HEADS].rearrange("p (t h) -> p t h", h=HEADS)
            chain(v.tensor_copy(GT[:, :, G_CUM, :], cum))
            v.tensor_copy(GT[:, :, G_ECUM, :], cum)
            v.tensor_tensor(GT[:, :, G_ETAIL, :], total, GT[:, :, G_CUM, :], ALU.subtract)
            v.tensor_copy(GT[:, :, G_ELAST, :], total).then_inc(sem("cum_read"), 1)
            dve.wait_ge(sem("g_exp"), 1)
            dve.wait_ge(sem("beta"), 1)
            chain(v.scalar_tensor_tensor(GT[:, :, G_NBE, :], GT[:, :, G_BETA, :], -1.0, GT[:, :, G_ECUM, :],
                                         ALU.mult, ALU.mult))

            chain(v.memset(RAW[:, :, 0:HALO], 0.0))
            chain(v.memset(RAWP[:, :, 0:HALO], 0.0))
            for i in range(2):
                chain(v.memset(WSUM[i][:, 0:HALO], 0.0))
            for g in range(GROUPS):
                if g % 2 == 0:
                    dve.wait_ge(unit_read, U_P + g + 2 + 2)
                src = RAWP[:, g % 2]
                for i in range(g + 1):
                    dst = WSUM[i % 2]
                    lag = 1 << i
                    chain(v.tensor_tensor(dst[:, HALO:], src[:, HALO:], src[:, HALO - lag:HALO + SEQ - lag],
                                          ALU.add))
                    src = dst
                win = 2 << g
                frame = RAWP[:, g % 2, HALO:]
                chain(v.scalar_tensor_tensor(MIXED[:, g, :], src[:, HALO:], 1.0 / win, frame, ALU.mult,
                                             ALU.subtract))
                chain(v.tensor_tensor(MIXED[:, g, 0:win], src[:, HALO:HALO + win], COUNT[:, 0:win], ALU.mult))
                v.tensor_tensor(MIXED[:, g, 0:win], MIXED[:, g, 0:win], frame[:, 0:win], ALU.subtract)\
                    .then_inc(pooled, 1)
            with dve.Fori(0, 3) as j:
                for s in range(2):
                    for h in range(2):
                        w = 4 * j + 2 * s + h
                        dve.wait_ge(unit_read, w + U_QKV + 3)
                        dve.wait_ge(cout_done, w + 1)
                        for k in range(CONV_K):
                            if k:
                                dve.wait_ge(tap, w * (2 * CONV_K - 2) + 2 * k)
                            for c in range(2):
                                src = RAW[:, c, HALO - CONV_K + 1 + k + h * HALF:HALO - CONV_K + 1 + k + (h + 1) * HALF]
                                wt = CONVW[:, bass.ds(4 * j + 2 * s + c, 1), k]
                                if k == 0:
                                    ins = v.tensor_scalar(CACC[:, h, c, :], src, wt, None, ALU.mult)
                                else:
                                    ins = v.scalar_tensor_tensor(CACC[:, h, c, :], src, wt, CACC[:, h, c, :],
                                                                 ALU.mult, ALU.add)
                                if k < CONV_K - 1:
                                    ins.then_inc(tap, 1)
                        ins.then_inc(conv_done, 1)
            dve.wait_ge(tile_read, Q_MIX + 4)
            v.memset(ST[:, :, :], 0.0).then_inc(sem("state"), 1)

            def delta_step(n, m, par, scan, prep):
                new = 1 - par

                def of_scan(name):
                    dve.wait_ge(sem(name), n + 1)

                def of_prep(name):
                    dve.wait_ge(sem(name), m + 1)

                def bank(b):
                    return PS[:, b, :].rearrange("p (h t) -> p h t", h=HEADS)

                def signal(ins, name):
                    ins.then_inc(sem(name), 1)

                over = lambda t: t.unsqueeze(2).broadcast_to([P, HEADS, P])
                mask = lambda i: MASK[:, i, :].unsqueeze(1).broadcast_to([P, HEADS, P])
                if prep:
                    signal(v.tensor_copy(GTN[new][:, :, :], GT[:, bass.ds(m, 1), :, :].squeeze(1)), "scalars")
                    of_prep("k0")
                    signal(v.tensor_tensor(SQ[:, :, :], K0[:, :, :], K0[:, :, :], ALU.mult), "k_sq")
                    of_prep("q0")
                    signal(v.tensor_tensor(SQ2[:, :, :], Q0[:, :, :], Q0[:, :, :], ALU.mult), "q_sq")
                    of_prep("k_sq")
                    signal(v.tensor_reduce(SS[:, 2, :], SQ[:, :, :], AX.X, ALU.add), "k_ss")
                    of_prep("q_sq")
                    signal(v.tensor_reduce(SS[:, 3, :], SQ2[:, :, :], AX.X, ALU.add), "q_ss")
                    of_prep("k_ss")
                    v.tensor_scalar(SS[:, 0, :], SS[:, 2, :], 1.0, L2_EPS, ALU.mult, ALU.add)
                    of_prep("q_ss")
                    signal(v.tensor_scalar(SS[:, 1, :], SS[:, 3, :], float(HD), HD * L2_EPS, ALU.mult, ALU.add),
                           "norm_arg")
                if scan:
                    of_scan("k_state")
                    of_scan("v_beta")
                    for h in range(HEADS):
                        ins = v.scalar_tensor_tensor(R[:, h, :], PS[:, 6, h * P:(h + 1) * P],
                                                     GTN[par][:, G_NBE, h:h + 1], VB[par][:, h, :],
                                                     ALU.mult, ALU.add)
                    signal(ins, "resid")
                if prep:
                    of_prep("cum_rows")
                    of_prep("scalars")
                    signal(v.tensor_tensor(DIF[:, :, :], bank(5), over(GTN[new][:, G_CUM, :]), ALU.subtract), "dif")
                    of_prep("dif")
                    signal(v.tensor_scalar(E1[:, :, :], DIF[:, :, :], 0.0, None, ALU.max), "dif_pos")
                    signal(v.tensor_scalar(E2[:, :, :], DIF[:, :, :], 0.0, None, ALU.min), "dif_neg")
                    of_prep("norm_inv")
                    signal(v.tensor_tensor(KN[:, :, :], K0[:, :, :], over(RN[:, 0, :]), ALU.mult), "k_unit")
                    signal(v.tensor_tensor(QN[:, :, :], Q0[:, :, :], over(RN[:, 1, :]), ALU.mult), "q_unit")
                if scan:
                    of_scan("kv_outer")
                    for h in range(HEADS):
                        ins = v.scalar_tensor_tensor(ST[:, h, :], ST[:, h, :], GTN[par][:, G_ELAST, h:h + 1],
                                                     PS[:, 6, h * P:(h + 1) * P], ALU.mult, ALU.add)
                    signal(ins, "state")
                    of_scan("o_intra")
                    signal(v.tensor_tensor(O[:, :, :], QS[:, :, :], bank(7), ALU.add), "o")
                    of_scan("o")
                    signal(v.tensor_tensor(OSQ[:, :, :], O[:, :, :], O[:, :, :], ALU.mult), "o_sq")
                    of_scan("o_sq")
                    signal(v.tensor_reduce(SSO[:, 0, :], OSQ[:, :, :], AX.X, ALU.add), "o_ss")
                    of_scan("o_ss")
                    signal(v.tensor_scalar(SSO[:, 1, :], SSO[:, 0, :], 1.0 / HD, RMS_EPS, ALU.mult, ALU.add),
                           "rms_arg")
                if prep:
                    of_prep("kk")
                    of_prep("decay_beta")
                    signal(v.tensor_tensor(L[:, :, :], bank(4), E1[:, :, :], ALU.mult), "low")
                    of_prep("low")
                    signal(v.tensor_tensor(T[:, :, :], L[:, :, :], mask(M_NEG1), ALU.mult), "inv_part")
                    of_prep("inv_part")
                    signal(v.tensor_tensor(T[:, :, :], T[:, :, :], mask(M_ID), ALU.add), "inv0")
                if scan:
                    of_scan("rms_inv")
                    signal(v.tensor_tensor(ON[:, :, :], O[:, :, :], over(RNO[:, :]), ALU.mult), "o_unit")
                if prep:
                    of_prep("qk")
                    of_prep("decayT_up")
                    signal(v.tensor_tensor(ATT[new][:, :, :], bank(5), E2[:, :, :], ALU.mult), "att")
                if scan:
                    of_scan("oT_ps")
                    dve.wait_ge(sem("z_in"), n * 16 + 16)
                    signal(v.scalar_tensor_tensor(FEAT[:, 0:HEADS, bass.ds(n * P, P)], bank(7), DNW[:, 0:1],
                                                  ZS[:, :, :], ALU.mult, ALU.mult), "oT")
                if prep:
                    for lv in range(LEVELS):
                        b = 2 << lv
                        half = lambda t, i: t.rearrange("p h (c two b) -> p h c two b", two=2, b=b)[:, :, :, i, :]
                        ps = lambda i: PS[:, i, 0:256].rearrange("p (h c b) -> p h c b", h=HEADS, b=b)
                        dve.wait_ge(sem("lev_m_ps"), m * LEVELS + lv + 1)
                        dve.wait_ge(sem("mm_zero"), m * LEVELS + lv + 1)
                        for h in range(HEADS):
                            ins = v.tensor_tensor(half(MM[lv % 2][:, h:h + 1, :], 0).squeeze(1), ps(4)[:, h],
                                                  half(mask(M_LEV + lv)[:, 0:1, :], 0).squeeze(1), ALU.mult)
                        ins.then_inc(sem("lev_m"), 1)
                        dve.wait_ge(sem("lev_pT"), m * LEVELS + lv + 1)
                        for h in range(HEADS):
                            to = half(TT[new][:, h:h + 1, :], 1).squeeze(1)
                            ins = v.tensor_tensor(to, to, ps(5)[:, h], ALU.subtract)
                        ins.then_inc(sem("invT"), 1)

            delta_step(None, 0, 1, False, True)
            with dve.Fori(0, 3) as j:
                for r in range(2):
                    delta_step(2 * j + r, 2 * j + r + 1, r, True, True)
            delta_step(NT - 2, NT - 1, 0, True, True)
            delta_step(NT - 1, None, 1, True, False)
            for h in range(2):
                for k in range(0, 4, 2):
                    i = 4 + 2 * h + k // 2
                    dve.wait_ge(feat_hi, i + 1)
                    to = (slice(None), slice(k, k + 2), slice(h * HALF, (h + 1) * HALF))
                    v.tensor_tensor(XTl[to], FEAT[to], XTh[to].bitcast(F32), ALU.subtract).then_inc(scan_lo, 1)

            for s in range(4):
                for i in range(4):
                    w = 4 * s + i
                    dve.wait_ge(unit_ready, U_MIX + w + 1)
                    dve.wait_ge(gate_in[i % 2], 16 * (w // 2 + 1))
                    dve.wait_ge(h_lo, H_MIX + w + 1)
                    v.tensor_tensor(H32[:, i % 2, :], GATE[:, i % 2, 0, :], PS[:, 2 * (i % 2), :], ALU.mult)
                    v.tensor_tensor(SIG[:, i % 2, :], GATE[:, i % 2, 1, :], PS[:, 2 * (i % 2) + 1, :], ALU.mult)\
                        .then_inc(gated_b, 1)
                    dve.wait_ge(gated_b, w + 3)
                    dve.sem_inc(unit_read, 1)
                if s == 0:
                    dve.wait_ge(x_back, 16)
                residual_add(Q_MIX + 16 * s, Q_MIX)
            dve.wait_ge(tile_read, Q_LN2 + 4)
            layer_norm("ln2")

            for s in range(4):
                for h in range(2):
                    dve.wait_ge(q_hi, 2 * s + h + 1)
                    to = (slice(None), slice(None), slice(h * HALF, (h + 1) * HALF))
                    v.scalar_tensor_tensor(HTl[to], PS[:, 2 * h:2 * h + 2, :], XD ** -0.5, HTh[to].bitcast(F32),
                                           ALU.mult, ALU.subtract).then_inc(q_lo, 1)
                    dve.wait_ge(q_lo, 2 * s + h + 1)
                    dve.sem_inc(unit_read, 1)
                for i in range(NT + 2):
                    if i < NT:
                        dve.wait_ge(s_ready, 8 * s + i + 1)
                        v.tensor_reduce(NEGMAX[:, i:i + 1], PS[:, 4 + i % 2, 0:N_MEM], AX.X, ALU.max, negate=True)\
                            .then_inc(neg_max, 1)
                        dve.wait_ge(s_read, 8 * s + i + 3)
                        v.reciprocal(RINV[:, i:i + 1], RSUM[:, i:i + 1]).then_inc(r_inv, 1)
                        dve.wait_ge(r_inv, 8 * s + i + 1)
                        v.tensor_scalar(PR[:, i % 4, :], PR[:, i % 4, :], RINV[:, i:i + 1], None, ALU.mult)\
                            .then_inc(p_norm, 1)
                    if i >= 2:
                        t = i - 2
                        dve.wait_ge(pt_hi, 8 * s + t + 1)
                        to = (slice(None), slice(None), slice(t % 4 * P, (t % 4 + 1) * P))
                        v.tensor_tensor(PTl[to], PS[:, 6 + t % 2, 0:N_MEM].rearrange("p (m t) -> p m t", m=MT),
                                        PTh[to].bitcast(F32), ALU.subtract).then_inc(pt_lo, 1)
                    if i in (NT // 2 + 1, NT + 1):
                        h = i // (NT + 1)
                        dve.wait_ge(o_hi, 2 * s + h + 1)
                        to = (slice(None), slice(None), slice(h * HALF, (h + 1) * HALF))
                        v.tensor_tensor(HTl[to], PS[:, 2 * h:2 * h + 2, :], HTh[to].bitcast(F32), ALU.subtract)\
                            .then_inc(o_lo, 1)
                        dve.wait_ge(o_lo, 2 * s + h + 1)
                        dve.sem_inc(unit_read, 1)
                dve.sem_inc(kvh_used, 1)
                residual_add(Q_XA + 16 * s, Q_XA)
            dve.wait_ge(tile_read, Q_LN3 + 4)
            layer_norm("ln3")
            dve.wait_ge(x_scaled, 4 * NT)
            ffn(U_FFN2, Q_FFN2, H_FFN2)
            dve.wait_ge(tile_read, Q_FFN2 + 16 * PAIRS + 4)
            layer_norm("ln4")


LN_ORDER_HALF = {"mem": 0, "ln1": 1, "ln2": 3, "ln3": 5, "ln4": 7}

_INS = ["x", "mem", "ffn1_w_gate", "ffn1_w_up", "ffn1_w_down", "ln1_g", "ln1_b", "w_in", "conv_w", "a_log",
        "dt_bias", "dn_norm_w", "w_dn_branch", "pool_w", "pool_scale", "w_pool_branch", "w_mix_out", "ln2_g",
        "ln2_b", "mem_ln_g", "mem_ln_b", "xa_wq", "xa_wk", "xa_wv", "xa_wo", "ln3_g", "ln3_b",
        "ffn2_w_gate", "ffn2_w_up", "ffn2_w_down", "ln4_g", "ln4_b"]


def kernel(**inputs):
    import concourse.bacc as bacc
    from concourse.bass_utils import run_bass_kernel_spmd

    nc = bacc.Bacc("TRN2", target_bir_lowering=False, num_devices=1)
    arrays, args = {}, {}
    given = {name: np.ascontiguousarray(inputs[name]) for name in _INS}
    given["conv_w"] = np.ascontiguousarray(given["conv_w"][0].reshape(CONV_K, CH_Z, P).transpose(2, 1, 0))
    given["pool_scale"] = np.ascontiguousarray(given["pool_scale"].reshape(GROUPS, P).T)
    given["dn_norm_w"] = given["dn_norm_w"].reshape(P, 1)
    given["masks"] = host_masks()
    given["counts"] = host_counts()
    for name, v in given.items():
        arrays[f"in_{name}"] = v
        args[name] = nc.dram_tensor(f"in_{name}", v.shape, F32, kind="ExternalInput").ap()
    args["out"] = nc.dram_tensor("out_x", (1, SEQ, D), F32, kind="ExternalOutput").ap()
    build(nc, args)
    r = run_bass_kernel_spmd(nc, [arrays], core_ids=[0])
    return r.results[0]["out_x"]
```

```python
from contextlib import ExitStack

import numpy as np
import concourse.bass as bass
from concourse import mybir

P = 128
SEQ = 1024
D = 1024
KD = D // P
NT = SEQ // P
HALF = 512
D_FF = 2816
PAIRS = D_FF // (2 * P)
N_MEM = 256
MT = N_MEM // P
HEADS = 4
HD = 128
XD = 256
QKV = 3 * HEADS * HD
CONV_K = 4
GROUPS = 4
HALO = 16
LN_EPS = 1e-5
RMS_EPS = 1e-6
L2_EPS = 1e-6
ALPHA = 2.0 ** 0.25
LEVELS = 6

COL_Z = QKV
COL_AB = COL_Z + HEADS * HD
COL_P = COL_AB + 2 * HEADS
COL_GDN = COL_P + GROUPS * P
COL_GPOOL = COL_GDN + D

CH_Z = QKV // P
CH_GDN = CH_Z + HEADS
CH_GPOOL = CH_GDN + KD
CHUNKS = CH_GPOOL + KD

F32 = mybir.dt.float32
F32R = mybir.dt.float32r
ALU = mybir.AluOpType
ACT = mybir.ActivationFunctionType
AX = mybir.AxisListType

S_FFN1 = 0
S_P = S_FFN1 + 2 * PAIRS
S_QKV = S_P + 2
S_Z = S_QKV + 6
S_GATE = S_Z + 2
S_MIX = S_GATE + NT
S_XA = S_MIX + 4
S_FFN2 = S_XA + 4
S_END = S_FFN2 + 2 * PAIRS

U_KV, U_FFN1 = 0, 8
U_P = U_FFN1 + 4 * PAIRS
U_QKV = U_P + 4
U_Z = U_QKV + 12
U_MIX = U_Z + 4
U_XA = U_MIX + 16
U_FFN2 = U_XA + 16
U_END = U_FFN2 + 4 * PAIRS

Q_MEM, Q_X = 0, 2 * MT
Q_FFN1 = Q_X + 2 * NT
Q_LN1 = Q_FFN1 + 16 * PAIRS
Q_AB = Q_LN1 + 2 * NT
Q_POOL = Q_AB + 3
Q_MIX = Q_POOL + 2 * GROUPS
Q_LN2 = Q_MIX + 16 * 4
Q_XA = Q_LN2 + 2 * NT
Q_LN3 = Q_XA + 16 * 4
Q_FFN2 = Q_LN3 + 2 * NT

D_FFN1, D_MIX = 0, PAIRS
D_XA = D_MIX + 4
D_FFN2 = D_XA + 4

LAG = {"ln1": 3, "ln2": 3, "ln3": 3, "ln4": 0}
REGION = {"ln1": Q_FFN1 + 16 * (PAIRS - 1), "ln2": Q_MIX + 16 * 3, "ln3": Q_XA + 16 * 3,
          "ln4": Q_FFN2 + 16 * (PAIRS - 1)}


def sum_tile(name, t, n):
    behind = max(0, t - LAG[name]) if name != "ln4" else 0
    return REGION[name] + 2 * t + 2 * behind + n


def turned_tile(name, t, g):
    if name in ("mem", "x"):
        return (Q_MEM if name == "mem" else Q_X) + 2 * t + g
    return REGION[name] + 2 * min(NT, t + LAG[name] + 1) + 2 * t + g


X_AFTER = {3: (0, 1, 2, 3), 4: (4,), 5: (5,), 6: (6, 7)}

HEAD_ORDER = [("queries", 0), ("more", 0), ("scores", 0), ("more", 1), ("turn", 0), ("scores", 1), ("more", 2),
              ("turn", 1), ("scores", 2), ("more", 3), ("turn", 2), ("scores", 3), ("more", 4), ("turn", 3),
              ("queries", 1), ("output", 0), ("scores", 4), ("sum", 0), ("scores", 5), ("sum", 1), ("turn", 4),
              ("sum", 2), ("scores", 6), ("sum", 3), ("turn", 5), ("scores", 7), ("sum", 4), ("turn", 6),
              ("sum", 5), ("turn", 7), ("output", 1)] + [("sum", i) for i in range(6, 16)]
MORE = [range(0, 4), range(4, 7), range(7, 10), range(10, 13), range(13, 16)]


SUMS_BEFORE = {"ln1": 0, "ln2": 0, "ln3": 3, "ln4": 0}
STATS_BEFORE = {"ln1": 0, "ln2": 0, "ln3": 2, "ln4": 0}


def head_order(s):
    return [(kind, i) for kind, i in HEAD_ORDER
            if not (s == HEADS - 1 and kind == "sum" and i >= 2 * SUMS_BEFORE["ln3"])]


H_FFN1, H_MIX = 0, 4 * PAIRS
H_FFN2 = H_MIX + 16

M_ID, M_UP, M_ONE, M_LOW, M_NEG1, M_LEV = 0, 1, 2, 3, 4, 5
N_MASKS = M_LEV + LEVELS


def host_masks():
    i = np.arange(P)[:, None]
    j = np.arange(P)[None, :]
    m = np.zeros((P, N_MASKS, P), np.float32)
    m[:, M_ID] = i == j
    m[:, M_UP] = i <= j
    m[:, M_ONE] = 1.0
    m[:, M_LOW] = i > j

    def level(b):
        return (i // (2 * b) == j // (2 * b)) & (i // b % 2 == 1) & (j // b % 2 == 0)

    m[:, M_NEG1] = -1.0 * level(1)
    for n in range(LEVELS):
        m[:, M_LEV + n] = level(2 << n)
    return m


def host_counts():
    c = np.zeros((P, 32), np.float32)
    c[:, 0:HALO] = 1.0 / (np.arange(HALO) + 1.0)
    c[:, HALO:] = -0.5
    return c


def build(nc, a):
    with ExitStack() as ctx:
        base = 16512
        place = {}

        def at(name, shape, dtype, where=None, offset=0):
            nonlocal base
            size = int(np.prod(shape[1:])) * 4
            if where is None:
                address = base
                base += (size + 31) // 32 * 32
            else:
                address = place[where] + offset
            place[name] = address
            return nc.alloc_sbuf_tensor_at(name, shape, dtype, offset=address)

        X = at("X", [P, NT, D], F32)
        XTh = at("XTh", [P, KD, SEQ], F32R)
        XTl = at("XTl", [P, KD, SEQ], F32R)
        GUraw = at("GUraw", [P, KD, 256], F32)
        GUh = at("GUh", [P, 2, KD, 256], F32R)
        GUl = at("GUl", [P, 2, KD, 256], F32R)
        DWraw = at("DWraw", [P, 2, D], F32)
        DWh = at("DWh", [P, 2, D], F32R)
        DWl = at("DWl", [P, 2, D], F32R)
        HTh = at("HTh", [P, 2, SEQ], F32R)
        HTl = at("HTl", [P, 2, SEQ], F32R)
        SIG = at("SIG", [P, 2, HALF], F32)
        H32 = at("H32", [P, 2, HALF], F32)
        PTh = at("PTh", [P, 2, HALF], F32R)
        PTl = at("PTl", [P, 2, HALF], F32R)
        LNG = at("LNG", [P, D], F32)
        LNB = at("LNB", [P, D], F32)
        MASK = at("MASK", [P, N_MASKS, P], F32)
        COUNT = at("COUNT", [P, 32], F32)
        BNS = at("BNS", [P, 2, 2, 6], F32)
        MV = at("MV", [P, NT, 2], F32)
        VE = at("VE", [P, NT], F32)
        RSTD = at("RSTD", [P, NT], F32)
        CONVW = at("CONVW", [P, CH_Z, CONV_K], F32)
        PSCALE = at("PSCALE", [P, GROUPS], F32)
        DNW = at("DNW", [P, 1], F32)
        HPAR = at("HPAR", [P, 2, HEADS], F32)
        G_G, G_CUM, G_ECUM, G_ETAIL, G_ELAST, G_BETA, G_NBE = range(7)
        GT = at("GT", [P, NT, 7, HEADS], F32)
        GTN = [at("GTN0", [P, 7, HEADS], F32), at("GTN1", [P, 7, HEADS], F32)]
        SS = at("SS", [P, 4, HEADS], F32)
        SSO = at("SSO", [P, 2, HEADS], F32)
        RN = at("RN", [P, 2, HEADS], F32)
        RNO = at("RNO", [P, HEADS], F32)
        assert base <= 229368, base

        KV = at("KV", [P, 2, 2, 2, XD], F32R, "LNG")
        PR = at("PR", [P, 4, N_MEM], F32, "SIG")
        NEGMAX = at("NEGMAX", [P, 8], F32, "H32")
        RSUM = at("RSUM", [P, 8], F32, "H32", 32)
        RINV = at("RINV", [P, 8], F32, "H32", 64)
        KVO = at("KVO", [P, 2, 2, 2 * N_MEM], F32R, "DWh")
        MEMX = at("MEMX", [P, MT, D], F32, "PTh")
        MTh = at("MTh", [P, KD, N_MEM], F32R, "HTh")
        MTl = at("MTl", [P, KD, N_MEM], F32R, "HTl")
        KW = [GUraw, at("KW1", [P, KD, 256], F32, "DWraw"), at("KW2", [P, KD, 256], F32, "DWl"),
              at("KW3", [P, KD, 256], F32, "SIG")]
        FRAMES = 2 * (HALO + SEQ) * 4
        RAWP = at("RAWP", [P, 2, HALO + SEQ], F32, "DWraw")
        RAW = at("RAW", [P, 2, HALO + SEQ], F32, "DWraw", FRAMES)
        POOLW = at("POOLW", [P, GROUPS, P], F32, "DWraw", 2 * FRAMES)
        CACC = at("CACC", [P, 2, 2, HALF], F32, "HTh")
        WSUM = [at("WSUM0", [P, HALO + SEQ], F32, "DWraw", 2 * FRAMES + GROUPS * P * 4),
                at("WSUM1", [P, HALO + SEQ], F32, "HTl")]
        COUT = at("COUT", [P, 2, 2, HALF], F32, "SIG")
        MIXED = at("MIXED", [P, GROUPS, SEQ], F32, "PTh")
        ABRAW = at("ABRAW", [P, KD, 8], F32, "PTh")
        ABh = at("ABh", [P, KD, 8], F32R, "PTh", 256)
        ABl = at("ABl", [P, KD, 8], F32R, "PTh", 512)
        ABT = at("ABT", [P, NT, 8], F32, "PTh", 768)
        AB1 = at("AB1", [P, NT, HEADS], F32, "PTh", 1024)
        AB2 = at("AB2", [P, NT, HEADS], F32, "PTh", 1152)
        AB3 = at("AB3", [P, NT, HEADS], F32, "PTh", 1280)
        ABROWS = at("ABROWS", [2 * HEADS, SEQ], F32, "PTl")
        AB4 = at("AB4", [P, HEADS], F32, "PTh", 1408)
        GATE = at("GATE", [P, 2, 2, HALF], F32, "PTh")
        FEAT = at("FEAT", [P, KD, SEQ], F32, "X")
        GOUT = at("GOUT", [P, 4, HALF], F32, "SIG")
        spots = [place["DWraw"] + i * 2048 for i in range(20)] + [place["PTh"] + i * 2048 for i in range(8)]

        def delta(name, spot, count=1):
            place[name] = spots[spot]
            return nc.alloc_sbuf_tensor_at(name, [P, HEADS * count, P], F32, offset=spots[spot])

        QKVS = delta("QKVS", 0, 3)
        KN, QN, DIF = delta("KN", 0), delta("QN", 1), delta("DIF", 2)
        K0, Q0, V0 = delta("K0", 3), delta("Q0", 4), delta("V0", 5)
        L, LT, T = delta("L", 3), delta("LT", 4), delta("T", 5)
        SQ, SQ2 = delta("SQ", 6), delta("SQ2", 7)
        E1, E2 = delta("E1", 6), delta("E2", 7)
        MM = [delta("MM0", 8), delta("MM1", 9)]
        two = lambda name, spot: [delta(name + str(i), spot + i) for i in range(2)]
        KT, QT, KDEC, VB, TT = two("KT", 10), two("QT", 12), two("KDEC", 14), two("VB", 16), two("TT", 18)
        ATT = two("ATT", 20)
        R, VN, QS, O, ST, ZS = (delta(x, 22 + i) for i, x in enumerate(("R", "VN", "QS", "O", "ST", "ZS")))
        OSQ, ON = R, QS

        gamma = lambda name: DWraw[:, 0, :] if name == "ln3" else LNG[:, :]
        beta = lambda name: DWraw[:, 1, :] if name == "ln3" else LNB[:, :]

        PS = ctx.enter_context(nc.psum_tensor("PS", [P, 8, 512], F32))
        ident = MASK[:, M_ID, :]

        proj_scratch = nc.dram_tensor("proj_scratch", [CHUNKS, P, SEQ], F32, kind="Internal").ap()
        kv_scratch = nc.dram_tensor("kv_scratch", [HEADS, P, 2, 2, 2 * N_MEM], F32, kind="Internal").ap()
        proj_v = proj_scratch.rearrange("c p t -> p c t")
        gate_v = proj_scratch[CH_GDN:CHUNKS].rearrange("(g c) p t -> p g c t", g=2)
        x_scratch = nc.dram_tensor("x_scratch", [P, NT, D], F32, kind="Internal").ap()
        rows = lambda w: w.rearrange("o (k p) n -> p (o k) n", p=P)
        col = lambda v: v.rearrange("o n -> (o n)")
        w_in = rows(a["w_in"])
        x_v = a["x"].rearrange("b (t p) d -> p (b t) d", p=P)
        out_v = a["out"].rearrange("b (t p) d -> p (b t) d", p=P)
        mem_v = a["mem"].rearrange("b (t p) d -> p (b t) d", p=P)

        sems = {}

        def sem(name):
            if name not in sems:
                sems[name] = ctx.enter_context(nc.semaphore(name))
            return sems[name]

        gu_in, gu_hi, gu_lo = sem("gu_in"), sem("gu_hi"), sem("gu_lo")
        dw_in, dw_hi, dw_lo = sem("dw_in"), sem("dw_hi"), sem("dw_lo")
        unit_ready, unit_read = sem("unit_ready"), sem("unit_read")
        first_chunk = sem("first_chunk")
        tile_ready, tile_read = sem("tile_ready"), sem("tile_read")
        act_out, h_hi, h_lo = sem("act_out"), sem("h_hi"), sem("h_lo")
        const_in, mask_in = sem("const_in"), sem("mask_in")
        mem_in = [sem("mem_in0"), sem("mem_in1")]
        x_in = [sem("x_in0"), sem("x_in1")]
        kw_in = [sem(f"kw_in{i}") for i in range(4)]
        kw_hi, kw_lo = sem("kw_hi"), sem("kw_lo")
        gamma_in, beta_in = sem("gamma_in"), sem("beta_in")
        bn_step, ln_mean = sem("bn_step"), sem("ln_mean")
        ln_var, ln_rstd, ln_scaled = sem("ln_var"), sem("ln_rstd"), sem("ln_scaled")
        ln_hat, ln_done, xt_hi = sem("ln_hat"), sem("ln_done"), sem("xt_hi")
        kv_hi, kv_lo = sem("kv_hi"), sem("kv_lo")
        kv_stored = [sem("kv_stored0"), sem("kv_stored1")]
        small_step = sem("small_step")
        ab_in, ab_split, ab_done = sem("ab_in"), sem("ab_split"), sem("ab_done")
        tap, conv_done = sem("tap"), sem("conv_done")
        cout_done = sem("cout_done")
        stored = [sem("stored0"), sem("stored1")]
        pooled, pool_w_in = sem("pooled"), sem("pool_w_in")
        gate_in = [sem("gate_in0"), sem("gate_in1")]
        gated_b = sem("gated_b")
        keys_in, values_in, kvh_used = sem("keys_in"), sem("values_in"), sem("kvh_used")
        q_hi, q_lo, o_hi, o_lo = sem("q_hi"), sem("q_lo"), sem("o_hi"), sem("o_lo")
        s_ready, s_read, neg_max = sem("s_ready"), sem("s_read"), sem("neg_max")
        r_inv, p_norm = sem("r_inv"), sem("p_norm")
        pt_ready, pt_hi, pt_lo = sem("pt_ready"), sem("pt_hi"), sem("pt_lo")
        out_stored = sem("out_stored")
        x_spilled, x_back = sem("x_spilled"), sem("x_back")
        gp_ready, gp_read = sem("gp_ready"), sem("gp_read")
        gate_stored = [sem(f"gate_stored{i}") for i in range(4)]
        feat_hi, feat_lo, scan_lo = sem("feat_hi"), sem("feat_lo"), sem("scan_lo")

        LN_ORDER = {"mem": 0, "ln1": 1, "ln2": 2, "ln3": 3, "ln4": 4}
        LN_BASE = {"mem": 0, "ln1": MT, "ln2": MT + NT, "ln3": MT + 2 * NT, "ln4": MT + 3 * NT}
        XT_BASE = {"mem": 0, "x": 2 * MT, "ln1": 2 * MT + 2 * NT, "ln2": 2 * MT + 4 * NT, "ln3": 2 * MT + 6 * NT}

        block = ctx.enter_context(nc.Block())

        @block.sync
        def _(sp):
            def load_gu(n, src_a, src_b):
                sp.wait_ge(gu_lo, n + 1)
                for dst, src in (src_a, src_b):
                    sp.dma_start(dst, src).then_inc(gu_in, 16)

            def load_cols(n, w, c):
                load_gu(n, (GUraw[:, 0:4, :], w[:, 0:4, bass.ds(c, 256)]),
                        (GUraw[:, 4:8, :], w[:, 4:8, bass.ds(c, 256)]))

            def load_gate_up(n, wg, wu, c):
                load_gu(n, (GUraw[:, :, 0:P], wg[:, :, bass.ds(c, P)]),
                        (GUraw[:, :, P:256], wu[:, :, bass.ds(c, P)]))

            def load_dw(m, w, row):
                sp.wait_ge(dw_lo, m + 1)
                for c in range(2):
                    sp.dma_start(DWraw[:, c, :], w[bass.ds(row + c * P, P), :]).then_inc(dw_in, 16)

            def load_ln(name, g, b):
                if name != "mem":
                    sp.wait_ge(ln_done, LN_BASE[name])
                if name == "ln3":
                    sp.wait_ge(dw_lo, D_XA + 4 + 1)
                sp.dma_start(gamma(name), g.broadcast_to([P, D])).then_inc(gamma_in, 16)
                sp.dma_start(beta(name), b.broadcast_to([P, D])).then_inc(beta_in, 16)

            def ffn_loads(s0, d0, wg, wu, wd, next_slots):
                with sp.Fori(0, PAIRS - 1) as j:
                    load_dw(d0 + j, wd, j * 256)
                    for c in range(2):
                        load_gate_up(s0 + 2 + 2 * j + c, wg, wu, j * 256 + 256 + c * P)
                load_dw(d0 + PAIRS - 1, wd, (PAIRS - 1) * 256)
                for f in next_slots:
                    f()

            for t in range(MT):
                sp.dma_start(MEMX[:, t, :], mem_v[:, t, :]).then_inc(mem_in[t], 16)
            load_ln("mem", a["mem_ln_g"], a["mem_ln_b"])
            sp.dma_start(COUNT[:, :], a["counts"]).then_inc(mask_in, 16)
            sp.dma_start(MASK[:, M_ID, :], a["masks"][:, M_ID, :]).then_inc(mask_in, 16)
            wk, wv = rows(a["xa_wk"]), rows(a["xa_wv"])

            def load_kv_weights(n):
                w = wk if n < 4 else wv
                if n >= 4:
                    sp.wait_ge(kw_lo, n - 3)
                for r in range(2):
                    sp.dma_start(KW[n % 4][:, 4 * r:4 * r + 4, :], w[:, 4 * r:4 * r + 4, n % 4 * 256:n % 4 * 256 + 256])\
                        .then_inc(kw_in[n % 4], 16)

            for n in range(4):
                load_kv_weights(n)
            for h in range(2):
                sp.dma_start(X[:, 4 * h:4 * h + 4, :], x_v[:, 4 * h:4 * h + 4, :]).then_inc(x_in[h], 16)
            for n in range(4, 8):
                load_kv_weights(n)
            wg, wu = rows(a["ffn1_w_gate"]), rows(a["ffn1_w_up"])
            sp.wait_ge(kw_lo, 6)
            for c in range(2):
                load_gate_up(S_FFN1 + c, wg, wu, c * P)
            sp.dma_start(MASK[:, M_ID + 1:, :], a["masks"][:, M_ID + 1:, :]).then_inc(const_in, 16)
            sp.dma_start(CONVW[:, :, :], a["conv_w"]).then_inc(const_in, 16)
            sp.dma_start(PSCALE[:, :], a["pool_scale"]).then_inc(const_in, 16)
            sp.dma_start(DNW[:, :], a["dn_norm_w"]).then_inc(const_in, 16)
            sp.dma_start(HPAR[:, 0, :], a["dt_bias"].broadcast_to([P, HEADS])).then_inc(const_in, 16)
            sp.dma_start(HPAR[:, 1, :], a["a_log"].broadcast_to([P, HEADS])).then_inc(const_in, 16)
            load_ln("ln1", a["ln1_g"], a["ln1_b"])
            ffn_loads(S_FFN1, D_FFN1, wg, wu, a["ffn1_w_down"][0],
                      [lambda c=c: load_cols(S_P + c, w_in, COL_P + c * 256) for c in range(2)])
            sp.wait_ge(ln_done, LN_BASE["ln1"] + NT)
            sp.dma_start(ABRAW[:, :, :], w_in[:, :, COL_AB:COL_AB + 8]).then_inc(ab_in, 16)
            sp.dma_start(POOLW[:, :, :], a["pool_w"].rearrange("o g c e -> c (o g) e")).then_inc(pool_w_in, 16)
            sp.dma_start(x_scratch, X[:, :, :]).then_inc(x_spilled, 16)
            with sp.Fori(0, 8) as j:
                load_cols(S_QKV + j, w_in, j * 256)
            for c in range(2):
                load_cols(S_GATE + c, w_in, COL_GDN + c * 256)
            wdn, wpo = rows(a["w_dn_branch"]), rows(a["w_pool_branch"])

            def load_branch(n, c):
                load_gu(n, (GUraw[:, 0:4, :], wdn[:, :, bass.ds(c, 256)]),
                        (GUraw[:, 4:8, :], wpo[:, :, bass.ds(c, 256)]))

            def load_qkv_tile(m):
                sp.dma_start(QKVS[:, :, :], proj_v[:, 0:CH_Z, bass.ds(m * P, P)]).then_inc(sem("qkv_in"), 16)

            def next_qkv_tile(m):
                for name in ("k_dec", "qT_ps", "dif_neg"):
                    sp.wait_ge(sem(name), m)
                load_qkv_tile(m)

            def load_z_tile(n):
                sp.dma_start(ZS[:, :, :], proj_v[:, CH_Z:CH_GDN, bass.ds(n * P, P)]).then_inc(sem("z_in"), 16)

            sp.wait_ge(tile_read, Q_MIX + 4)
            sp.wait_ge(conv_done, 12 + 1)
            for b in range(2):
                sp.wait_ge(stored[b], 16 * 7)
            load_qkv_tile(0)
            for b in range(2):
                sp.wait_ge(stored[b], 16 * 9)
            load_z_tile(0)
            with sp.Fori(0, NT - 2) as n:
                load_cols(S_GATE + 2 + n, w_in, n * 256 + COL_GDN + 512)
                next_qkv_tile(n + 1)
                sp.wait_ge(sem("oT"), n + 1)
                load_z_tile(n + 1)
            load_branch(S_MIX, 0)
            next_qkv_tile(NT - 1)
            sp.wait_ge(sem("oT"), NT - 1)
            load_z_tile(NT - 1)
            load_branch(S_MIX + 1, 256)
            for i in range(4):
                sp.wait_ge(gate_stored[i], 16 * (NT + 1))
            sp.wait_ge(sem("rms_arg"), NT)
            wmo = a["w_mix_out"][0]

            def load_gate(j, s, c, h):
                u = 4 * s + 2 * c + h
                sp.wait_ge(gated_b, j * 8 + u + 1)
                sp.dma_start(GATE[:, u % 2, :, :], gate_v[:, :, j * 4 + 2 * s + c, h * HALF:(h + 1) * HALF])\
                    .then_inc(gate_in[u % 2], 16)

            for j in range(2):
                for s in range(2):
                    load_dw(D_MIX + 2 * j + s, wmo, (2 * j + s) * 256)
                    for c in range(2):
                        for h in range(2):
                            load_gate(j, s, c, h)
                        if j == 0 and s == 0 and c == 0:
                            sp.wait_ge(feat_lo, 2)
                            sp.wait_ge(scan_lo, 6)
                            sp.wait_ge(x_spilled, 16)
                            sp.dma_start(X[:, :, :], x_scratch).then_inc(x_back, 16)
                    if j == 0:
                        load_branch(S_MIX + 2 + s, (2 + s) * 256)
                    else:
                        load_cols(S_XA + s, rows(a["xa_wq"]), s * 256)
            load_ln("ln2", a["ln2_g"], a["ln2_b"])
            wo = a["xa_wo"][0]
            wg, wu = rows(a["ffn2_w_gate"]), rows(a["ffn2_w_up"])
            for s in range(4):
                kv = kv_scratch[s].rearrange("p v h (c n) -> p v h c n", c=2)
                if s == 0:
                    for b in range(2):
                        sp.wait_ge(kv_stored[b], 16 * 5)
                    sp.wait_ge(ln_scaled, LN_BASE["ln2"] + NT)
                else:
                    sp.wait_ge(s_ready, 8 * s)
                sp.dma_start(KV[:, 0].bitcast(F32), kv[:, 0]).then_inc(keys_in, 16)
                if s == 0:
                    sp.wait_ge(ln_done, LN_BASE["ln2"] + NT)
                else:
                    sp.wait_ge(kvh_used, s + 1)
                sp.dma_start(KV[:, 1].bitcast(F32), kv[:, 1]).then_inc(values_in, 16)
                load_dw(D_XA + s, wo, s * 256)
                if s < 2:
                    load_cols(S_XA + 2 + s, rows(a["xa_wq"]), (2 + s) * 256)
                else:
                    load_gate_up(S_FFN2 + s - 2, wg, wu, (s - 2) * P)
            load_ln("ln3", a["ln3_g"], a["ln3_b"])
            sp.wait_ge(ln_done, LN_BASE["ln3"] + NT)
            ffn_loads(S_FFN2, D_FFN2, wg, wu, a["ffn2_w_down"][0], [])
            load_ln("ln4", a["ln4_g"], a["ln4_b"])
            for t in range(NT):
                sp.wait_ge(ln_done, LN_BASE["ln4"] + t + 1)
                sp.dma_start(out_v[:, t, :], X[:, t, :]).then_inc(out_stored, 16)
            sp.wait_ge(out_stored, 16 * NT)

        @block.tensor
        def _(pe):
            mm = nc.tensor.matmul

            def split_product(out, terms):
                for i, (lh, ll, rh, rl) in enumerate(terms):
                    mm(out, lh, rh, start=(i == 0), stop=False)
                    mm(out, lh, rl, start=False, stop=False)
                    last = mm(out, ll, rh, start=False, stop=(i == len(terms) - 1))
                return last

            def unit(u, par, products, early=False):
                pe.wait_ge(unit_read, u + 1)
                for m, (terms, width) in enumerate(products):
                    last = split_product(PS[:, 2 * par + m, 0:width], terms)
                    if early and m == 0:
                        last.then_inc(first_chunk, 1)
                last.then_inc(unit_ready, 1)

            def feature_terms(s, m, h, ks=range(KD)):
                t = slice(h * HALF, (h + 1) * HALF)
                c = slice(m * P, (m + 1) * P)
                return [(GUh[:, s, k, c], GUl[:, s, k, c], XTh[:, k, t], XTl[:, k, t]) for k in ks]

            def slot_ready(n):
                pe.wait_ge(gu_lo, n + 2)

            def down_tile(t, n, q):
                tok, cs = slice(t * P, (t + 1) * P), slice(n * 512, (n + 1) * 512)
                split_product(PS[:, 4 + q % 4, :], [(HTh[:, c, tok], HTl[:, c, tok], DWh[:, c, cs], DWl[:, c, cs])
                                                    for c in range(2)]).then_inc(tile_ready, 1)

            def down(m, q0, qp, ready):
                pe.wait_ge(dw_lo, m + 2)
                for t in range(NT):
                    if t % 4 == 0:
                        ready(t // 4)
                    for n in range(2):
                        pe.wait_ge(tile_read, q0 + 2 * t + n + 1)
                        down_tile(t, n, qp + 2 * t + n)

            def transposes(name, t, src):
                for g in range(2):
                    q = turned_tile(name, t, g)
                    pe.wait_ge(tile_read, q + 1)
                    for k in range(4):
                        c = 4 * g + k
                        last = nc.tensor.transpose(PS[:, 4 + q % 4, k * P:(k + 1) * P],
                                                   src[:, t, c * P:(c + 1) * P], ident)
                    last.then_inc(tile_ready, 1)

            def turned(name, t):
                pe.wait_ge(tile_read, turned_tile(name, t, 1) + 5)

            def first_unit(par, first, count, early):
                for i in range(first, first + count):
                    m, k, part = i // 24, i % 24 // 3, i % 3
                    c = slice(m * P, (m + 1) * P)
                    ins = mm(PS[:, m, :], (GUh, GUh, GUl)[part][:, par, k, c],
                             (XTh, XTl, XTh)[part][:, k, 0:HALF], start=(i % 24 == 0), stop=(i % 24 == 23))
                    if early and i == 23:
                        ins.then_inc(first_chunk, 1)
                if first + count == 48:
                    ins.then_inc(unit_ready, 1)

            def down_and_norm(m, name, ready, slot=None, u=None):
                pe.wait_ge(dw_lo, m + 2)
                lag = LAG[name]
                share = -(-48 // (lag + 1))
                for i in range(NT + lag):
                    if i < SUMS_BEFORE[name]:
                        continue
                    if i < NT:
                        if i % 4 == 0 or i == SUMS_BEFORE[name]:
                            ready(i // 4)
                        for n in range(2):
                            q = sum_tile(name, i, n)
                            pe.wait_ge(tile_read, q + 1)
                            down_tile(i, n, q)
                    else:
                        if i == NT:
                            slot_ready(slot)
                            turned(name, 3)
                            pe.wait_ge(unit_read, u + 1)
                        first_unit(slot % 2, (i - NT) * share, share, name == "ln2")
                    if slot is not None and i >= lag:
                        pe.wait_ge(ln_done, LN_BASE[name] + i - lag + 1)
                        transposes(name, i - lag, X)
                if slot is not None:
                    first_unit(slot % 2, lag * share, 48 - lag * share, name == "ln2")
                    turned(name, NT - 1)

            def ffn(s0, u0, d0, q0, h0, first_done, name, slot, u):
                def units(j, first):
                    for c in range(2):
                        slot_ready(s0 + 2 * j + c)
                        for h in range(2):
                            i = 2 * c + h
                            if not (first and i == 0):
                                unit(u0 + 4 * j + i, i % 2, [(feature_terms(c, m, h), HALF) for m in range(2)])

                def pair(j, first=False):
                    units(j, first)
                    down(d0 + j, q0 + 16 * j, q0, lambda h: pe.wait_ge(h_lo, h0 + 4 * j + 3 + h + 2))

                pair(0, first_done)
                with pe.Fori(1, PAIRS - 1) as j:
                    pair(j)
                units(PAIRS - 1, False)
                down_and_norm(d0 + PAIRS - 1, name,
                              lambda h: pe.wait_ge(h_lo, h0 + 4 * (PAIRS - 1) + 3 + h + 2), slot, u)

            pe.wait_ge(mask_in, 32)
            for t in range(MT):
                pe.wait_ge(ln_done, LN_BASE["mem"] + t + 1)
                transposes("mem", t, MEMX)
            turned("mem", MT - 1)
            for s in range(8):
                pe.wait_ge(kw_lo, s + 1)
                if s < 4:
                    unit(s, s % 2, [([(GUh[:, s % 2, k, m * P:(m + 1) * P], GUl[:, s % 2, k, m * P:(m + 1) * P],
                                       MTh[:, k, :], MTl[:, k, :]) for k in range(KD)], N_MEM)
                                    for m in range(2)])
                else:
                    unit(s, s % 2, [([(MTh[:, k, m * P:(m + 1) * P], MTl[:, k, m * P:(m + 1) * P],
                                       GUh[:, s % 2, k, :], GUl[:, s % 2, k, :]) for k in range(KD)], XD)
                                    for m in range(2)])
                for t in X_AFTER.get(s, ()):
                    pe.wait_ge(x_in[t // 4], 16)
                    transposes("x", t, X)
            turned("x", NT - 1)
            ffn(S_FFN1, U_FFN1, D_FFN1, Q_FFN1, H_FFN1, False, "ln1", S_P, U_P)

            unit(U_P + 1, 1, [(feature_terms(0, m, 1), HALF) for m in range(2)])
            pe.wait_ge(ab_split, 2)
            for h in range(2):
                q = Q_AB + h
                pe.wait_ge(tile_read, q + 1)
                split_product(PS[0:2 * HEADS, 4 + q % 4, :],
                              [(ABh[:, k, :], ABl[:, k, :], XTh[:, k, h * HALF:(h + 1) * HALF],
                                XTl[:, k, h * HALF:(h + 1) * HALF]) for k in range(KD)]).then_inc(tile_ready, 1)
            pe.wait_ge(sem("ab_rows"), 2)
            q = Q_AB + 2
            pe.wait_ge(tile_read, q + 1)
            for t in range(NT):
                last = nc.tensor.transpose(PS[:, 4 + q % 4, 8 * t:8 * t + 8], ABROWS[:, t * P:(t + 1) * P],
                                           MASK[0:2 * HEADS, M_ID, 0:2 * HEADS])
            last.then_inc(tile_ready, 1)
            slot_ready(S_P + 1)
            for h in range(2):
                unit(U_P + 2 + h, h, [(feature_terms(1, m, h), HALF) for m in range(2)])
            pe.wait_ge(const_in, 16 * 6)
            pe.wait_ge(ab_done, 1)
            g = GT[:, :, G_G, :]
            mm(PS[:, 4, 0:NT * HEADS], MASK[:, M_UP, :], g, start=True, stop=True)
            mm(PS[:, 5, 0:NT * HEADS], MASK[:, M_ONE, :], g, start=True, stop=True).then_inc(sem("cum_ready"), 1)

            def project(n, first_u, count):
                with pe.Fori(0, count) as j:
                    for s in range(2):
                        slot_ready(n + 2 * j + s)
                        for h in range(2):
                            unit(first_u + 4 * j + 2 * s + h, h, [(feature_terms(s, m, h), HALF) for m in range(2)])

            project(S_QKV, U_QKV, 3)

            def z_slot(s):
                slot_ready(S_Z + s)
                for h in range(2):
                    unit(U_Z + 2 * s + h, h, [(feature_terms(s, m, h), HALF) for m in range(2)])

            z_slot(0)
            pe.wait_ge(pool_w_in, 16)
            pe.wait_ge(sem("cum_read"), 1)
            for g in range(GROUPS):
                pe.wait_ge(pooled, g + 1)
                for h in range(2):
                    q = Q_POOL + 2 * g + h
                    pe.wait_ge(tile_read, q + 1)
                    mm(PS[:, 4 + q % 4, :], POOLW[:, g, :], MIXED[:, g, h * HALF:(h + 1) * HALF],
                       start=True, stop=True).then_inc(tile_ready, 1)
            z_slot(1)

            def flip(bank, src, name):
                for h in range(HEADS):
                    last = nc.tensor.transpose(PS[:, bank, h * P:(h + 1) * P], src(h), ident)
                last.then_inc(sem(name), 1)

            def product(bank, lhsT, rhs, name):
                for h in range(HEADS):
                    last = mm(PS[:, bank, h * P:(h + 1) * P], lhsT(h), rhs(h), start=True, stop=True)
                last.then_inc(sem(name), 1)

            of = lambda t: (lambda h: t[:, h, :])

            def delta_step(n, m, par, scan, prep):
                new = 1 - par
                done = [0]

                def fill(count):
                    if not prep:
                        return
                    count = min(count, 96 - done[0])
                    if done[0] == 0:
                        slot_ready(S_GATE + m)
                    for i in range(done[0], done[0] + count):
                        g, k3 = i // 24, i % 24
                        k, part = k3 // 3, k3 % 3
                        if k3 == 0:
                            pe.wait_ge(gp_read, m * 4 + g + 1)
                        c = slice(g // 2 * P, (g // 2 + 1) * P)
                        t = slice(g % 2 * HALF, (g % 2 + 1) * HALF)
                        w = (GUh, GUh, GUl)[part][:, new, k, c]
                        x = (XTh, XTl, XTh)[part][:, k, t]
                        ins = mm(PS[:, g % 2, :], w, x, start=(k3 == 0), stop=(k3 == 23))
                        if k3 == 23:
                            ins.then_inc(gp_ready, 1)
                    done[0] += count

                def of_scan(name):
                    pe.wait_ge(sem(name), n + 1)

                def of_prep(name):
                    pe.wait_ge(sem(name), m + 1)

                if prep:
                    pe.wait_ge(sem("qkv_in"), m * 16 + 16)
                    flip(2, lambda h: QKVS[:, HEADS + h, :], "k_tok")
                    flip(3, lambda h: QKVS[:, h, :], "q_tok")
                    flip(4, lambda h: QKVS[:, 2 * HEADS + h, :], "v_tok")
                    of_prep("scalars")
                    product(5, lambda h: GTN[new][:, G_G, h:h + 1].broadcast_to([P, P]),
                            lambda h: MASK[:, M_UP, :], "cum_rows")
                if scan:
                    pe.wait_ge(sem("state"), n + 1)
                    product(6, of(KT[par]), of(ST), "k_state")
                    product(7, of(QT[par]), of(ST), "q_state")
                fill(8)
                if scan:
                    of_scan("resid")
                    product(6, of(TT[par]), of(R), "v_new_ps")
                fill(8 if scan else 24)
                if scan:
                    of_scan("v_new")
                    if prep:
                        product(6, of(KDEC[par]), of(VN), "kv_outer")
                    of_scan("q_state_dec")
                    product(7, of(ATT[par]), of(VN), "o_intra")
                if prep:
                    of_prep("k_unit")
                    flip(2, of(KN), "kT_ps")
                    of_prep("q_unit")
                    flip(3, of(QN), "qT_ps")
                fill(4)
                if prep:
                    of_prep("kT")
                    of_prep("v0")
                    product(4, of(KT[new]), of(KT[new]), "kk")
                    of_prep("qT")
                    of_prep("dif")
                    product(5, of(KT[new]), of(QT[new]), "qk")
                fill(4)
                if prep:
                    of_prep("low")
                    flip(2, of(L), "lowT_ps")
                    of_prep("inv0")
                    flip(3, of(T), "inv0T_ps")
                if scan:
                    of_scan("o_unit")
                    flip(7, of(ON), "oT_ps")
                fill(4)
                if prep:
                    of_prep("lowT")
                    of_prep("att")
                    for lv in range(LEVELS):
                        b = 2 << lv
                        even = lambda t: t.rearrange("p (c two b) -> p c two b", two=2, b=b)[:, :, 0, :]
                        odd = lambda t: t.rearrange("p (c two b) -> p c two b", two=2, b=b)[:, :, 1, :]
                        if lv:
                            pe.wait_ge(sem("inv"), m * (LEVELS - 1) + lv)
                        for h in range(HEADS):
                            last = mm(PS[:, 4, h * 64:(h + 1) * 64], LT[:, h, :], even(T[:, h, :]),
                                      start=True, stop=True)
                        last.then_inc(sem("lev_m_ps"), 1)
                        fill(4)
                        pe.wait_ge(sem("lev_m"), m * LEVELS + lv + 1)
                        if lv == 0:
                            of_prep("inv0T")
                        for h in range(HEADS):
                            last = mm(PS[:, 5, h * 64:(h + 1) * 64], MM[lv % 2][:, h, :],
                                      odd(TT[new][:, h, :]), start=True, stop=True)
                        last.then_inc(sem("lev_pT"), 1)
                        fill(4)
                        pe.wait_ge(sem("invT"), m * LEVELS + lv + 1)
                        if lv < LEVELS - 1:
                            flip(2, of(TT[new]), "inv_ps")
                            fill(4)
                    fill(96 - done[0])

            pe.wait_ge(unit_read, U_MIX + 2)
            pe.wait_ge(tile_read, Q_MIX + 4)
            delta_step(None, 0, 1, False, True)
            with pe.Fori(0, 3) as j:
                for r in range(2):
                    delta_step(2 * j + r, 2 * j + r + 1, r, True, True)
            delta_step(NT - 2, NT - 1, 0, True, True)
            delta_step(NT - 1, None, 1, True, False)

            pe.wait_ge(gp_read, 4 * NT + 2)
            pe.wait_ge(sem("oT"), NT)
            for s in range(4):
                slot_ready(S_MIX + s)
                for c in range(2):
                    for h in range(2):
                        i = 2 * c + h
                        pe.wait_ge(unit_read, U_MIX + 4 * s + i + 1)
                        if s == 0 and c == 0:
                            pe.wait_ge(feat_lo, 2)
                            pe.wait_ge(scan_lo, 2)
                        split_product(PS[:, 2 * h + 1, :], feature_terms(s % 2, c, h, range(4, 8)))
                        if s == 0 and c == 0:
                            pe.wait_ge(scan_lo, 2 * h + 4)
                        split_product(PS[:, 2 * h, :], feature_terms(s % 2, c, h, range(0, 4)))\
                            .then_inc(unit_ready, 1)
                ready = lambda h: pe.wait_ge(h_lo, H_MIX + 4 * s + 3 + h + 2)
                if s < 3:
                    down(D_MIX + s, Q_MIX + 16 * s, Q_MIX, ready)
                else:
                    down_and_norm(D_MIX + s, "ln2", ready, S_XA, U_XA)

            for s in range(HEADS):
                for kind, i in head_order(s):
                    tok = slice(i * P, (i + 1) * P)
                    if kind == "queries" and i == 0 and s > 0:
                        slot_ready(S_XA + s)
                        unit(U_XA + 4 * s, 0, [(feature_terms(s % 2, m, 0), HALF) for m in range(2)], True)
                    elif kind == "more":
                        if i == 0:
                            pe.wait_ge(unit_read, U_XA + 4 * s + 2)
                        for j in MORE[i]:
                            m, k = j // KD, j % KD
                            c = slice(m * P, (m + 1) * P)
                            for part in range(3):
                                ins = mm(PS[:, 2 + m, :], (GUh, GUh, GUl)[part][:, s % 2, k, c],
                                         (XTh, XTl, XTh)[part][:, k, HALF:], start=(k == 0 and part == 0),
                                         stop=(k == KD - 1 and part == 2))
                            if j == KD - 1:
                                ins.then_inc(first_chunk, 1)
                        if i == len(MORE) - 1:
                            ins.then_inc(unit_ready, 1)
                    elif kind == "scores":
                        if i == 0:
                            pe.wait_ge(keys_in, 16 * (s + 1))
                        if i % 4 == 0:
                            pe.wait_ge(q_lo, 2 * (2 * s + i // 4) + 2)
                        pe.wait_ge(s_read, 8 * s + i + 1)
                        split_product(PS[:, 4, 0:N_MEM],
                                      [(HTh[:, c, tok], HTl[:, c, tok], KV[:, 0, 0, c, :], KV[:, 0, 1, c, :])
                                       for c in range(2)]).then_inc(s_ready, 1)
                    elif kind == "turn":
                        pe.wait_ge(p_norm, 8 * s + i + 1)
                        pe.wait_ge(pt_lo, 8 * s + i + 1)
                        for m in range(MT):
                            last = nc.tensor.transpose(PS[:, 5, m * P:(m + 1) * P],
                                                       PR[:, i % 4, m * P:(m + 1) * P], ident)
                        last.then_inc(pt_ready, 1)
                    elif kind == "output":
                        pe.wait_ge(pt_lo, 8 * s + 4 * i + 4 + 1)
                        if i == 0:
                            pe.wait_ge(values_in, 16 * (s + 1))
                        unit(U_XA + 4 * s + 2 + i, i,
                             [([(KV[:, 1, 0, m, c * P:(c + 1) * P], KV[:, 1, 1, m, c * P:(c + 1) * P],
                                 PTh[:, m, :], PTl[:, m, :]) for m in range(MT)], HALF) for c in range(2)], True)
                    elif kind == "sum":
                        if i == 0:
                            pe.wait_ge(dw_lo, D_XA + s + 2)
                        if i % 8 == 0:
                            pe.wait_ge(o_lo, 2 * (2 * s + i // 8) + 2)
                        q = Q_XA + 16 * s + i
                        pe.wait_ge(tile_read, q + 3)
                        down_tile(i // 2, i % 2, 2 + q % 2)
            pe.wait_ge(tile_read, Q_XA + 16 * 3 + 2 * SUMS_BEFORE["ln3"] + 4)
            pe.wait_ge(pt_lo, 8 * HEADS + 1)
            down_and_norm(D_XA + 3, "ln3", lambda h: pe.wait_ge(o_lo, 2 * (2 * 3 + h) + 2), S_FFN2, U_FFN2)
            ffn(S_FFN2, U_FFN2, D_FFN2, Q_FFN2, H_FFN2, True, "ln4", None, None)

        @block.scalar
        def _(act):
            op = nc.scalar.activation

            def split_gu(n, par):
                act.wait_ge(gu_in, n * 32 + 32)
                op(GUh[:, par, :, :], GUraw[:, :, :], ACT.Copy).then_inc(gu_hi, 1)

            def split_dw(m, q):
                act.wait_ge(dw_in, m * 32 + 32)
                act.wait_ge(tile_ready, q)
                op(DWh[:, :, :], DWraw[:, :, :], ACT.Copy).then_inc(dw_hi, 1)

            def unit_wait(u):
                act.wait_ge(unit_ready, u + 1)

            def transposed_hi(name, t, dst):
                for g in range(2):
                    q = turned_tile(name, t, g)
                    act.wait_ge(tile_ready, q + 1)
                    op(dst[:, 4 * g:4 * g + 4, t * P:(t + 1) * P],
                       PS[:, 4 + q % 4, :].rearrange("p (k t) -> p k t", k=4), ACT.Copy).then_inc(xt_hi, 1)

            def normalise(name, t, x):
                act.wait_ge(ln_scaled, LN_BASE[name] + t + 1)
                act.wait_ge(ln_rstd, LN_BASE[name] + t + 1)
                op(x[:, t, :], x[:, t, :], ACT.Copy, scale=RSTD[:, t:t + 1]).then_inc(ln_hat, 1)

            def layer_norm(name):
                last = name == "ln4"
                for i in range(NT + LAG[name]):
                    if i >= LAG[name] and not last:
                        transposed_hi(name, i - LAG[name], XTh)
                    if i < NT:
                        normalise(name, i, X)

            def ffn(s0, u0, d0, q0, h0, last_phase):
                def pair(j, more):
                    split_dw(d0 + j, q0 + 16 * j)
                    for c in range(2):
                        for h in range(2):
                            i = 2 * c + h
                            u = u0 + 4 * j + i
                            unit_wait(u)
                            op(SIG[:, i % 2, :], PS[:, 2 * (i % 2), :], ACT.Silu).then_inc(act_out, 1)
                            act.wait_ge(unit_read, u + 3)
                            op(HTh[:, c, h * HALF:(h + 1) * HALF], H32[:, i % 2, :], ACT.Copy).then_inc(h_hi, 1)
                        if more:
                            split_gu(s0 + 2 + 2 * j + c, c)
                if last_phase:
                    with act.Fori(0, PAIRS - 1) as j:
                        pair(j, True)
                    pair(PAIRS - 1, False)
                else:
                    with act.Fori(0, PAIRS) as j:
                        pair(j, True)

            def split_kv_weights(n):
                act.wait_ge(kw_in[n % 4], 32 * (n // 4 + 1))
                op(GUh[:, n % 2, :, :], KW[n % 4][:, :, :], ACT.Copy).then_inc(kw_hi, 1)

            def store_kv(s):
                act.wait_ge(kv_lo, s + 1)
                act.dma_start(kv_scratch[s % 4, :, s // 4, :, :], KVO[:, s % 2, :, :].bitcast(F32))\
                    .then_inc(kv_stored[s % 2], 16)

            for t in range(MT):
                normalise("mem", t, MEMX)
            split_kv_weights(0)
            for t in range(MT):
                transposed_hi("mem", t, MTh)
            split_kv_weights(1)
            for s in range(8):
                unit_wait(s)
                if s + 2 < 8:
                    split_kv_weights(s + 2)
                else:
                    split_gu(S_FFN1 + s - 6, s % 2)
                if s:
                    store_kv(s - 1)
                act.wait_ge(kv_stored[s % 2], 16 * (s // 2 + 1))
                v = KVO[:, s % 2, 0, :].rearrange("p (c n) -> p c n", c=2)
                op(v, PS[:, 2 * (s % 2):2 * (s % 2) + 2, 0:256], ACT.Copy).then_inc(kv_hi, 1)
                for t in X_AFTER.get(s, ()):
                    transposed_hi("x", t, XTh)
            store_kv(7)
            for b in range(2):
                act.wait_ge(kv_stored[b], 16 * 5)
            ffn(S_FFN1, U_FFN1, D_FFN1, Q_FFN1, H_FFN1, False)
            layer_norm("ln1")

            def raw_frames(dst, h, u):
                act.wait_ge(unit_ready, u + 1)
                op(dst[:, :, HALO + h * HALF:HALO + (h + 1) * HALF], PS[:, 2 * h:2 * h + 2, :], ACT.Copy)\
                    .then_inc(unit_read, 1)

            act.wait_ge(const_in, 16 * 6)
            act.wait_ge(ab_in, 16)
            op(ABh[:, :, :], ABRAW[:, :, :], ACT.Copy).then_inc(ab_split, 1)
            for h in range(2):
                raw_frames(RAWP, h, U_P + h)
            split_gu(S_P + 2, 0)
            act.wait_ge(sem("ab_sum"), 1)
            op(GT[:, :, G_BETA, :], ABT[:, :, HEADS:], ACT.Sigmoid).then_inc(sem("beta"), 1)
            op(AB2[:, :, :], AB1[:, :, :], ACT.Abs).then_inc(sem("ab_abs"), 1)
            act.wait_ge(sem("ab_abs"), 1)
            op(AB2[:, :, :], AB2[:, :, :], ACT.Exp, scale=-1.0).then_inc(sem("ab_abs"), 1)
            op(AB4[:, :], HPAR[:, 1, :], ACT.Exp).then_inc(sem("a_exp"), 1)
            act.wait_ge(sem("ab_abs"), 2)
            op(AB2[:, :, :], AB2[:, :, :], ACT.Ln, bias=1.0).then_inc(sem("ab_ln"), 1)
            act.wait_ge(pooled, 2)
            for h in range(2):
                raw_frames(RAWP, h, U_P + 2 + h)
            split_gu(S_P + 3, 1)
            act.wait_ge(sem("cum_read"), 1)
            op(GT[:, :, G_ECUM:G_ELAST + 1, :], GT[:, :, G_ECUM:G_ELAST + 1, :], ACT.Exp).then_inc(sem("g_exp"), 1)

            def store(j, par, chunks, h):
                act.wait_ge(cout_done, j + 3)
                act.dma_start(chunks[:, :, h * HALF:(h + 1) * HALF], COUT[:, par, :, :]).then_inc(stored[par], 16)

            with act.Fori(0, 3) as j:
                for s in range(2):
                    for h in range(2):
                        v = 4 * j + 2 * s + h
                        act.wait_ge(conv_done, v + 1)
                        raw_frames(RAW, h, v + U_QKV)
                        act.wait_ge(conv_done, v + 2)
                        act.wait_ge(stored[h], j * 32 + 16 * s + 16)
                        op(COUT[:, h, :, :], CACC[:, h, :, :], ACT.Silu).then_inc(cout_done, 1)
                        store(v, h, proj_v[:, bass.ds(4 * j + 2 * s, 2), :], h)
                    split_gu(S_QKV + 2 + 2 * j + s, s)
            def pooling_out():
                act.wait_ge(x_spilled, 16)
                for g in range(GROUPS):
                    for h in range(2):
                        q = Q_POOL + 2 * g + h
                        act.wait_ge(tile_ready, q + 1)
                        op(FEAT[:, 4 + g, h * HALF:(h + 1) * HALF], PS[:, 4 + q % 4, :], ACT.Copy,
                           scale=PSCALE[:, g:g + 1]).then_inc(tile_read, 1)

            for s in range(2):
                for h in range(2):
                    v = 12 + 2 * s + h
                    act.wait_ge(unit_ready, v + U_QKV + 1)
                    act.wait_ge(stored[h], 16 * (v // 2 + 1))
                    op(COUT[:, h, :, :], PS[:, 2 * h:2 * h + 2, :], ACT.Silu).then_inc(cout_done, 1)
                    act.wait_ge(cout_done, v + 3)
                    act.sem_inc(unit_read, 1)
                    store(v, h, proj_v[:, CH_Z + 2 * s:CH_Z + 2 * s + 2, :], h)
                if s == 0:
                    split_gu(S_GATE, 0)
                    pooling_out()

            def copy(dst, bank, name):
                op(dst[:, :, :], PS[:, bank, :].rearrange("p (h t) -> p h t", h=HEADS), ACT.Copy)\
                    .then_inc(sem(name), 1)

            def delta_step(n, m, par, scan, prep):
                new = 1 - par

                def of_scan(name):
                    act.wait_ge(sem(name), n + 1)

                def of_prep(name):
                    act.wait_ge(sem(name), m + 1)

                def gate(g):
                    act.wait_ge(gp_ready, m * 4 + g + 1)
                    act.wait_ge(gate_stored[g], m * 16 + 16)
                    op(GOUT[:, g, :], PS[:, g % 2, :], ACT.Sigmoid).then_inc(gp_read, 1)
                    act.wait_ge(gp_read, m * 4 + g + 3)
                    dst = proj_scratch[bass.ds(m * 2 + CH_GDN + g // 2, 1), :, g % 2 * HALF:(g % 2 + 1) * HALF]
                    act.dma_start(dst.rearrange("c p t -> p (c t)"), GOUT[:, g, :]).then_inc(gate_stored[g], 16)

                if prep:
                    for src, dst, bank, name in (("k_tok", K0, 2, "k0"), ("q_tok", Q0, 3, "q0"),
                                                 ("v_tok", V0, 4, "v0")):
                        of_prep(src)
                        copy(dst, bank, name)
                if scan:
                    of_scan("q_state")
                    for h in range(HEADS):
                        last = op(QS[:, h, :], PS[:, 7, h * P:(h + 1) * P], ACT.Copy,
                                  scale=GTN[par][:, G_ECUM, h:h + 1])
                    last.then_inc(sem("q_state_dec"), 1)
                    of_scan("v_new_ps")
                    copy(VN, 6, "v_new")
                if prep:
                    of_prep("dif_pos")
                    op(E1[:, :, :], E1[:, :, :], ACT.Exp, scale=-1.0).then_inc(sem("decay"), 1)
                    of_prep("dif_neg")
                    op(E2[:, :, :], E2[:, :, :], ACT.Exp).then_inc(sem("decayT"), 1)
                    of_prep("kT_ps")
                    copy(KT[new], 2, "kT")
                    of_prep("qT_ps")
                    copy(QT[new], 3, "qT")
                    split_gu(S_GATE + 1 + m, par)
                    gate(0)
                    of_prep("lowT_ps")
                    copy(LT, 2, "lowT")
                    of_prep("inv0T_ps")
                    copy(TT[new], 3, "inv0T")
                    for lv in range(LEVELS - 1):
                        act.wait_ge(sem("inv_ps"), m * (LEVELS - 1) + lv + 1)
                        copy(T, 2, "inv")
                        if lv % 2:
                            gate(lv // 2 + 1)
                    gate(3)
                else:
                    for g in range(GROUPS):
                        op(XTh[:, 4 + g, :], FEAT[:, 4 + g, :], ACT.Copy).then_inc(feat_hi, 1)

            for b in range(2):
                act.wait_ge(stored[b], 16 * 9)
            delta_step(None, 0, 1, False, True)
            with act.Fori(0, 3) as j:
                for r in range(2):
                    delta_step(2 * j + r, 2 * j + r + 1, r, True, True)
            delta_step(NT - 2, NT - 1, 0, True, True)
            delta_step(NT - 1, None, 1, True, False)
            act.wait_ge(sem("oT"), NT)
            for h in range(2):
                for k in range(0, 4, 2):
                    to = (slice(None), slice(k, k + 2), slice(h * HALF, (h + 1) * HALF))
                    op(XTh[to], FEAT[to], ACT.Copy).then_inc(feat_hi, 1)
            split_gu(S_MIX + 1, 1)

            for s in range(4):
                split_dw(D_MIX + s, Q_MIX + 16 * s)
                for i in range(4):
                    u = U_MIX + 4 * s + i
                    unit_wait(u)
                    act.wait_ge(sem("merged"), 4 * s + i + 1)
                    op(HTh[:, i // 2, i % 2 * HALF:(i % 2 + 1) * HALF], H32[:, i % 2, :], ACT.Copy)\
                        .then_inc(h_hi, 1)
                split_gu(S_MIX + 2 + s, s % 2)
            layer_norm("ln2")

            def rounded(s, number, i, hi, scale):
                for c in range(2):
                    if c == 0:
                        act.wait_ge(first_chunk, 4 * s + number + 1)
                    else:
                        unit_wait(U_XA + 4 * s + number)
                    op(HTh[:, c, i * HALF:(i + 1) * HALF], PS[:, 2 * i + c, :], ACT.Copy, scale=scale)\
                        .then_inc(hi, 1)

            for s in range(HEADS):
                split_dw(D_XA + s, Q_XA + 16 * s)
                for kind, i in head_order(s):
                    if kind == "queries":
                        rounded(s, i, i, q_hi, XD ** -0.5)
                    elif kind == "scores":
                        act.wait_ge(neg_max, 8 * s + i + 1)
                        if 8 * s + i >= 4:
                            act.wait_ge(pt_ready, 8 * s + i - 3)
                        op(PR[:, i % 4, :], PS[:, 4, 0:N_MEM], ACT.Exp, bias=NEGMAX[:, i:i + 1],
                           accum_out=RSUM[:, i:i + 1]).then_inc(s_read, 1)
                    elif kind == "turn":
                        act.wait_ge(pt_ready, 8 * s + i + 1)
                        op(PTh[:, :, i % 4 * P:(i % 4 + 1) * P],
                           PS[:, 5, 0:N_MEM].rearrange("p (m t) -> p m t", m=MT), ACT.Copy).then_inc(pt_hi, 1)
                    elif kind == "output":
                        if i == 0:
                            split_gu(S_XA + 2 + s, s % 2)
                        rounded(s, 2 + i, i, o_hi, 1.0)
            layer_norm("ln3")
            ffn(S_FFN2, U_FFN2, D_FFN2, Q_FFN2, H_FFN2, True)
            layer_norm("ln4")

        @block.gpsimd
        def _(pool):
            tt = nc.gpsimd.tensor_tensor

            def split_gu(n, par):
                pool.wait_ge(gu_hi, n + 1)
                tt(GUl[:, par, :, :], GUraw[:, :, :], GUh[:, par, :, :].bitcast(F32), ALU.subtract)\
                    .then_inc(gu_lo, 1)

            def split_dw(m):
                pool.wait_ge(dw_hi, m + 1)
                tt(DWl[:, :, :], DWraw[:, :, :], DWh[:, :, :].bitcast(F32), ALU.subtract).then_inc(dw_lo, 1)

            def split_half(v, i):
                pool.wait_ge(h_hi, v + 1)
                to = (slice(None), i // 2, slice(i % 2 * HALF, (i % 2 + 1) * HALF))
                tt(HTl[to], H32[:, i % 2, :], HTh[to].bitcast(F32), ALU.subtract).then_inc(h_lo, 1)

            def rstd(name, t):
                pool.wait_ge(ln_var, LN_BASE[name] + t + 1)
                tt(RSTD[:, t:t + 1], VE[:, t:t + 1], COUNT[:, HALO:HALO + 1], ALU.pow).then_inc(ln_rstd, 1)

            def add_beta(name, t):
                pool.wait_ge(ln_hat, LN_BASE[name] + t + 1)
                tt(X[:, t, :], X[:, t, :], beta(name), ALU.add).then_inc(ln_done, 1)

            def layer_norm(name):
                for t in range(NT + 1):
                    if t < NT:
                        rstd(name, t)
                    if t == 1:
                        pool.wait_ge(beta_in, 16 * (LN_ORDER[name] + 1))
                    if t:
                        add_beta(name, t - 1)

            def ffn(s0, d0, h0, last_phase):
                def pair(j, more):
                    split_dw(d0 + j)
                    for c in range(2):
                        for h in range(2):
                            split_half(h0 + 4 * j + 2 * c + h, 2 * c + h)
                        if more:
                            split_gu(s0 + 2 + 2 * j + c, c)
                if last_phase:
                    with pool.Fori(0, PAIRS - 1) as j:
                        pair(j, True)
                    pair(PAIRS - 1, False)
                else:
                    with pool.Fori(0, PAIRS) as j:
                        pair(j, True)

            pool.sem_inc(gu_lo, 1)
            pool.sem_inc(dw_lo, 1)
            pool.sem_inc(h_lo, 2)
            pool.sem_inc(gp_read, 2)
            for i in range(4):
                pool.sem_inc(gate_stored[i], 16)
            pool.wait_ge(mask_in, 32)
            for t in range(MT):
                rstd("mem", t)
            for n in range(2):
                split_gu(S_FFN1 + n, n)
            ffn(S_FFN1, D_FFN1, H_FFN1, False)
            layer_norm("ln1")
            pool.wait_ge(ab_split, 1)
            tt(ABl[:, :, :], ABRAW[:, :, :], ABh[:, :, :].bitcast(F32), ALU.subtract).then_inc(ab_split, 1)
            with pool.Fori(0, (S_Z - S_P) // 2) as j:
                for s in range(2):
                    split_gu(S_P + 2 + 2 * j + s, s)
            split_gu(S_GATE, 0)

            def pooling_lo(g):
                pool.wait_ge(feat_hi, g + 1)
                tt(XTl[:, 4 + g, :], FEAT[:, 4 + g, :], XTh[:, 4 + g, :].bitcast(F32), ALU.subtract)\
                    .then_inc(feat_lo, 1)

            def delta_step(n, m, par, scan, prep):
                new = 1 - par

                def of_scan(name):
                    pool.wait_ge(sem(name), n + 1)

                def of_prep(name):
                    pool.wait_ge(sem(name), m + 1)

                over = lambda kind: GTN[new][:, kind, :].unsqueeze(2).broadcast_to([P, HEADS, P])
                mask = lambda i: MASK[:, i, :].unsqueeze(1).broadcast_to([P, HEADS, P])
                if prep:
                    of_prep("norm_arg")
                    tt(RN[:, :, :], SS[:, 0:2, :], COUNT[:, HALO:HALO + 8].rearrange("p (a h) -> p a h", a=2),
                       ALU.pow).then_inc(sem("norm_inv"), 1)
                    of_prep("v0")
                    tt(VB[new][:, :, :], V0[:, :, :], over(G_BETA), ALU.mult).then_inc(sem("v_beta"), 1)
                    of_prep("decay")
                    tt(E1[:, :, :], E1[:, :, :], mask(M_LOW), ALU.mult).then_inc(sem("decay_low"), 1)
                    of_prep("decay_low")
                    tt(E1[:, :, :], E1[:, :, :], over(G_BETA), ALU.mult).then_inc(sem("decay_beta"), 1)
                if scan:
                    if not prep:
                        pooling_lo(0)
                    of_scan("rms_arg")
                    tt(RNO[:, :], SSO[:, 1, :], COUNT[:, HALO:HALO + HEADS], ALU.pow).then_inc(sem("rms_inv"), 1)
                if prep:
                    of_prep("decayT")
                    tt(E2[:, :, :], E2[:, :, :], mask(M_UP), ALU.mult).then_inc(sem("decayT_up"), 1)
                    of_prep("k_unit")
                    tt(KDEC[new][:, :, :], KN[:, :, :], over(G_ETAIL), ALU.mult).then_inc(sem("k_dec"), 1)
                    for lv in range(LEVELS):
                        if lv >= 2:
                            pool.wait_ge(sem("lev_pT"), m * LEVELS + lv - 1)
                        tt(MM[lv % 2][:, :, :], mask(M_ID), mask(M_ID), ALU.subtract).then_inc(sem("mm_zero"), 1)
                        if lv == 1:
                            split_gu(S_GATE + 1 + m, par)
                else:
                    pooling_lo(1)
                    split_gu(S_MIX + 1, 1)

            delta_step(None, 0, 1, False, True)
            with pool.Fori(0, 3) as j:
                for r in range(2):
                    delta_step(2 * j + r, 2 * j + r + 1, r, True, True)
            delta_step(NT - 2, NT - 1, 0, True, True)
            delta_step(NT - 1, None, 1, True, False)

            for s in range(4):
                split_dw(D_MIX + s)
                for i in range(4):
                    v = 4 * s + i
                    pool.wait_ge(gated_b, v + 3)
                    tt(H32[:, i % 2, :], H32[:, i % 2, :], SIG[:, i % 2, :], ALU.add).then_inc(sem("merged"), 1)
                    split_half(H_MIX + v, i)
                split_gu(S_MIX + 2 + s, s % 2)
            layer_norm("ln2")
            for s in range(4):
                split_dw(D_XA + s)
                split_gu(S_XA + 2 + s, s % 2)
            layer_norm("ln3")
            ffn(S_FFN2, D_FFN2, H_FFN2, True)
            layer_norm("ln4")

        @block.vector
        def _(dve):
            v = nc.vector

            steps = [0]

            def chain(ins):
                steps[0] += 1
                ins.then_inc(small_step, 1)
                dve.wait_ge(small_step, steps[0])

            def stats(name, t, x, between):
                b = LN_BASE[name] + t
                for i in range(2):
                    if x is X:
                        dve.wait_ge(tile_read, sum_tile(name, t, i) + 5)
                    v.bn_stats(BNS[:, t % 2, i, :], x[:, t, i * 512:(i + 1) * 512]).then_inc(bn_step, 1)
                between(0)
                dve.wait_ge(bn_step, 2 * b + 2)
                v.bn_aggr(MV[:, t, :], BNS[:, t % 2, :, :]).then_inc(ln_mean, 1)
                between(1)
                dve.wait_ge(ln_mean, b + 1)
                v.tensor_scalar(VE[:, t:t + 1], MV[:, t, 1:2], LN_EPS, None, ALU.add).then_inc(ln_var, 1)
                if t == 0:
                    dve.wait_ge(gamma_in, 16 * (LN_ORDER[name] + 1))
                v.scalar_tensor_tensor(x[:, t, :], x[:, t, :], MV[:, t, 0:1], gamma(name), ALU.subtract, ALU.mult)\
                    .then_inc(ln_scaled, 1)

            def transposed_lo(name, t, g, dst_h, dst_l):
                q = turned_tile(name, t, g)
                dve.wait_ge(xt_hi, XT_BASE[name] + 2 * t + g + 1)
                to = (slice(None), slice(4 * g, 4 * g + 4), slice(t * P, (t + 1) * P))
                v.tensor_tensor(dst_l[to], PS[:, 4 + q % 4, :].rearrange("p (k t) -> p k t", k=4),
                                dst_h[to].bitcast(F32), ALU.subtract).then_inc(tile_read, 1)

            def add_and_norm(name):
                last = name == "ln4"

                def turned_lo(t, g):
                    if t >= 0 and not last:
                        transposed_lo(name, t, g, XTh, XTl)

                lag = LAG[name]
                for i in range(STATS_BEFORE[name], NT + lag):
                    if i < NT:
                        for n in range(2 if i >= SUMS_BEFORE[name] else 0):
                            q = sum_tile(name, i, n)
                            dve.wait_ge(tile_ready, q + 1)
                            c = slice(n * 512, (n + 1) * 512)
                            v.tensor_tensor(X[:, i, c], X[:, i, c], PS[:, 4 + q % 4, :], ALU.add)\
                                .then_inc(tile_read, 1)
                        stats(name, i, X, lambda g: turned_lo(i - lag, g))
                    else:
                        for g in range(2):
                            turned_lo(i - lag, g)

            def residual_add(q0, qp, first=False):
                i = 0
                for t in range(NT):
                    for n in range(2):
                        dve.wait_ge(tile_ready, q0 + i + 1)
                        c = slice(n * 512, (n + 1) * 512)
                        if first:
                            ins = v.scalar_tensor_tensor(X[:, t, c], X[:, t, c], ALPHA, PS[:, 4 + (qp + i) % 4, :],
                                                         ALU.mult, ALU.add)
                        else:
                            ins = v.tensor_tensor(X[:, t, c], X[:, t, c], PS[:, 4 + (qp + i) % 4, :], ALU.add)
                        ins.then_inc(tile_read, 1)
                        i += 1

            def ffn(u0, q0, h0, name):
                def units(j):
                    for i in range(4):
                        dve.wait_ge(act_out, j * 4 + (h0 if h0 == 0 else 4 * PAIRS) + i + 1)
                        dve.wait_ge(h_lo, j * 4 + h0 + i + 1)
                        v.scalar_tensor_tensor(H32[:, i % 2, :], SIG[:, i % 2, :], 0.5,
                                               PS[:, 2 * (i % 2) + 1, :], ALU.mult, ALU.mult)\
                            .then_inc(unit_read, 1)

                units(0)
                residual_add(q0, q0, True)
                with dve.Fori(1, PAIRS - 1) as j:
                    units(j)
                    residual_add(q0 + 16 * j, q0)
                units(PAIRS - 1)
                add_and_norm(name)

            dve.sem_inc(unit_read, 2)
            dve.sem_inc(tile_read, 4)
            dve.sem_inc(kv_stored[0], 16)
            dve.sem_inc(kv_stored[1], 16)
            dve.sem_inc(stored[0], 16)
            dve.sem_inc(stored[1], 16)
            dve.sem_inc(conv_done, 1)
            dve.sem_inc(cout_done, 2)
            dve.sem_inc(gated_b, 2)
            dve.sem_inc(kvh_used, 1)
            dve.sem_inc(s_read, 1)
            dve.sem_inc(pt_lo, 1)

            for t in range(MT):
                dve.wait_ge(mem_in[t], 16)
                stats("mem", t, MEMX, lambda g: None)

            def split_kv_weights(n):
                dve.wait_ge(kw_hi, n + 1)
                v.tensor_tensor(GUl[:, n % 2, :, :], KW[n % 4][:, :, :], GUh[:, n % 2, :, :].bitcast(F32),
                                ALU.subtract).then_inc(kw_lo, 1)

            dve.wait_ge(beta_in, 16)
            for t in range(MT):
                dve.wait_ge(ln_hat, t + 1)
                v.tensor_tensor(MEMX[:, t, :], MEMX[:, t, :], LNB[:, :], ALU.add).then_inc(ln_done, 1)
            split_kv_weights(0)
            for t in range(MT):
                for g in range(2):
                    transposed_lo("mem", t, g, MTh, MTl)
            split_kv_weights(1)
            for s in range(8):
                if s + 2 < 8:
                    split_kv_weights(s + 2)
                dve.wait_ge(kv_hi, s + 1)
                r = lambda i: KVO[:, s % 2, i, :].rearrange("p (c n) -> p c n", c=2)
                v.tensor_tensor(r(1), PS[:, 2 * (s % 2):2 * (s % 2) + 2, 0:256], r(0).bitcast(F32),
                                ALU.subtract).then_inc(kv_lo, 1)
                dve.wait_ge(kv_lo, s + 1)
                dve.sem_inc(unit_read, 1)
                for t in X_AFTER.get(s, ()):
                    for g in range(2):
                        transposed_lo("x", t, g, XTh, XTl)
            ffn(U_FFN1, Q_FFN1, H_FFN1, "ln1")

            dve.wait_ge(const_in, 16 * 6)
            for h in range(2):
                q = Q_AB + h
                dve.wait_ge(tile_ready, q + 1)
                v.tensor_copy(ABROWS[:, h * HALF:(h + 1) * HALF], PS[0:2 * HEADS, 4 + q % 4, :])\
                    .then_inc(tile_read, 1)
                dve.wait_ge(tile_read, q + 5)
                dve.sem_inc(sem("ab_rows"), 1)
            q = Q_AB + 2
            dve.wait_ge(tile_ready, q + 1)
            v.tensor_copy(ABT[:, :, :], PS[:, 4 + q % 4, 0:8 * NT].rearrange("p (t c) -> p t c", t=NT))\
                .then_inc(tile_read, 1)
            dve.wait_ge(tile_read, q + 5)
            v.tensor_tensor(AB1[:, :, :], ABT[:, :, 0:HEADS],
                            HPAR[:, 0, :].unsqueeze(1).broadcast_to([P, NT, HEADS]), ALU.add)\
                .then_inc(sem("ab_sum"), 1)
            dve.wait_ge(sem("ab_sum"), 1)
            chain(v.tensor_scalar(AB3[:, :, :], AB1[:, :, :], 0.0, None, ALU.max))
            dve.wait_ge(sem("ab_ln"), 1)
            chain(v.tensor_tensor(AB3[:, :, :], AB3[:, :, :], AB2[:, :, :], ALU.add))
            dve.wait_ge(sem("a_exp"), 1)
            v.scalar_tensor_tensor(GT[:, :, G_G, :], AB3[:, :, :], -1.0,
                                   AB4[:, :].unsqueeze(1).broadcast_to([P, NT, HEADS]), ALU.mult, ALU.mult)\
                .then_inc(ab_done, 1)

            def pool_group(g):
                if g % 2 == 0:
                    dve.wait_ge(unit_read, U_P + g + 2 + 2)
                src = RAWP[:, g % 2]
                for i in range(g + 1):
                    dst = WSUM[i % 2]
                    lag = 1 << i
                    chain(v.tensor_tensor(dst[:, HALO:], src[:, HALO:], src[:, HALO - lag:HALO + SEQ - lag],
                                          ALU.add))
                    src = dst
                win = 2 << g
                frame = RAWP[:, g % 2, HALO:]
                chain(v.scalar_tensor_tensor(MIXED[:, g, :], src[:, HALO:], 1.0 / win, frame, ALU.mult,
                                             ALU.subtract))
                chain(v.tensor_tensor(MIXED[:, g, 0:win], src[:, HALO:HALO + win], COUNT[:, 0:win], ALU.mult))
                v.tensor_tensor(MIXED[:, g, 0:win], MIXED[:, g, 0:win], frame[:, 0:win], ALU.subtract)\
                    .then_inc(pooled, 1)
            chain(v.memset(RAW[:, :, 0:HALO], 0.0))
            chain(v.memset(RAWP[:, :, 0:HALO], 0.0))
            for i in range(2):
                chain(v.memset(WSUM[i][:, 0:HALO], 0.0))
            for g in range(2):
                pool_group(g)
            dve.wait_ge(sem("cum_ready"), 1)
            cum = PS[:, 4, 0:NT * HEADS].rearrange("p (t h) -> p t h", h=HEADS)
            total = PS[:, 5, 0:NT * HEADS].rearrange("p (t h) -> p t h", h=HEADS)
            chain(v.tensor_copy(GT[:, :, G_CUM, :], cum))
            v.tensor_copy(GT[:, :, G_ECUM, :], cum)
            v.tensor_tensor(GT[:, :, G_ETAIL, :], total, GT[:, :, G_CUM, :], ALU.subtract)
            v.tensor_copy(GT[:, :, G_ELAST, :], total).then_inc(sem("cum_read"), 1)
            dve.wait_ge(sem("g_exp"), 1)
            dve.wait_ge(sem("beta"), 1)
            chain(v.scalar_tensor_tensor(GT[:, :, G_NBE, :], GT[:, :, G_BETA, :], -1.0, GT[:, :, G_ECUM, :],
                                         ALU.mult, ALU.mult))

            for g in range(2, GROUPS):
                pool_group(g)
            with dve.Fori(0, 3) as j:
                for s in range(2):
                    for h in range(2):
                        w = 4 * j + 2 * s + h
                        dve.wait_ge(unit_read, w + U_QKV + 3)
                        dve.wait_ge(cout_done, w + 1)
                        for k in range(CONV_K):
                            if k:
                                dve.wait_ge(tap, w * (2 * CONV_K - 2) + 2 * k)
                            for c in range(2):
                                src = RAW[:, c, HALO - CONV_K + 1 + k + h * HALF:HALO - CONV_K + 1 + k + (h + 1) * HALF]
                                wt = CONVW[:, bass.ds(4 * j + 2 * s + c, 1), k]
                                if k == 0:
                                    ins = v.tensor_scalar(CACC[:, h, c, :], src, wt, None, ALU.mult)
                                else:
                                    ins = v.scalar_tensor_tensor(CACC[:, h, c, :], src, wt, CACC[:, h, c, :],
                                                                 ALU.mult, ALU.add)
                                if k < CONV_K - 1:
                                    ins.then_inc(tap, 1)
                        ins.then_inc(conv_done, 1)
            dve.wait_ge(tile_read, Q_MIX + 4)
            v.memset(ST[:, :, :], 0.0).then_inc(sem("state"), 1)

            def pooling_lo(g):
                dve.wait_ge(feat_hi, g + 1)
                v.tensor_tensor(XTl[:, 4 + g, :], FEAT[:, 4 + g, :], XTh[:, 4 + g, :].bitcast(F32), ALU.subtract)\
                    .then_inc(scan_lo, 1)

            def delta_step(n, m, par, scan, prep):
                new = 1 - par

                def of_scan(name):
                    dve.wait_ge(sem(name), n + 1)

                def of_prep(name):
                    dve.wait_ge(sem(name), m + 1)

                def bank(b):
                    return PS[:, b, :].rearrange("p (h t) -> p h t", h=HEADS)

                def signal(ins, name):
                    ins.then_inc(sem(name), 1)

                over = lambda t: t.unsqueeze(2).broadcast_to([P, HEADS, P])
                mask = lambda i: MASK[:, i, :].unsqueeze(1).broadcast_to([P, HEADS, P])
                if prep:
                    signal(v.tensor_copy(GTN[new][:, :, :], GT[:, bass.ds(m, 1), :, :].squeeze(1)), "scalars")
                    of_prep("k0")
                    signal(v.tensor_tensor(SQ[:, :, :], K0[:, :, :], K0[:, :, :], ALU.mult), "k_sq")
                    of_prep("q0")
                    signal(v.tensor_tensor(SQ2[:, :, :], Q0[:, :, :], Q0[:, :, :], ALU.mult), "q_sq")
                    of_prep("k_sq")
                    signal(v.tensor_reduce(SS[:, 2, :], SQ[:, :, :], AX.X, ALU.add), "k_ss")
                    of_prep("q_sq")
                    signal(v.tensor_reduce(SS[:, 3, :], SQ2[:, :, :], AX.X, ALU.add), "q_ss")
                    of_prep("k_ss")
                    v.tensor_scalar(SS[:, 0, :], SS[:, 2, :], 1.0, L2_EPS, ALU.mult, ALU.add)
                    of_prep("q_ss")
                    signal(v.tensor_scalar(SS[:, 1, :], SS[:, 3, :], float(HD), HD * L2_EPS, ALU.mult, ALU.add),
                           "norm_arg")
                if scan:
                    of_scan("k_state")
                    of_scan("v_beta")
                    for h in range(HEADS):
                        ins = v.scalar_tensor_tensor(R[:, h, :], PS[:, 6, h * P:(h + 1) * P],
                                                     GTN[par][:, G_NBE, h:h + 1], VB[par][:, h, :],
                                                     ALU.mult, ALU.add)
                    signal(ins, "resid")
                if prep:
                    of_prep("cum_rows")
                    of_prep("scalars")
                    signal(v.tensor_tensor(DIF[:, :, :], bank(5), over(GTN[new][:, G_CUM, :]), ALU.subtract), "dif")
                    of_prep("dif")
                    signal(v.tensor_scalar(E1[:, :, :], DIF[:, :, :], 0.0, None, ALU.max), "dif_pos")
                    signal(v.tensor_scalar(E2[:, :, :], DIF[:, :, :], 0.0, None, ALU.min), "dif_neg")
                    of_prep("norm_inv")
                    signal(v.tensor_tensor(KN[:, :, :], K0[:, :, :], over(RN[:, 0, :]), ALU.mult), "k_unit")
                    signal(v.tensor_tensor(QN[:, :, :], Q0[:, :, :], over(RN[:, 1, :]), ALU.mult), "q_unit")
                if scan and prep:
                    of_scan("kv_outer")
                    for h in range(HEADS):
                        ins = v.scalar_tensor_tensor(ST[:, h, :], ST[:, h, :], GTN[par][:, G_ELAST, h:h + 1],
                                                     PS[:, 6, h * P:(h + 1) * P], ALU.mult, ALU.add)
                    signal(ins, "state")
                if scan:
                    of_scan("o_intra")
                    signal(v.tensor_tensor(O[:, :, :], QS[:, :, :], bank(7), ALU.add), "o")
                    of_scan("o")
                    signal(v.tensor_tensor(OSQ[:, :, :], O[:, :, :], O[:, :, :], ALU.mult), "o_sq")
                    of_scan("o_sq")
                    signal(v.tensor_reduce(SSO[:, 0, :], OSQ[:, :, :], AX.X, ALU.add), "o_ss")
                    of_scan("o_ss")
                    signal(v.tensor_scalar(SSO[:, 1, :], SSO[:, 0, :], 1.0 / HD, RMS_EPS, ALU.mult, ALU.add),
                           "rms_arg")
                    if not prep:
                        pooling_lo(2)
                if prep:
                    of_prep("kk")
                    of_prep("decay_beta")
                    signal(v.tensor_tensor(L[:, :, :], bank(4), E1[:, :, :], ALU.mult), "low")
                    of_prep("low")
                    signal(v.tensor_tensor(T[:, :, :], L[:, :, :], mask(M_NEG1), ALU.mult), "inv_part")
                    of_prep("inv_part")
                    signal(v.tensor_tensor(T[:, :, :], T[:, :, :], mask(M_ID), ALU.add), "inv0")
                if scan:
                    of_scan("rms_inv")
                    signal(v.tensor_tensor(ON[:, :, :], O[:, :, :], over(RNO[:, :]), ALU.mult), "o_unit")
                    if not prep:
                        pooling_lo(3)
                if prep:
                    of_prep("qk")
                    of_prep("decayT_up")
                    signal(v.tensor_tensor(ATT[new][:, :, :], bank(5), E2[:, :, :], ALU.mult), "att")
                if scan:
                    of_scan("oT_ps")
                    dve.wait_ge(sem("z_in"), n * 16 + 16)
                    signal(v.scalar_tensor_tensor(FEAT[:, 0:HEADS, bass.ds(n * P, P)], bank(7), DNW[:, 0:1],
                                                  ZS[:, :, :], ALU.mult, ALU.mult), "oT")
                if prep:
                    for lv in range(LEVELS):
                        b = 2 << lv
                        half = lambda t, i: t.rearrange("p h (c two b) -> p h c two b", two=2, b=b)[:, :, :, i, :]
                        ps = lambda i: PS[:, i, 0:256].rearrange("p (h c b) -> p h c b", h=HEADS, b=b)
                        dve.wait_ge(sem("lev_m_ps"), m * LEVELS + lv + 1)
                        dve.wait_ge(sem("mm_zero"), m * LEVELS + lv + 1)
                        for h in range(HEADS):
                            ins = v.tensor_tensor(half(MM[lv % 2][:, h:h + 1, :], 0).squeeze(1), ps(4)[:, h],
                                                  half(mask(M_LEV + lv)[:, 0:1, :], 0).squeeze(1), ALU.mult)
                        ins.then_inc(sem("lev_m"), 1)
                        dve.wait_ge(sem("lev_pT"), m * LEVELS + lv + 1)
                        for h in range(HEADS):
                            to = half(TT[new][:, h:h + 1, :], 1).squeeze(1)
                            ins = v.tensor_tensor(to, to, ps(5)[:, h], ALU.subtract)
                        ins.then_inc(sem("invT"), 1)

            delta_step(None, 0, 1, False, True)
            with dve.Fori(0, 3) as j:
                for r in range(2):
                    delta_step(2 * j + r, 2 * j + r + 1, r, True, True)
            delta_step(NT - 2, NT - 1, 0, True, True)
            delta_step(NT - 1, None, 1, True, False)
            for h in range(2):
                for k in range(0, 4, 2):
                    i = 4 + 2 * h + k // 2
                    dve.wait_ge(feat_hi, i + 1)
                    to = (slice(None), slice(k, k + 2), slice(h * HALF, (h + 1) * HALF))
                    v.tensor_tensor(XTl[to], FEAT[to], XTh[to].bitcast(F32), ALU.subtract).then_inc(scan_lo, 1)

            for s in range(4):
                for i in range(4):
                    w = 4 * s + i
                    dve.wait_ge(unit_ready, U_MIX + w + 1)
                    dve.wait_ge(gate_in[i % 2], 16 * (w // 2 + 1))
                    dve.wait_ge(h_lo, H_MIX + w + 1)
                    v.tensor_tensor(H32[:, i % 2, :], GATE[:, i % 2, 0, :], PS[:, 2 * (i % 2), :], ALU.mult)
                    v.tensor_tensor(SIG[:, i % 2, :], GATE[:, i % 2, 1, :], PS[:, 2 * (i % 2) + 1, :], ALU.mult)\
                        .then_inc(gated_b, 1)
                    dve.wait_ge(gated_b, w + 3)
                    dve.sem_inc(unit_read, 1)
                if s == 0:
                    dve.wait_ge(x_back, 16)
                if s < 3:
                    residual_add(Q_MIX + 16 * s, Q_MIX, s == 0)
            add_and_norm("ln2")

            def rest_of(s, i, hi, lo, scale):
                for c in range(2):
                    count = 2 * (2 * s + i) + c + 1
                    dve.wait_ge(hi, count)
                    to = (slice(None), c, slice(i * HALF, (i + 1) * HALF))
                    v.scalar_tensor_tensor(HTl[to], PS[:, 2 * i + c, :], scale, HTh[to].bitcast(F32),
                                           ALU.mult, ALU.subtract).then_inc(lo, 1)
                dve.wait_ge(lo, count)
                dve.sem_inc(unit_read, 1)

            for s in range(HEADS):
                for kind, i in head_order(s):
                    if kind == "queries":
                        rest_of(s, i, q_hi, q_lo, XD ** -0.5)
                    elif kind == "scores":
                        dve.wait_ge(s_ready, 8 * s + i + 1)
                        v.tensor_reduce(NEGMAX[:, i:i + 1], PS[:, 4, 0:N_MEM], AX.X, ALU.max, negate=True)\
                            .then_inc(neg_max, 1)
                        dve.wait_ge(s_read, 8 * s + i + 2)
                        v.reciprocal(RINV[:, i:i + 1], RSUM[:, i:i + 1]).then_inc(r_inv, 1)
                        dve.wait_ge(r_inv, 8 * s + i + 1)
                        v.tensor_scalar(PR[:, i % 4, :], PR[:, i % 4, :], RINV[:, i:i + 1], None, ALU.mult)\
                            .then_inc(p_norm, 1)
                    elif kind == "turn":
                        dve.wait_ge(pt_hi, 8 * s + i + 1)
                        to = (slice(None), slice(None), slice(i % 4 * P, (i % 4 + 1) * P))
                        v.tensor_tensor(PTl[to], PS[:, 5, 0:N_MEM].rearrange("p (m t) -> p m t", m=MT),
                                        PTh[to].bitcast(F32), ALU.subtract).then_inc(pt_lo, 1)
                    elif kind == "output":
                        if s == HEADS - 1 and i == 1:
                            for t in range(STATS_BEFORE["ln3"]):
                                stats("ln3", t, X, lambda g: None)
                        rest_of(s, i, o_hi, o_lo, 1.0)
                        if i == 1:
                            dve.sem_inc(kvh_used, 1)
                    elif kind == "sum":
                        q = Q_XA + 16 * s + i
                        dve.wait_ge(tile_ready, q + 1)
                        to = X[:, i // 2, i % 2 * 512:(i % 2 + 1) * 512]
                        sums = PS[:, 6 + q % 2, :]
                        if s == 0:
                            ins = v.scalar_tensor_tensor(to, to, ALPHA, sums, ALU.mult, ALU.add)
                        else:
                            ins = v.tensor_tensor(to, to, sums, ALU.add)
                        ins.then_inc(tile_read, 1)
            add_and_norm("ln3")
            ffn(U_FFN2, Q_FFN2, H_FFN2, "ln4")


_INS = ["x", "mem", "ffn1_w_gate", "ffn1_w_up", "ffn1_w_down", "ln1_g", "ln1_b", "w_in", "conv_w", "a_log",
        "dt_bias", "dn_norm_w", "w_dn_branch", "pool_w", "pool_scale", "w_pool_branch", "w_mix_out", "ln2_g",
        "ln2_b", "mem_ln_g", "mem_ln_b", "xa_wq", "xa_wk", "xa_wv", "xa_wo", "ln3_g", "ln3_b",
        "ffn2_w_gate", "ffn2_w_up", "ffn2_w_down", "ln4_g", "ln4_b"]


def kernel(**inputs):
    import concourse.bacc as bacc
    from concourse.bass_utils import run_bass_kernel_spmd

    nc = bacc.Bacc("TRN2", target_bir_lowering=False, num_devices=1)
    arrays, args = {}, {}
    given = {name: np.ascontiguousarray(inputs[name]) for name in _INS}
    given["conv_w"] = np.ascontiguousarray(given["conv_w"][0].reshape(CONV_K, CH_Z, P).transpose(2, 1, 0))
    given["pool_scale"] = np.ascontiguousarray(given["pool_scale"].reshape(GROUPS, P).T)
    given["dn_norm_w"] = given["dn_norm_w"].reshape(P, 1)
    given["masks"] = host_masks()
    given["counts"] = host_counts()
    for name, v in given.items():
        arrays[f"in_{name}"] = v
        args[name] = nc.dram_tensor(f"in_{name}", v.shape, F32, kind="ExternalInput").ap()
    args["out"] = nc.dram_tensor("out_x", (1, SEQ, D), F32, kind="ExternalOutput").ap()
    build(nc, args)
    r = run_bass_kernel_spmd(nc, [arrays], core_ids=[0])
    return r.results[0]["out_x"]
```
